# Optimizing a Trainium2 kernel written in Bass

```python
import jax, jax.numpy as jnp
from jax import lax
import numpy as np
import math

D_MODEL = 2048
BATCH = 1
SEQ = 256
DEPTH = 2

PLE_DIM = 256
POOL_EXPAND = 2
E_POOL = POOL_EXPAND * D_MODEL
POOL_WINDOWS = (2, 4, 8, 16)
N_POOL_GROUPS = len(POOL_WINDOWS)
G_POOL = E_POOL // N_POOL_GROUPS
N_HEADS = D_MODEL // 128
Q_RANK = 512
KV_RANK = 512
NOPE_DIM = 128
ROPE_DIM = 64
V_DIM = 128
QK_DIM = NOPE_DIM + ROPE_DIM
E_MLA = N_HEADS * V_DIM
ROPE_THETA = 10000.0
Q_BLOCK = 128
SM_SCALE = QK_DIM ** -0.5
NEG_INF = -1e30
EPS = 1e-6
N_POOL_LAYERS = (DEPTH + 1) // 2
N_MLA_LAYERS = DEPTH // 2
MLA_IN_DIM = Q_RANK + KV_RANK + ROPE_DIM + E_MLA


def rms_norm(x, g):
    xf = x.astype(jnp.float32)
    y = xf * lax.rsqrt(jnp.mean(xf * xf, axis=-1, keepdims=True) + EPS)
    return (y * g.astype(jnp.float32)).astype(x.dtype)

def rope(x, cos, sin):
    x1, x2 = jnp.split(x.astype(jnp.float32), 2, axis=-1)
    out = jnp.concatenate([x1 * cos - x2 * sin, x2 * cos + x1 * sin], axis=-1)
    return out.astype(x.dtype)

def pool_mixer(xn, w_in, w_group, scale, w_out):
    B, S, _ = xn.shape
    z = xn @ w_in
    u, g = jnp.split(z, 2, axis=-1)
    uf = u.astype(jnp.float32)
    csum = jnp.concatenate([jnp.zeros((B, 1, E_POOL), jnp.float32), jnp.cumsum(uf, axis=1)], axis=1)
    t = jnp.arange(S)
    pooled = []
    for j, w in enumerate(POOL_WINDOWS):
        sl = slice(j * G_POOL, (j + 1) * G_POOL)
        c = csum[:, :, sl]
        lagged = jnp.concatenate([jnp.zeros((B, w - 1, G_POOL), jnp.float32), c[:, :S - w + 1]], axis=1)
        count = jnp.minimum(t + 1, w).astype(jnp.float32)[None, :, None]
        pooled.append((c[:, 1:] - lagged) / count - uf[:, :, sl])
    pooled = jnp.stack(pooled, axis=2).astype(xn.dtype)
    mixed = jnp.einsum('bsgc,gcd->bsgd', pooled, w_group).reshape(B, S, E_POOL)
    return (mixed * scale * jax.nn.silu(g)) @ w_out

def causal_block_attention(q, k, v):
    B, S, H, Dq = q.shape
    nb = S // Q_BLOCK
    qb = q.reshape(B, nb, Q_BLOCK, H, Dq).transpose(1, 0, 2, 3, 4)
    kpos = jnp.arange(S)

    def one_block(args):
        qi, blk = args
        qpos = blk * Q_BLOCK + jnp.arange(Q_BLOCK)
        s = jnp.einsum('bqhd,bkhd->bhqk', qi, k, preferred_element_type=jnp.float32) * SM_SCALE
        s = jnp.where(kpos[None, :] <= qpos[:, None], s, NEG_INF)
        pr = jax.nn.softmax(s, axis=-1).astype(v.dtype)
        return jnp.einsum('bhqk,bkhd->bqhd', pr, v)

    out = lax.map(one_block, (qb, jnp.arange(nb)))
    return out.transpose(1, 0, 2, 3, 4).reshape(B, S, H, V_DIM)

def mla_mixer(xn, cos, sin, w_in, q_norm, w_uq, kv_norm, w_ukv, w_out):
    B, S, _ = xn.shape
    z = xn @ w_in
    q_lat = z[..., :Q_RANK]
    kv_lat = z[..., Q_RANK:Q_RANK + KV_RANK]
    k_pe = z[..., Q_RANK + KV_RANK:Q_RANK + KV_RANK + ROPE_DIM]
    g = z[..., Q_RANK + KV_RANK + ROPE_DIM:]
    q = (rms_norm(q_lat, q_norm) @ w_uq).reshape(B, S, N_HEADS, QK_DIM)
    kv = (rms_norm(kv_lat, kv_norm) @ w_ukv).reshape(B, S, N_HEADS, NOPE_DIM + V_DIM)
    q_nope, q_pe = q[..., :NOPE_DIM], q[..., NOPE_DIM:]
    k_nope, v = kv[..., :NOPE_DIM], kv[..., NOPE_DIM:]
    q_pe = rope(q_pe, cos[:, :, None, :], sin[:, :, None, :])
    k_pe = rope(k_pe, cos, sin)
    q = jnp.concatenate([q_nope, q_pe], axis=-1)
    k = jnp.concatenate([k_nope, jnp.broadcast_to(k_pe[:, :, None, :], (B, S, N_HEADS, ROPE_DIM))], axis=-1)
    o = causal_block_attention(q, k, v).reshape(B, S, E_MLA)
    return (o * jax.nn.silu(g)) @ w_out

def first_inputs(seed: int = 0) -> dict:
    key = jax.random.key(seed)
    ks = jax.random.split(key, 24)
    f32 = jnp.float32

    def nrm(k, shape, fan_in):
        return jax.random.normal(k, shape, f32) * (fan_in ** -0.5)

    def gain(k, shape):
        return 1.0 + 0.02 * jax.random.normal(k, shape, f32)

    offs = jax.random.randint(ks[2], (BATCH, 1), 0, 1024, dtype=jnp.int32)
    positions = offs + jnp.arange(SEQ, dtype=jnp.int32)[None, :]
    return {
        "x": jax.random.normal(ks[0], (BATCH, SEQ, D_MODEL), f32),
        "p": jax.random.normal(ks[1], (DEPTH, BATCH, SEQ, PLE_DIM), f32),
        "positions": positions,
        "pre_norm": gain(ks[3], (DEPTH, D_MODEL)),
        "post_norm": gain(ks[4], (DEPTH, D_MODEL)),
        "pool_w_in": nrm(ks[5], (N_POOL_LAYERS, D_MODEL, 2 * E_POOL), D_MODEL),
        "pool_w_group": nrm(ks[6], (N_POOL_LAYERS, N_POOL_GROUPS, G_POOL, G_POOL), G_POOL),
        "pool_scale": gain(ks[7], (N_POOL_LAYERS, E_POOL)),
        "pool_w_out": nrm(ks[8], (N_POOL_LAYERS, E_POOL, D_MODEL), E_POOL),
        "mla_w_in": nrm(ks[9], (N_MLA_LAYERS, D_MODEL, MLA_IN_DIM), D_MODEL),
        "mla_q_norm": gain(ks[10], (N_MLA_LAYERS, Q_RANK)),
        "mla_w_uq": nrm(ks[11], (N_MLA_LAYERS, Q_RANK, N_HEADS * QK_DIM), Q_RANK),
        "mla_kv_norm": gain(ks[12], (N_MLA_LAYERS, KV_RANK)),
        "mla_w_ukv": nrm(ks[13], (N_MLA_LAYERS, KV_RANK, N_HEADS * (NOPE_DIM + V_DIM)), KV_RANK),
        "mla_w_out": nrm(ks[14], (N_MLA_LAYERS, E_MLA, D_MODEL), E_MLA),
        "ple_norm": gain(ks[15], (DEPTH, D_MODEL)),
        "ple_w_gate": nrm(ks[16], (DEPTH, D_MODEL, D_MODEL), D_MODEL),
        "ple_w_proj": nrm(ks[17], (DEPTH, PLE_DIM, D_MODEL), PLE_DIM),
    }

def first_block(x, p, positions, pre_norm, post_norm, pool_w_in, pool_w_group, pool_scale, pool_w_out,
              mla_w_in, mla_q_norm, mla_w_uq, mla_kv_norm, mla_w_ukv, mla_w_out,
              ple_norm, ple_w_gate, ple_w_proj):
    inv_freq = ROPE_THETA ** (-jnp.arange(0, ROPE_DIM, 2, dtype=jnp.float32) / ROPE_DIM)
    ang = positions.astype(jnp.float32)[..., None] * inv_freq
    cos, sin = jnp.cos(ang), jnp.sin(ang)
    h = x
    for i in range(DEPTH):
        xn = rms_norm(h, pre_norm[i])
        j = i // 2
        if i % 2 == 0:
            out = pool_mixer(xn, pool_w_in[j], pool_w_group[j], pool_scale[j], pool_w_out[j])
        else:
            out = mla_mixer(xn, cos, sin, mla_w_in[j], mla_q_norm[j], mla_w_uq[j],
                            mla_kv_norm[j], mla_w_ukv[j], mla_w_out[j])
        h = h + rms_norm(out, post_norm[i])
        gate = jax.nn.sigmoid(rms_norm(h, ple_norm[i]) @ ple_w_gate[i])
        h = h + (p[i] @ ple_w_proj[i]) * gate
    return h


DEPTH_2 = 1

MEM_LEN = 256
HEAD_DIM = 64
A_WIDTH = 3 * D_MODEL // 8
A_HEADS = A_WIDTH // HEAD_DIM
A_PATTERNS = ((128, 1), (512, 4), (2048, 16))
B_WIDTH = D_MODEL // 4
B_HEADS = B_WIDTH // HEAD_DIM
BLOCK_Q = 128
C_HEADS = 4
C_VW = 3 * D_MODEL // 8
C_DV = C_VW // C_HEADS
C_DK = C_DV // 2
C_KW = C_HEADS * C_DK
C_GATE_RANK = 16
C_GATE_TAU = 16.0
C_CHUNK = 64
MIX_WIDTH = A_WIDTH + B_WIDTH + C_VW
PROJ_SPLITS = (A_WIDTH, A_WIDTH, A_WIDTH, B_WIDTH, B_WIDTH, B_WIDTH, B_HEADS, C_KW, C_KW, C_VW, C_VW, C_GATE_RANK)
PROJ_WIDTH = sum(PROJ_SPLITS)
CROSS_HEADS = 4
CROSS_DH = 128
CROSS_WIDTH = CROSS_HEADS * CROSS_DH
D_FF = ((8 * D_MODEL // 3 + 127) // 128) * 128
CONV_W = 3
REL_BUCKETS = 32
REL_MAX_DIST = 2048


def rms_norm_2(x, g):
    xf = x.astype(jnp.float32)
    y = xf * lax.rsqrt(jnp.mean(xf * xf, axis=-1, keepdims=True) + EPS)
    return (y * g.astype(jnp.float32)).astype(x.dtype)

def t5_bucket(dist):
    max_exact = REL_BUCKETS // 2
    d = np.maximum(dist, 1).astype(np.float32)
    large = max_exact + (np.log(d / max_exact) / math.log(REL_MAX_DIST / max_exact)
                         * (REL_BUCKETS - max_exact)).astype(np.int32)
    return np.where(dist < max_exact, dist, np.minimum(large, REL_BUCKETS - 1)).astype(np.int32)

def dilated_pattern(q, k, v, rel_table, window, dilation):
    B, S, H, Dh = q.shape
    span = window // dilation
    L = S // dilation
    nb = -(-L // span)
    Lp = nb * span

    def classes(t):
        t = t.reshape(B, L, dilation, H, Dh).transpose(0, 3, 2, 1, 4)
        return jnp.pad(t, ((0, 0), (0, 0), (0, 0), (0, Lp - L), (0, 0)))

    def band(t):
        t = jnp.pad(classes(t), ((0, 0), (0, 0), (0, 0), (span, 0), (0, 0)))
        t = t.reshape(B, H, dilation, nb + 1, span, Dh)
        return jnp.concatenate([t[:, :, :, :-1], t[:, :, :, 1:]], axis=4)

    qb = classes(q).reshape(B, H, dilation, nb, span, Dh)
    kb, vb = band(k), band(v)
    i = np.arange(span)[:, None]
    j = np.arange(2 * span)[None, :]
    step = i + span - j
    valid = (step >= 0) & (step <= span) & (np.arange(nb)[:, None, None] * span + j - span >= 0)
    bias = rel_table[t5_bucket(np.clip(step, 0, span) * dilation)]
    bias = jnp.transpose(bias, (2, 0, 1)).astype(jnp.float32)
    logits = jnp.einsum('bhrnid,bhrnjd->bhrnij', qb, kb,
                        preferred_element_type=jnp.float32) * HEAD_DIM ** -0.5
    logits = jnp.where(valid, logits + bias[None, :, None, None], -jnp.inf)
    m = jnp.max(logits, axis=-1, keepdims=True)
    p = jnp.exp(logits - m)
    s = jnp.sum(p, axis=-1, keepdims=True)
    o = jnp.einsum('bhrnij,bhrnjd->bhrnid', p.astype(v.dtype), vb,
                   preferred_element_type=jnp.float32) / s
    lse = (m + jnp.log(s))[..., 0]
    o = o.reshape(B, H, dilation, Lp, Dh)[:, :, :, :L].transpose(0, 3, 2, 1, 4).reshape(B, S, H, Dh)
    lse = lse.reshape(B, H, dilation, Lp)[:, :, :, :L].transpose(0, 3, 2, 1).reshape(B, S, H)
    return o, lse

def dilated_mixture_attention(q, k, v, rel_table):
    outs, lses = [], []
    for window, dilation in A_PATTERNS:
        o, lse = dilated_pattern(q, k, v, rel_table, window, dilation)
        outs.append(o)
        lses.append(lse)
    w = jax.nn.softmax(jnp.stack(lses, axis=0), axis=0)
    return jnp.sum(w[..., None] * jnp.stack(outs, axis=0), axis=0)

def forgetting_attention(q, k, v, f_logit):
    B, S, H, Dh = q.shape
    c = jnp.cumsum(jax.nn.log_sigmoid(f_logit.astype(jnp.float32)), axis=1)
    cT = c.transpose(0, 2, 1)
    nq = S // BLOCK_Q
    qb = q.reshape(B, nq, BLOCK_Q, H, Dh).transpose(1, 0, 2, 3, 4)
    cb = cT.reshape(B, H, nq, BLOCK_Q).transpose(2, 0, 1, 3)
    kpos = jnp.arange(S)

    def block(args):
        n, qn, cn = args
        logits = jnp.einsum('bihd,bjhd->bhij', qn, k,
                            preferred_element_type=jnp.float32) * HEAD_DIM ** -0.5
        logits = logits + (cn[..., :, None] - cT[..., None, :])
        qpos = n * BLOCK_Q + jnp.arange(BLOCK_Q)
        logits = jnp.where(kpos[None, :] <= qpos[:, None], logits, -jnp.inf)
        p = jax.nn.softmax(logits, axis=-1)
        return jnp.einsum('bhij,bjhd->bihd', p.astype(v.dtype), v)

    ob = lax.map(block, (jnp.arange(nq), qb, cb))
    return ob.transpose(1, 0, 2, 3, 4).reshape(B, S, H, Dh)

def gla_chunked(q, k, v, log_alpha):
    B, S, H, DK = q.shape
    nc = S // C_CHUNK

    def chunks(t):
        return t.astype(jnp.float32).reshape(B, nc, C_CHUNK, H, t.shape[-1]).transpose(1, 0, 3, 2, 4)

    qc, kc, vc, gc = chunks(q * DK ** -0.5), chunks(k), chunks(v), chunks(log_alpha)
    causal = np.tril(np.ones((C_CHUNK, C_CHUNK), dtype=bool))[:, :, None]

    def step(state, inp):
        qn, kn, vn, gn = inp
        b = jnp.cumsum(gn, axis=2)
        o_inter = jnp.einsum('bhik,bhkv->bhiv', qn * jnp.exp(b), state)
        diff = b[:, :, :, None, :] - b[:, :, None, :, :]
        decay = jnp.exp(jnp.where(causal, diff, -jnp.inf))
        a = jnp.einsum('bhik,bhjk,bhijk->bhij', qn, kn, decay)
        o_intra = jnp.einsum('bhij,bhjv->bhiv', a, vn)
        b_last = b[:, :, -1:, :]
        state = state * jnp.exp(b_last[:, :, 0, :])[..., None] + \
            jnp.einsum('bhjk,bhjv->bhkv', kn * jnp.exp(b_last - b), vn)
        return state, o_inter + o_intra

    state0 = jnp.zeros((B, H, DK, v.shape[-1]), jnp.float32)
    _, o = lax.scan(step, state0, (qc, kc, vc, gc))
    return o.transpose(1, 0, 3, 2, 4).reshape(B, S, H, v.shape[-1])

def hybrid_mixer(h, w_in, f_bias, rel_table, c_gate_w2, c_gate_b, c_norm, w_out):
    B, S, _ = h.shape
    proj = h @ w_in
    qa, ka, va, qb, kb, vb, fl, qc, kc, vc, rc, gl = jnp.split(
        proj, np.cumsum(PROJ_SPLITS)[:-1].tolist(), axis=-1)

    def heads(t, n):
        return t.reshape(B, S, n, -1)

    o_a = dilated_mixture_attention(heads(qa, A_HEADS), heads(ka, A_HEADS), heads(va, A_HEADS), rel_table)
    o_b = forgetting_attention(heads(qb, B_HEADS), heads(kb, B_HEADS), heads(vb, B_HEADS), fl + f_bias)
    log_alpha = jax.nn.log_sigmoid((gl @ c_gate_w2 + c_gate_b).astype(jnp.float32)) / C_GATE_TAU
    o_c = gla_chunked(heads(qc, C_HEADS), heads(kc, C_HEADS), heads(vc, C_HEADS), heads(log_alpha, C_HEADS))
    o_c = rms_norm_2(o_c.astype(h.dtype), c_norm).reshape(B, S, C_VW) * jax.nn.silu(rc)
    mixed = jnp.concatenate([o_a.reshape(B, S, A_WIDTH).astype(h.dtype),
                             o_b.reshape(B, S, B_WIDTH).astype(h.dtype),
                             o_c.astype(h.dtype)], axis=-1)
    return mixed @ w_out

def memory_cross_attention(h, mem_n, w_q, w_kv, w_o):
    B, S, _ = h.shape
    M = mem_n.shape[1]
    q = (h @ w_q).reshape(B, S, CROSS_HEADS, CROSS_DH)
    k, v = jnp.split(mem_n @ w_kv, 2, axis=-1)
    k = k.reshape(B, M, CROSS_HEADS, CROSS_DH)
    v = v.reshape(B, M, CROSS_HEADS, CROSS_DH)
    logits = jnp.einsum('bshd,bmhd->bhsm', q, k, preferred_element_type=jnp.float32) * CROSS_DH ** -0.5
    p = jax.nn.softmax(logits, axis=-1)
    o = jnp.einsum('bhsm,bmhd->bshd', p.astype(v.dtype), v).reshape(B, S, CROSS_WIDTH)
    return o @ w_o

def conv_ffn(h, w_up, conv_w, conv_b, w_down):
    S = h.shape[1]
    val, gate = jnp.split(h @ w_up, 2, axis=-1)
    gp = jnp.pad(gate, ((0, 0), (CONV_W - 1, 0), (0, 0)))
    g = conv_b
    for i in range(CONV_W):
        g = g + conv_w[i] * gp[:, i:i + S]
    return (jax.nn.silu(g) * val) @ w_down

def second_inputs(seed: int = 0) -> dict:
    key = jax.random.key(seed)
    ks = jax.random.split(key, 21)

    def nrm(k, shape, scale):
        return jax.random.normal(k, shape, jnp.float32) * scale

    def gain(k, shape):
        return 1.0 + 0.05 * jax.random.normal(k, shape, jnp.float32)

    return {
        'x': nrm(ks[0], (BATCH, SEQ, D_MODEL), 1.0),
        'mem': nrm(ks[1], (BATCH, MEM_LEN, D_MODEL), 1.0),
        'rel_table': nrm(ks[2], (REL_BUCKETS, A_HEADS), 0.5),
        'mem_norm': gain(ks[3], (D_MODEL,)),
        'norm_final': gain(ks[4], (D_MODEL,)),
        'norm_mix': gain(ks[5], (DEPTH_2, D_MODEL)),
        'w_in': nrm(ks[6], (DEPTH_2, D_MODEL, PROJ_WIDTH), D_MODEL ** -0.5),
        'f_bias': 3.0 + nrm(ks[7], (DEPTH_2, B_HEADS), 0.1),
        'c_gate_w2': nrm(ks[8], (DEPTH_2, C_GATE_RANK, C_KW), C_GATE_RANK ** -0.5),
        'c_gate_b': nrm(ks[9], (DEPTH_2, C_KW), 0.1),
        'c_norm': gain(ks[10], (DEPTH_2, C_DV)),
        'w_out': nrm(ks[11], (DEPTH_2, MIX_WIDTH, D_MODEL), MIX_WIDTH ** -0.5),
        'norm_cross': gain(ks[12], (DEPTH_2, D_MODEL)),
        'w_cq': nrm(ks[13], (DEPTH_2, D_MODEL, CROSS_WIDTH), D_MODEL ** -0.5),
        'w_ckv': nrm(ks[14], (DEPTH_2, D_MODEL, 2 * CROSS_WIDTH), D_MODEL ** -0.5),
        'w_co': nrm(ks[15], (DEPTH_2, CROSS_WIDTH, D_MODEL), CROSS_WIDTH ** -0.5),
        'norm_ffn': gain(ks[16], (DEPTH_2, D_MODEL)),
        'w_up': nrm(ks[17], (DEPTH_2, D_MODEL, 2 * D_FF), D_MODEL ** -0.5),
        'conv_w': nrm(ks[18], (DEPTH_2, CONV_W, D_FF), CONV_W ** -0.5),
        'conv_b': nrm(ks[19], (DEPTH_2, D_FF), 0.02),
        'w_down': nrm(ks[20], (DEPTH_2, D_FF, D_MODEL), D_FF ** -0.5),
    }

def second_block(x, mem, rel_table, mem_norm, norm_final, norm_mix, w_in, f_bias, c_gate_w2,
              c_gate_b, c_norm, w_out, norm_cross, w_cq, w_ckv, w_co, norm_ffn, w_up,
              conv_w, conv_b, w_down):
    mem_n = rms_norm_2(mem, mem_norm)
    for l in range(DEPTH_2):
        x = x + hybrid_mixer(rms_norm_2(x, norm_mix[l]), w_in[l], f_bias[l], rel_table,
                             c_gate_w2[l], c_gate_b[l], c_norm[l], w_out[l])
        x = x + memory_cross_attention(rms_norm_2(x, norm_cross[l]), mem_n, w_cq[l], w_ckv[l], w_co[l])
        x = x + conv_ffn(rms_norm_2(x, norm_ffn[l]), w_up[l], conv_w[l], conv_b[l], w_down[l])
    return rms_norm_2(x, norm_final)


def setup_inputs(seed=0):
    out = dict(first_inputs(seed))
    for name, value in second_inputs(seed + 1).items():
        if name != "x":
            out[name + "_2"] = value
    return out


def reference(
    x, p, positions, pre_norm, post_norm, pool_w_in, pool_w_group, pool_scale, pool_w_out,
    mla_w_in, mla_q_norm, mla_w_uq, mla_kv_norm, mla_w_ukv, mla_w_out, ple_norm, ple_w_gate,
    ple_w_proj, mem_2, rel_table_2, mem_norm_2, norm_final_2, norm_mix_2, w_in_2, f_bias_2,
    c_gate_w2_2, c_gate_b_2, c_norm_2, w_out_2, norm_cross_2, w_cq_2, w_ckv_2, w_co_2,
    norm_ffn_2, w_up_2, conv_w_2, conv_b_2, w_down_2,
):
    x = first_block(
        x, p, positions, pre_norm, post_norm, pool_w_in, pool_w_group, pool_scale, pool_w_out,
        mla_w_in, mla_q_norm, mla_w_uq, mla_kv_norm, mla_w_ukv, mla_w_out, ple_norm, ple_w_gate,
        ple_w_proj,
    )
    return second_block(
        x, mem_2, rel_table_2, mem_norm_2, norm_final_2, norm_mix_2, w_in_2, f_bias_2,
        c_gate_w2_2, c_gate_b_2, c_norm_2, w_out_2, norm_cross_2, w_cq_2, w_ckv_2, w_co_2,
        norm_ffn_2, w_up_2, conv_w_2, conv_b_2, w_down_2,
    )


_drawn_inputs = setup_inputs


def setup_inputs(seed=0):
    import zlib

    import numpy as np

    out = dict(_drawn_inputs(seed))
    spreads = {}
    factors = {'pool_scale': 2.949,
     'mla_q_norm': 4.87,
     'mla_kv_norm': 3.716,
     'ple_norm': 8.0,
     'mem_norm_2': 8.0,
     'f_bias_2': 64.0,
     'c_gate_b_2': 7.554,
     'c_norm_2': 5.779,
     'norm_cross_2': 8.0,
     'conv_b_2': 38.233,
     'norm_ffn_2': 8.0}
    for name, (base, spread) in spreads.items():
        noise = np.random.default_rng([zlib.crc32(name.encode()), seed]).standard_normal(out[name].shape)
        drawn = base * np.exp(spread * noise) if base else spread * noise
        out[name] = __import__('jax').numpy.asarray(drawn.astype(out[name].dtype))
    for name, factor in factors.items():
        out[name] = (out[name] * factor).astype(out[name].dtype)
    return out
```

```python
import math
from contextlib import ExitStack, contextmanager

import numpy as np

import concourse.bass as bass
from concourse import mybir

F32, F32R, I32 = mybir.dt.float32, mybir.dt.float32r, mybir.dt.int32
ACT = mybir.ActivationFunctionType
ALU = mybir.AluOpType
AXX = mybir.AxisListType.X

D = 2048
T = 256
KT = D // 128
NCH = D // 512
EPS = 1e-6
E_POOL = 4096
WINDOWS = (2, 4, 8, 16)
HEADS = 16
Q_RANK = KV_RANK = 512
NOPE, ROPE, VD = 128, 64, 128
A_W, B_W, C_KW, C_VW = 768, 512, 384, 768
A_H, B_H, C_H, C_DK, C_DV = 12, 8, 4, 96, 192
Z_W = 3 * A_W + 3 * B_W + B_H + 2 * C_KW + 2 * C_VW + 16
Z_QA, Z_KA, Z_VA = 0, A_W, 2 * A_W
Z_QB, Z_KB, Z_VB = 3 * A_W, 3 * A_W + B_W, 3 * A_W + 2 * B_W
Z_FL = 3 * A_W + 3 * B_W
Z_QC = Z_FL + B_H
Z_KC = Z_QC + C_KW
Z_VC = Z_KC + C_KW
Z_RC = Z_VC + C_VW
Z_GL = Z_RC + C_VW
D_FF = 5504
FKT = D_FF // 128
BUCKETS, MAX_DIST = 32, 2048
MASKED = -1e30
RAW, RING, LEAD = 8, 4, 3

LINEARS = [("pool", 160, 24), ("pool_out", 64, 4), ("proj0", 4, 4), ("gate0", 32, 4), ("mla_in", 49, 7), ("uq", 12, 6),
           ("ukv", 16, 8), ("mla_out", 32, 4), ("proj1", 4, 4), ("gate1", 32, 4), ("ckv", 16, 2), ("z", 97, 13),
           ("out2", 32, 4), ("cq", 8, 1), ("co", 8, 4), ("up", 176, 22), ("down", 96, 4)]
UNITS_END = {n: sum(u for _, u, _ in LINEARS[:k + 1]) for k, (n, _, _) in enumerate(LINEARS)}
CHUNKS_END = {n: sum(c for _, _, c in LINEARS[:k + 1]) for k, (n, _, _) in enumerate(LINEARS)}
TOTAL_UNITS = UNITS_END["down"]

GAIN_TILES = [
    [("pre0", 16), ("pre1", 16), ("ple0", 16), ("ple1", 16), ("pool_scale", 32), ("q_norm", 4), ("kv_norm", 4), ("mix", 16)],
    [("cross", 16), ("ffn", 16), ("mem", 16), ("conv_b", 43)],
    [("conv_w0", 43), ("conv_w1", 43)],
    [("conv_w2", 43)],
]
GAIN = {name: 128 * t + sum(n for _, n in tile[:k]) for t, tile in enumerate(GAIN_TILES) for k, (name, _) in enumerate(tile)}


def shape_constants():
    s, t = np.arange(128)[:, None], np.arange(256)[None, :]
    ident = np.eye(128, dtype=np.float32)
    band = np.zeros((128, 4, 384), np.float32)
    for j, w in enumerate(WINDOWS):
        full = np.zeros((256, 256), np.float32)
        for q in range(256):
            full[max(0, q - w + 1):q + 1, q] = np.float32(1.0) / np.float32(min(q + 1, w))
            full[q, q] -= 1.0
        band[:, j, :256] = full[:128]
        band[:, j, 256:] = full[128:, 128:]
    causal = np.where(s + 128 - t >= 0, 0.0, MASKED).astype(np.float32)
    m = np.arange(384)
    dist = 255 - m
    d = np.maximum(dist, 1).astype(np.float32)
    half = BUCKETS // 2
    large = half + (np.log(d / half) / math.log(MAX_DIST / half) * (BUCKETS - half)).astype(np.int32)
    bucket = np.where(dist < half, dist, np.minimum(large, BUCKETS - 1))
    rel = np.zeros((33, 384), np.float32)
    for c in range(384):
        if dist[c] >= 0:
            rel[bucket[c], c] = 1.0
            kept = int(dist[c] <= 128) + int(dist[c] % 4 == 0) + int(dist[c] % 16 == 0)
            rel[32, c] = np.log(np.float32(kept)) if kept else MASKED
        else:
            rel[32, c] = MASKED
    a, b = np.arange(128)[:, None], np.arange(128)[None, :]
    decay = [(a > b), (a <= b)]
    masks = [np.eye(128, dtype=bool)]
    for size in (128, 64, 32, 16, 8, 4, 2):
        mid = b // size * size + size // 2
        decay.append(((b >= mid) & (a >= mid) & (a <= b)) | ((b < mid) & (a > b) & (a < mid)))
        masks.append((a // size == b // size) & (b % size >= size // 2) & (a % size < size // 2))
    decay = np.stack(decay, 1).astype(np.float32).reshape(128, 9 * 128)
    masks = np.stack(masks, 1).astype(np.float32).reshape(128, 8 * 128)
    trio = np.concatenate([(a <= b), np.ones((128, 128), bool)], 1).astype(np.float32)
    freq = (10000.0 ** (-np.arange(0, ROPE, 2, dtype=np.float32) / np.float32(ROPE))).astype(np.float32)
    return {"ident": ident, "flip": np.ascontiguousarray(ident[::-1]), "band": band.reshape(128, 4 * 384), "causal": causal, "rel": rel, "decay": decay,
            "masks": masks, "trio": trio, "freq": freq[None, :]}


class Tally:

    def __init__(self):
        self.n, self.reg, self.per = {}, None, {}

    def at(self, name, k=0):
        v = self.n.get(name, 0) + k
        return self.reg * self.per[name] + v if self.reg is not None and self.per.get(name) else v

    def add(self, name, k=1):
        self.n[name] = self.n.get(name, 0) + k

    @contextmanager
    def loop(self, reg, turns, **per):
        begin = dict(self.n)
        self.reg, self.per = reg, per
        yield
        got = {k: v - begin.get(k, 0) for k, v in self.n.items() if v != begin.get(k, 0)}
        assert got == {k: v for k, v in per.items() if v}, f"loop counts {got}, said {per}"
        for k, v in got.items():
            self.n[k] = begin.get(k, 0) + turns * v
        self.reg, self.per = None, {}


def units_of(nkt, width=512):
    if nkt == FKT:
        return [(2 * u, 2 * u + 1) for u in range(19)] + [(k,) for k in range(38, 43)]
    per = 1024 // width if width < 256 else 2
    return [tuple(range(k, min(k + per, nkt))) for k in range(0, nkt, per)]


def build(nc, a, out):
    ctx = ExitStack()
    ctx.enter_context(nc.allow_non_contiguous_dma(reason="narrow weight columns, vectors"))
    sems = {}

    def S(name):
        if name not in sems:
            sems[name] = ctx.enter_context(nc.semaphore(name))
        return sems[name]

    base = (nc.sbuf_base + 63) // 64 * 64
    limit = nc.sbuf_usable_end

    def at(name, off, shape, dt=F32):
        size = int(np.prod(shape[1:])) * 4
        assert base + off + size <= limit, (name, base + off + size - limit)
        return nc.alloc_sbuf_tensor_at(name, shape, dt, offset=base + off)[:]

    pos = [0]

    def fixed(name, shape, dt=F32):
        off = pos[0]
        pos[0] += (int(np.prod(shape[1:])) * 4 + 31) // 32 * 32
        return at(name, off, shape, dt)

    raw = fixed("raw", [128, RAW, 1024])
    w_hi = fixed("w_hi", [128, RING, 1024], F32R)
    w_lo = fixed("w_lo", [128, RING, 1024], F32R)
    h = fixed("h", [128, 2, D])
    ident = fixed("identity", [128, 128])
    gain = fixed("gain_columns", [128, 512])
    causal = fixed("causal_mask", [128, 256])
    junk = fixed("junk", [128, 512])
    sums = fixed("square_sums", [128, 16, 2, 4])
    ms = fixed("mean_square", [128, 16, 2])
    rt = fixed("root", [128, 16, 2])
    rstd = fixed("rstd", [128, 16, 2])
    rc_cos = fixed("rope_cos", [128, 2, 32])
    rc_sin = fixed("rope_sin", [128, 2, 32])
    A0 = pos[0]

    def arena(name, off, shape, dt=F32):
        return at(name, A0 + off, shape, dt)

    xh = arena("x_hi", 0, [128, KT, T], F32R)
    xl = arena("x_lo", 16384, [128, KT, T], F32R)
    rows = arena("gain_rows", 32768, [128, 4, 128])
    y32 = arena("pool_y", 32768, [128, 32, T])
    band = arena("band", 65536, [128, 4, 384])
    ut = arena("u_tokens", 71680, [128, 2, 1024])
    sg = arena("silu_gate", 79872, [128, 2, 1024])
    plh = arena("pooled_hi", 88064, [128, 8, T], F32R)
    pll = arena("pooled_lo", 96256, [128, 8, T], F32R)
    mxs = arena("mixed_gated", 104448, [128, 2, 2, 512])
    yh = arena("pool_y_hi", 0, [128, 32, T], F32R)
    yl = arena("pool_y_lo", 32768, [128, 32, T], F32R)
    outt = arena("mixer_out", 65536, [128, 2, D])
    proj = arena("ple_proj", 81920, [128, 2, D])
    pgain = arena("post_gain", 98304, [128, D])
    sig = arena("ple_gate", 106496, [128, 2, 2, 512])
    ptok = arena("ple_tokens", 114688, [128, 2, 256])
    ph = arena("ple_hi", 116736, [128, 2, T], F32R)
    pl = arena("ple_lo", 118784, [128, 2, T], F32R)
    lat = arena("latents", 32768, [128, 2, 1024])
    kpe = arena("k_pe", 40960, [128, 2, 64])
    kpt = arena("k_pe_T", 41472, [64, T])
    gm = arena("mla_gate", 42496, [128, 2, D])
    qt = arena("mla_q", 58880, [128, 2, HEADS * 192])
    kv = arena("mla_kv", 83456, [128, 2, HEADS * 256])
    qlh = arena("q_lat_hi", 0, [128, 4, T], F32R)
    qll = arena("q_lat_lo", 4096, [128, 4, T], F32R)
    klh = arena("kv_lat_hi", 8192, [128, 4, T], F32R)
    kll = arena("kv_lat_lo", 12288, [128, 4, T], F32R)
    ra = arena("rope_a", 16384, [128, 2, HEADS, 32])
    rb = arena("rope_b", 20480, [128, 2, HEADS, 32])
    rc_ = arena("rope_c", 24576, [128, 2, HEADS, 32])
    rd = arena("rope_d", 28672, [128, 2, HEADS, 32])
    posi = arena("positions", 112640, [128, 2], I32)
    posf = arena("positions_f", 112672, [128, 2])
    freqs = arena("rope_freq", 112704, [128, 32])
    ang = arena("angle", 112896, [128, 2, 32])
    turns_ = arena("angle_turns", 113152, [128, 2, 32])
    red = arena("angle_reduced", 113408, [128, 2, 32])
    SQ = [arena(f"q_staged{j}", 7680 * j, [128, 2, 192]) for j in range(4)]
    SK = [arena(f"k_staged{j}", 7680 * j + 1536, [128, 2, 128]) for j in range(4)]
    QK = [arena(f"qk_T{j}", 7680 * j + 2560, [128, 2, T]) for j in range(4)]
    PTS = [arena(f"p_T{j}", 7680 * j + 2560, [128, 4, 128]) for j in range(4)]
    QP = [arena(f"q_pe_T{j}", 7680 * j + 4608, [64, T]) for j in range(4)]
    LG_ = [arena(f"logits{j}", 7680 * j + 5632, [128, 512]) for j in range(4)]
    assert 7680 * 4 <= 32768
    nmx = arena("neg_max", 30720, [128, 4, 2])
    psm = arena("prob_sum", 30752, [128, 4, 2])
    prc = arena("prob_scale", 30784, [128, 4, 2])
    KVM = 115456 - 512
    memt = arena("mem_tokens", 32768, [128, 2, D])
    kvm = arena("mem_kv", KVM, [128, 2, 1024])
    z = arena("z", 32768, [128, 2, Z_W])
    relb = arena("rel_bias", 82112, [128, A_H, T])
    mix = arena("mixed", 94400, [128, 2, D])
    lgd = arena("log_decay", 110784, [128, 2, 392])
    reltab = arena("rel_table", 0, [33, A_H])
    relone = arena("rel_onehot", 64, [33, 384])
    relrow = arena("rel_rows", 1600, [A_H, 384])
    lx = arena("gate_logits", 4096, [128, 2, 392])
    la = arena("gate_abs", 8192, [128, 2, 392])
    lm = arena("gate_min", 12288, [128, 2, 392])
    glt = arena("gl_T", 16384, [17, T])
    w2a = arena("gate_w2", 18432, [17, C_KW])
    fbias = arena("f_bias", 20480, [128, B_H])
    flip = arena("flip", 24576, [128, 128])
    trio = arena("running_sum", 20736, [128, 256])
    lf8 = arena("log_forget", 21760, [128, 2, B_H])
    crow, ncrow = junk[0:B_H, 0:256], junk[0:B_H, 256:512]
    ck2 = arena("forget_k", 32768, [2, B_H, T])
    cq2 = arena("forget_q", 32768 + 4 * Z_W, [2, B_H, T])
    gq = arena("gla_q_T", 0, [96, C_H, T])
    gk = arena("gla_k_T", 4096, [96, C_H, T])
    ge = arena("gla_decay", 8192, [96, C_H, T])
    gqs = arena("gla_q_decayed", 12288, [96, C_H, T])
    gks = arena("gla_k_decayed", 16384, [96, C_H, T])
    gat = arena("gla_attn", 20480, [128, 3, C_H, 128])
    gmask = arena("gla_masks", 26624, [128, 8, 128])
    dmat = arena("gla_sums", 32768, [128, 9, 128])
    oc = arena("gla_out", 37376, [128, 2, C_H, C_DV])
    cnb = arena("c_norm", 43520, [128, C_DV])
    cst = arena("gla_stats", 44288, [128, 3, 8])
    osq = arena("gla_squares", 32768 + 4 * Z_W, [128, 2, C_H, C_DV])
    cqt = arena("cross_q", 32768, [128, 2, 512])
    cot = arena("cross_out", 36864, [128, 2, 512])
    fy = arena("ffn_y", 32768, [128, FKT, T])
    fgs = arena("ffn_gate", 76800, [128, 2, 512])
    fvs = arena("ffn_val", 80896, [128, 2, 512])
    fcv = arena("ffn_conv", 84992, [128, 4, T])
    fyl = arena("ffn_y_lo", 32768, [128, FKT, T], F32R)
    fyh = arena("ffn_y_hi", 76800, [128, FKT, T], F32R)
    fgain = arena("final_gain", 0, [128, D])
    fout = arena("final_out", 8192, [128, 2, D])

    ps = ctx.enter_context(nc.psum_tensor("ps", [128, 8, 512], F32))[:]

    def MM(s, tt):
        return ps[:, 2 * s + tt, :]

    def TB(b):
        return ps[:, 4 + b, :]

    rel_scratch = nc.dram_tensor("rel_scratch", (A_H, 384), F32, kind="Internal").ap()

    def weights(ap):
        return ap.rearrange("(k p) n -> p k n", p=128)

    w_pool = weights(a["pool_w_in"][0])
    w_group = a["pool_w_group"][0].rearrange("g (k p) n -> p g k n", p=128)
    w_pout = weights(a["pool_w_out"][0])
    w_proj = [weights(a["ple_w_proj"][n]) for n in range(2)]
    w_gate = [weights(a["ple_w_gate"][n]) for n in range(2)]
    w_min = weights(a["mla_w_in"][0])
    w_uq, w_ukv, w_mout = weights(a["mla_w_uq"][0]), weights(a["mla_w_ukv"][0]), weights(a["mla_w_out"][0])
    w_ckv, w_cq, w_co = weights(a["w_ckv_2"][0]), weights(a["w_cq_2"][0]), weights(a["w_co_2"][0])
    w_in2, w_out2 = weights(a["w_in_2"][0]), weights(a["w_out_2"][0])
    w_up, w_down = weights(a["w_up_2"][0]), weights(a["w_down_2"][0])

    def tokens(ap):
        return ap.rearrange("(t p) n -> p t n", p=128)

    UNITS_POOL = 4 * 8 + 2 * 4
    WB = len(WINDOWS)

    def products(eng, linear, more=0):
        eng.wait_ge(S("w_used"), UNITS_END[linear] + RING + more)

    def evacuated(eng, linear):
        for back in (2, 1):
            c = CHUNKS_END[linear] - back
            eng.wait_ge(S(f"mm_free{c % 2}"), c // 2 + 2)

    def banks_read(eng, t):
        for b in range(4):
            eng.wait_ge(S(f"t_free{b}"), (t.n["bank"] - b + 3) // 4 + 1)

    def gated(eng, n, chunks=4):
        eng.wait_ge(S("gated"), 2 + 4 * n + chunks)

    AT = {"mla": 0, "a": 16, "b": 28, "cross": 36, "end": 40}

    def heads_done(eng, before):
        eng.wait_ge(S("at_done"), AT[before] + 4)

    block = ctx.enter_context(nc.Block())

    @block.sync
    def _(sp):
        t = Tally()

        def unit(src, kts, width):
            slot = t.n.get("unit", 0) % RAW
            sp.wait_ge(S("w_lo"), t.at("unit", 1))
            if t.reg is not None:
                sp.sem_inc(S("units_begun"), 1)
            n = len(kts) * width
            dst = raw[:, slot, 0:n].rearrange("p (k n) -> p k n", n=width)
            sp.dma_start(dst, src).then_inc(S(f"raw_full{slot}"), 16)
            t.add("unit")

        def chunk(w, nkt, col, width=512):
            for kts in units_of(nkt, width):
                unit(w[:, kts[0]:kts[-1] + 1, bass.ds(col, width)], kts, width)

        def load(dst, src, sem):
            sp.dma_start(dst, src).then_inc(S(sem), 16)

        load(ident, a["c_ident"], "ident_in")
        for tt in range(2):
            load(h[:, tt, :], a["x"][0, tt * 128:(tt + 1) * 128, :], "h_in")
        vectors = {"pre0": a["pre_norm"][0], "pre1": a["pre_norm"][1], "ple0": a["ple_norm"][0], "ple1": a["ple_norm"][1],
                   "pool_scale": a["pool_scale"][0], "q_norm": a["mla_q_norm"][0], "kv_norm": a["mla_kv_norm"][0],
                   "mix": a["norm_mix_2"][0], "cross": a["norm_cross_2"][0], "ffn": a["norm_ffn_2"][0],
                   "mem": a["mem_norm_2"], "conv_b": a["conv_b_2"][0], "conv_w0": a["conv_w_2"][0, 0],
                   "conv_w1": a["conv_w_2"][0, 1], "conv_w2": a["conv_w_2"][0, 2]}
        for n, tile in enumerate(GAIN_TILES):
            at_row = 0
            for name, r in tile:
                load(rows[at_row:at_row + r, n, :], vectors[name].rearrange("(r c) -> r c", c=128), "rows_in")
                at_row += r
        load(posi, a["positions"].rearrange("o (t p) -> p (o t)", p=128), "pos_in")
        load(freqs, a["c_freq"].broadcast_to([128, 32]), "pos_in")
        load(band.rearrange("p w n -> p (w n)"), a["c_band"], "band_in")
        load(causal, a["c_causal"], "causal_in")

        with sp.Fori(0, WB) as g, t.loop(g, WB, unit=UNITS_POOL):
            for half in range(2):
                for c in range(2):
                    chunk(w_pool, KT, g * 1024 + (half * E_POOL + c * 512))
            for c in range(2):
                for kts in units_of(8):
                    unit(w_group[:, bass.ds(g, 1), kts[0]:kts[-1] + 1, c * 512:(c + 1) * 512].rearrange("p g k n -> p (g k) n"),
                         kts, 512)
        with sp.Fori(0, 2) as g, t.loop(g, 2, unit=32):
            for c in range(2):
                chunk(w_pout, 32, g * 1024 + c * 512)

        def columns(w, col=0):
            with sp.Fori(0, 2) as g, t.loop(g, 2, unit=16):
                for c in range(2):
                    chunk(w, KT, g * 1024 + (c * 512 + col))

        def layer_end(n):
            for c in range(NCH):
                chunk(w_proj[n], 2, c * 512)
            columns(w_gate[n])

        layer_end(0)
        chunk(w_min, KT, 0)
        chunk(w_min, KT, 512)
        chunk(w_min, KT, 1024, 64)
        columns(w_min, 1088)
        for c in range(6):
            chunk(w_uq, 4, c * 512)
        with sp.Fori(0, 2) as g, t.loop(g, 2, unit=8):
            for c in range(4):
                chunk(w_ukv, 4, g * 2048 + c * 512)
        columns(w_mout)
        layer_end(1)
        for c in range(2):
            chunk(w_ckv, KT, c * 512)
        with sp.Fori(0, 6) as g, t.loop(g, 6, unit=16):
            for c in range(2):
                chunk(w_in2, KT, g * 1024 + c * 512)
        chunk(w_in2, KT, 12 * 512, 24)
        columns(w_out2)
        chunk(w_cq, KT, 0)
        for c in range(NCH):
            chunk(w_co, 4, c * 512)
        with sp.Fori(0, 10) as g, t.loop(g, 10, unit=16):
            chunk(w_up, KT, g * 512 + D_FF)
            chunk(w_up, KT, g * 512)
        chunk(w_up, KT, 5120 + D_FF, 384)
        chunk(w_up, KT, 5120, 384)
        for c in range(NCH):
            chunk(w_down, FKT, c * 512)
        assert t.n["unit"] == TOTAL_UNITS, t.n
        for c in range(2):
            sp.wait_ge(S("final"), c + 1)
            load(out[0, c * 128:(c + 1) * 128, :], fout[:, c, :], "out_done")
        sp.wait_ge(S("out_done"), 32)

    @block.tensor
    def _(pe):
        t = Tally()
        pe.sem_inc(S("w_used"), RING)

        def take_bank():
            b = t.n.get("bank", 0) % 4
            pe.wait_ge(S(f"t_free{b}"), t.at(f"bank{b}", 1))
            t.add("bank")
            t.add(f"bank{b}")
            return b

        def to_bank(src, f0, tiles=2):
            b = take_bank()
            for k in range(tiles):
                for tt in range(2):
                    f = f0 + k * 128
                    last = pe.transpose(TB(b)[:, k * 256 + tt * 128:k * 256 + tt * 128 + 128], src[:, tt, f:f + 128], ident)
            last.then_inc(S("t_full"), 1)

        def xpose(src, nkt, ready=None):
            for g in range(nkt // 2):
                if ready:
                    ready(g)
                to_bank(src, g * 256)

        def last_banks(n):
            total = t.n["bank"]
            def ready(k):
                if k % 2 == 0:
                    g = total - n + k // 2
                    pe.wait_ge(S(f"t_free{g % 4}"), g // 4 + 2)
            return ready

        def chunk(xhi, xlo, nkt, width=512, ready=None):
            s = t.n.get("chunk", 0) % 2
            pe.wait_ge(S(f"mm_free{s}"), t.at(f"set{s}", 1))
            units = units_of(nkt, width)
            for kts in units:
                slot = t.n.get("unit", 0) % RING
                pe.wait_ge(S("w_lo"), t.at("unit", RAW + 1))
                for n, k in enumerate(kts):
                    if ready:
                        ready(k)
                    wh = w_hi[:, slot, n * width:(n + 1) * width]
                    wl = w_lo[:, slot, n * width:(n + 1) * width]
                    for tt in range(2):
                        tok = slice(tt * 128, tt * 128 + 128)
                        dst = MM(s, tt)[:, 0:width]
                        pe.matmul(dst, xhi[:, k, tok], wh, start=k == 0, stop=False)
                        pe.matmul(dst, xhi[:, k, tok], wl, start=False, stop=False)
                        last = pe.matmul(dst, xlo[:, k, tok], wh, start=False, stop=k == nkt - 1)
                last.then_inc(S("w_used"), 1)
                t.add("unit")
            t.add("chunk")
            t.add(f"set{s}")
            return s

        def columns(xhi=xh, xlo=xl, nkt=KT, turns=2, ready=None):
            with pe.Fori(0, turns) as g, t.loop(g, turns, unit=2 * len(units_of(nkt)), chunk=2, set0=1, set1=1):
                for c in range(2):
                    chunk(xhi, xlo, nkt, ready=ready if c == 0 else None)

        pe.wait_ge(S("ident_in"), 16)
        pe.wait_ge(S("rows_in"), 16 * sum(len(x) for x in GAIN_TILES))
        b = take_bank()
        for n, tile in enumerate(GAIN_TILES):
            r = sum(x for _, x in tile)
            last = pe.transpose(TB(b)[:, n * 128:n * 128 + r], rows[0:r, n, :], ident[0:r, 0:r])
        last.then_inc(S("t_full"), 1)

        pe.wait_ge(S("h_in"), 32)
        xpose(h, KT)
        pe.wait_ge(S("band_in"), 16)
        ready = last_banks(8)
        with pe.Fori(0, WB) as g, t.loop(g, WB, unit=UNITS_POOL, chunk=6, set0=3, set1=3, bank=8, bank0=2, bank1=2,
                                         bank2=2, bank3=2):
            for c in range(3):
                chunk(xh, xl, KT, ready=ready if c == 0 else None)
                if c == 1:
                    before = [(f"mm_free{s}", t.at(f"set{s}", 1)) for s in range(2)]
            for name, v in before:
                pe.wait_ge(S(name), v)
            for k2 in range(4):
                b = take_bank()
                for k in range(2):
                    f = (2 * k2 + k) * 128
                    pe.matmul(TB(b)[:, k * 256:k * 256 + 256], ut[:, 0, f:f + 128],
                              band[:, bass.ds(g, 1), 0:256].rearrange("p o n -> p (o n)"), start=True, stop=False)
                    last = pe.matmul(TB(b)[:, k * 256 + 128:k * 256 + 256], ut[:, 1, f:f + 128],
                                     band[:, bass.ds(g, 1), 256:384].rearrange("p o n -> p (o n)"), start=False, stop=True)
                last.then_inc(S("t_full"), 1)
            chunk(xh, xl, KT)
            for b in range(4):
                pe.wait_ge(S(f"t_free{b}"), t.at(f"bank{b}", 1))
            before = []
            for c in range(2):
                s = chunk(plh, pll, 8)
                before.append((f"mm_free{s}", t.at(f"set{s}", 1)))
            for c in range(2):
                pe.wait_ge(S(before[c][0]), before[c][1])
                for k2 in range(2):
                    to_bank(mxs[:, c, :, :], k2 * 256)
        columns(yh, yl, 32, ready=lambda k: pe.wait_ge(S("y_lo"), k // 8 + 1) if k % 8 == 0 else None)

        def layer_end(n):
            pe.wait_ge(S(f"ple_in{n}"), 16)
            xpose(ptok, 2)
            ready = last_banks(1)
            for c in range(NCH):
                chunk(ph, pl, 2, ready=ready if c == 0 else None)
            xpose(h, KT, lambda g: pe.wait_ge(S(f"h_post{n}"), g // 2 + 1))
            columns(ready=last_banks(8))

        layer_end(0)
        gated(pe, 0)
        xpose(h, KT)
        ready = last_banks(8)
        for n, width in enumerate((512, 512, 64)):
            chunk(xh, xl, KT, width, ready if n == 0 else None)
        columns()
        pe.wait_ge(S("k_roped"), 1)
        b = take_bank()
        for tt in range(2):
            last = pe.transpose(TB(b)[0:64, tt * 128:tt * 128 + 128], kpe[:, tt, :], ident)
        last.then_inc(S("t_full"), 1)
        xpose(lat[:, :, 0:512], 4)
        ready_q = last_banks(2)
        xpose(lat[:, :, 512:1024], 4)
        ready_kv = last_banks(2)
        for c in range(6):
            chunk(qlh, qll, 4, ready=ready_q if c == 0 else None)
        with pe.Fori(0, 2) as g, t.loop(g, 2, unit=8, chunk=4, set0=2, set1=2):
            for c in range(4):
                chunk(klh, kll, 4, ready=ready_kv if c == 0 else None)

        def attention(name, heads, d, dv, v_src, keys0=128, pe_part=False, forget=False):
            banks_read(pe, t)
            with pe.Fori(0, heads // 4) as i, t.loop(i, heads // 4, at=4):
                for j in range(4):
                    B, A = TB(j), ps[:, j, :]
                    pe.wait_ge(S("at_stage"), t.at("at", 1 + j))
                    pe.wait_ge(S("at_PTE"), t.at("at", 1 + j))
                    pe.wait_ge(S("at_done"), t.at("at", 1 + j))
                    pe.sem_inc(S("heads_begun"), 1)
                    for tt in range(2):
                        pe.transpose(B[0:d, tt * 128:tt * 128 + 128], SQ[j][:, tt, 0:d], ident)
                        if pe_part:
                            pe.transpose(A[0:64, tt * 128:tt * 128 + 128], SQ[j][:, tt, 128:192], ident)
                        last = pe.transpose(B[0:d, 256 + tt * 128:384 + tt * 128], SK[j][:, tt, 0:d], ident)
                    last.then_inc(S("at_T"), 1)
                for j in range(4):
                    A = ps[:, j, :]
                    pe.wait_ge(S("at_TE"), t.at("at", 1 + j))
                    for q, (c0, nk) in enumerate(((0, keys0), (keys0, 256))):
                        dst, tok = A[:, c0:c0 + nk], slice(q * 128, q * 128 + 128)
                        if forget:
                            pe.matmul(dst, QP[j][0:2, tok], ck2[:, bass.ds(i * 4 + j, 1), 0:nk].rearrange("p o n -> p (o n)"),
                                      start=True, stop=False)
                        if pe_part:
                            pe.matmul(dst, QP[j][0:64, tok], kpt[:, 0:nk], start=True, stop=False)
                        last = pe.matmul(dst, QK[j][0:d, 0, tok], QK[j][0:d, 1, 0:nk], start=not (forget or pe_part), stop=True)
                    last.then_inc(S("at_S"), 1)
                for j in range(4):
                    B = TB(j)
                    pe.wait_ge(S("at_P"), t.at("at", 1 + j))
                    for n in range((keys0 + 256) // 128):
                        last = pe.transpose(B[:, n * 128:n * 128 + 128], LG_[j][:, n * 128:n * 128 + 128], ident)
                    last.then_inc(S("at_PT"), 1)
                for j in range(4):
                    A = ps[:, j, :]
                    pe.wait_ge(S("at_PTE"), t.at("at", 5 + j))
                    n = 0
                    for q, nb in enumerate((keys0 // 128, 2)):
                        for kb in range(nb):
                            last = pe.matmul(A[:, q * dv:q * dv + dv], PTS[j][:, n, :], v_src(kb, i * 4 + j),
                                             start=kb == 0, stop=kb == nb - 1)
                            n += 1
                    last.then_inc(S("at_O"), 1)
                t.add("at", 4)
            pe.wait_ge(S("at_done"), t.at("at", 4))

        pe.wait_ge(S("mla_ready"), 1)
        attention("mla", HEADS, 128, VD, lambda kb, hd: kv[:, kb, bass.ds(hd * 256 + 128, 128)], pe_part=True)
        xpose(gm, KT)
        columns(ready=last_banks(8))
        layer_end(1)
        pe.wait_ge(S("mem_in"), 16)
        xpose(memt, KT)
        ready = last_banks(8)
        for c in range(2):
            chunk(xh, xl, KT, ready=ready if c == 0 else None)
        gated(pe, 1)
        xpose(h, KT)
        columns(turns=6, ready=last_banks(8))
        chunk(xh, xl, KT, 24)
        evacuated(pe, "z")
        pe.wait_ge(S("hyb_in"), 16 * 7)
        b = take_bank()
        pe.matmul(TB(b)[0:A_H, 0:384], reltab, relone, start=True, stop=True).then_inc(S("t_full"), 1)
        b = take_bank()
        for tt in range(2):
            last = pe.transpose(TB(b)[0:16, tt * 128:tt * 128 + 128], z[:, tt, Z_GL:Z_GL + 16], ident)
        last.then_inc(S("t_full"), 1)
        banks_read(pe, t)
        for tt in range(2):
            b = take_bank()
            pe.matmul(TB(b)[:, 0:C_KW], glt[:, tt * 128:tt * 128 + 128], w2a, start=True, stop=True).then_inc(S("t_full"), 1)
        pe.wait_ge(S("log_forget"), 1)
        b = take_bank()
        pe.matmul(TB(b)[0:B_H, 0:256], lf8[:, 0, :], trio, start=True, stop=False)
        pe.matmul(TB(b)[0:B_H, 128:256], lf8[:, 1, :], trio[:, 0:128], start=False, stop=True).then_inc(S("t_full"), 1)
        pe.wait_ge(S("rel_in"), 16 * A_H)
        for n in range(A_H // 2):
            b = take_bank()
            pe.matmul(TB(b), flip, relb[:, 2 * n:2 * n + 2, :].rearrange("p h n -> p (h n)"), start=True, stop=True).then_inc(S("t_full"), 1)
        attention("a", A_H, 64, 64, lambda kb, hd: z[:, kb, bass.ds(hd * 64 + Z_VA, 64)])
        pe.wait_ge(S("forget_in"), 32)
        attention("b", B_H, 64, 64, lambda kb, hd: z[:, kb, bass.ds(hd * 64 + Z_VB, 64)], forget=True)
        for hd in range(C_H):
            b = take_bank()
            for m, c0 in enumerate((Z_QC, Z_KC)):
                for tt in range(2):
                    last = pe.transpose(TB(b)[0:C_DK, m * 256 + tt * 128:m * 256 + tt * 128 + 128],
                                        z[:, tt, c0 + hd * C_DK:c0 + hd * C_DK + C_DK], ident)
            last.then_inc(S("t_full"), 1)

        def decay_sums(lv):
            s = lv % 2
            if lv >= 2:
                pe.wait_ge(S("gla_e"), lv - 1)
            for hd in range(C_H):
                for tt in range(2):
                    o = ps[0:C_DK, 2 * s + hd // 2, (hd % 2) * 256 + tt * 128:(hd % 2) * 256 + tt * 128 + 128]
                    last = pe.matmul(o, lgd[:, tt, hd * C_DK:hd * C_DK + C_DK], dmat[:, tt if lv == 0 else lv + 1, :], start=True, stop=True)
            last.then_inc(S("gla_d"), 1)

        pe.wait_ge(S("gla_in"), 48)
        decay_sums(0)
        banks_read(pe, t)
        for tt in range(2):
            b = take_bank()
            tok = slice(tt * 128, tt * 128 + 128)
            for hd in range(C_H):
                last = pe.matmul(TB(b)[:, hd * 128:hd * 128 + 128], gk[:, hd, tok], gq[:, hd, tok], start=True, stop=True)
            last.then_inc(S("t_full"), 1)
        for lv in range(8):
            if lv < 7:
                decay_sums(lv + 1)
            pe.wait_ge(S("gla_s"), lv + 1)
            for tt in range(2 if lv else 1):
                b = take_bank()
                ktok = slice(tt * 128, tt * 128 + 128)
                qtok = ktok if lv else slice(128, 256)
                for hd in range(C_H):
                    last = pe.matmul(TB(b)[:, hd * 128:hd * 128 + 128], gks[:, hd, ktok], gqs[:, hd, qtok], start=True, stop=True)
                last.then_inc(S("t_full"), 1)
        banks_read(pe, t)
        pe.wait_ge(S("gla_e"), 8)
        for hd in range(C_H):
            v0, v1 = (z[:, tt, Z_VC + hd * C_DV:Z_VC + (hd + 1) * C_DV] for tt in range(2))
            pe.matmul(ps[:, hd, 0:C_DV], gat[:, 0, hd, :], v0, start=True, stop=True)
            pe.matmul(ps[:, hd, C_DV:2 * C_DV], gat[:, 2, hd, :], v0, start=True, stop=False)
            last = pe.matmul(ps[:, hd, C_DV:2 * C_DV], gat[:, 1, hd, :], v1, start=False, stop=True)
        last.then_inc(S("gla_o"), 1)
        pe.wait_ge(S("mix_ready"), 1)
        xpose(mix, KT)
        columns(ready=last_banks(8))
        evacuated(pe, "out2")
        xpose(h, KT)
        chunk(xh, xl, KT, ready=last_banks(8))
        evacuated(pe, "cq")
        attention("cross", 4, 128, 128, lambda kb, hd: kvm[:, kb, bass.ds(hd * 128 + 512, 128)], keys0=256)
        xpose(cot, 4)
        ready = last_banks(2)
        for c in range(NCH):
            chunk(xh, xl, 4, ready=ready if c == 0 else None)
        evacuated(pe, "co")
        xpose(h, KT)

        def up_pair(width, ready=None):
            before = []
            for r in (ready, None):
                s = chunk(xh, xl, KT, width, r)
                before.append((f"mm_free{s}", t.at(f"set{s}", 1)))
            for n, src in enumerate((fgs, fvs)):
                pe.wait_ge(S(before[n][0]), before[n][1])
                for k2 in range(2):
                    to_bank(src, k2 * 256, min(2, width // 128 - 2 * k2))

        ready = last_banks(8)
        with pe.Fori(0, 10) as g, t.loop(g, 10, unit=16, chunk=2, set0=1, set1=1, bank=4, bank0=1, bank1=1, bank2=1, bank3=1):
            up_pair(512, ready)
        up_pair(384)
        for c in range(NCH):
            chunk(fyh, fyl, FKT, ready=lambda k: pe.wait_ge(S("fy_lo"), k // 8 + 1) if k % 8 == 0 and c == 0 else None)
        assert t.n["unit"] == TOTAL_UNITS and t.n["chunk"] == CHUNKS_END["down"], t.n

    @block.scalar
    def _(act):
        t = Tally()

        def hi(k):
            for _ in range(k):
                u = t.n.get("unit", 0)
                if t.reg is not None or u < TOTAL_UNITS:
                    slot = u % RAW
                    full = 16 * (u // RAW + 1)
                    act.wait_ge(S(f"raw_full{slot}"), t.reg * (t.per["unit"] * 16 // RAW) + full if t.reg is not None else full)
                    act.wait_ge(S("w_used"), t.at("unit", 1))
                    act.activation(w_hi[:, u % RING, :], raw[:, slot, :], ACT.Copy).then_inc(S("w_hi"), 1)
                t.add("unit")

        def chunk(units):
            hi(units)
            s = t.n.get("chunk", 0) % 2
            t.add("chunk")
            act.wait_ge(S("w_used"), t.at("unit", RING - LEAD))
            return s

        def skip(units):
            hi(units)
            t.add("chunk")

        def xpose_hi(dst, nkt, g0=None):
            for g in range(nkt // 2):
                act.wait_ge(S("t_full"), t.at("bank", 1))
                bank = TB(t.n["bank"] % 4)
                if g0 is None:
                    last = act.activation(dst[:, 2 * g:2 * g + 2, :].rearrange("p k n -> p (k n)"), bank, ACT.Copy)
                else:
                    for k in range(2):
                        last = act.activation(dst[:, 2 * g + k, :], bank[:, k * 256:k * 256 + 256], ACT.Copy,
                                              scale=gain[:, g0 + 2 * g + k:g0 + 2 * g + k + 1])
                last.then_inc(S("x_hi"), 1)
                t.add("bank")

        def square(src, dst, scale=1.0):
            if t.n.get("junk"):
                act.wait_ge(S("junk_written"), t.at("junk"))
            act.activation(junk, src, ACT.Square, scale=scale, accum_out=dst).then_inc(S("junk_written"), 1)
            t.add("junk")

        def squares(src, slot):
            for tt in range(2):
                for c in range(NCH):
                    square(src[:, tt, c * 512:(c + 1) * 512], sums[:, slot, tt, c:c + 1])
            act.wait_ge(S("junk_written"), t.at("junk"))
            act.sem_inc(S(f"sums{slot}"), 1)

        def root(slot):
            act.wait_ge(S(f"mean_square{slot}"), 1)
            act.activation(rt[:, slot, :], ms[:, slot, :], ACT.Sqrt).then_inc(S(f"root{slot}"), 1)

        def read_out(s, dst, func=ACT.Copy, scale=None, width=512):
            for tt in range(2):
                last = act.activation(dst(tt), MM(s, tt)[:, 0:width], func, scale=1.0 if scale is None else rstd[:, scale, tt:tt + 1])
            last.then_inc(S(f"mm_free{s}"), 1)

        hi(LEAD)
        act.wait_ge(S("t_full"), 1)
        for n, tile in enumerate(GAIN_TILES):
            r = sum(x for _, x in tile)
            last = act.activation(gain[:, n * 128:n * 128 + r], TB(0)[:, n * 128:n * 128 + r], ACT.Copy)
        last.then_inc(S("t_free0"), 1)
        t.add("bank")
        act.wait_ge(S("t_free0"), 2)
        xpose_hi(xh, KT, GAIN["pre0"])
        squares(h, 0)
        root(0)
        act.wait_ge(S("rope_reduced"), 2)
        act.activation(rc_sin, ang, ACT.Sin)
        act.activation(rc_cos, red, ACT.Sin).then_inc(S("rope_tables"), 1)
        act.wait_ge(S("rstd0"), 1)
        with act.Fori(0, WB) as g, t.loop(g, WB, unit=UNITS_POOL, chunk=6, bank=8):
            for c in range(2):
                read_out(chunk(8), lambda tt: ut[:, tt, c * 512:c * 512 + 512], scale=0)
            for c in range(2):
                read_out(chunk(8), lambda tt: sg[:, tt, c * 512:c * 512 + 512], ACT.Silu, scale=0)
                if c == 0:
                    xpose_hi(plh, 8)
            for c in range(2):
                skip(4)
            for c in range(2):
                for k2 in range(2):
                    b = t.n["bank"] % 4
                    act.wait_ge(S("t_full"), t.at("bank", 1))
                    for k in range(2):
                        f = c * 4 + 2 * k2 + k
                        last = act.activation(y32[:, bass.ds(g * 8 + f, 1), :].rearrange("p o n -> p (o n)"),
                                              TB(b)[:, k * 256:k * 256 + 256], ACT.Copy,
                                              scale=gain[:, bass.ds(g * 8 + (GAIN["pool_scale"] + f), 1)])
                    last.then_inc(S(f"t_free{b}"), 1)
                    t.add("bank")
        banks_read(act, t)
        products(act, "pool")
        for n in range(4):
            act.activation(yh[:, 8 * n:8 * n + 8, :], y32[:, 8 * n:8 * n + 8, :], ACT.Copy).then_inc(S("y_hi"), 1)

        def mixer_out(units, slot):
            with act.Fori(0, 2) as g, t.loop(g, 2, unit=2 * units, chunk=2, junk=4):
                for c in range(2):
                    s = chunk(units)
                    for tt in range(2):
                        square(MM(s, tt), sums[:, slot, tt, bass.ds(g * 2 + c, 1)])
                    read_out(s, lambda tt: outt[:, tt, bass.ds(g * 1024 + c * 512, 512)])

        def layer_end(n, slot):
            root(slot)
            xpose_hi(ph, 2)
            for c in range(NCH):
                read_out(chunk(1), lambda tt: proj[:, tt, c * 512:(c + 1) * 512])
            xpose_hi(xh, KT, GAIN[f"ple{n}"])
            squares(h, slot + 1)
            root(slot + 1)
            act.wait_ge(S(f"rstd{slot + 1}"), 1)
            with act.Fori(0, 2) as g, t.loop(g, 2, unit=16, chunk=2, gated=2):
                for c in range(2):
                    s = chunk(8)
                    act.wait_ge(S("gated"), t.at("gated", 1))
                    t.add("gated")
                    read_out(s, lambda tt: sig[:, c, tt, :], ACT.Sigmoid, scale=slot + 1)

        mixer_out(16, 1)
        layer_end(0, 1)
        xpose_hi(xh, KT, GAIN["pre1"])
        squares(h, 3)
        root(3)
        act.wait_ge(S("rstd3"), 1)
        for c in range(2):
            s = chunk(8)
            for tt in range(2):
                square(MM(s, tt), sums[:, 4 + c, tt, 0:1], rstd[:, 3, tt:tt + 1])
            read_out(s, lambda tt: lat[:, tt, c * 512:(c + 1) * 512], scale=3)
        read_out(chunk(1), lambda tt: kpe[:, tt, :], scale=3, width=64)
        with act.Fori(0, 2) as g, t.loop(g, 2, unit=16, chunk=2):
            for c in range(2):
                read_out(chunk(8), lambda tt: gm[:, tt, bass.ds(g * 1024 + c * 512, 512)], ACT.Silu, scale=3)
        root(4)
        root(5)
        act.wait_ge(S("t_full"), t.at("bank", 1))
        b = t.n["bank"] % 4
        act.activation(kpt, TB(b)[0:64, 0:256], ACT.Copy).then_inc(S(f"t_free{b}"), 1)
        t.add("bank")
        xpose_hi(qlh, 4, GAIN["q_norm"])
        xpose_hi(klh, 4, GAIN["kv_norm"])
        act.wait_ge(S("rstd4"), 1)
        act.wait_ge(S("rstd5"), 1)
        for c in range(6):
            read_out(chunk(2), lambda tt: qt[:, tt, c * 512:(c + 1) * 512], scale=4)
        with act.Fori(0, 2) as g, t.loop(g, 2, unit=8, chunk=4):
            for c in range(4):
                read_out(chunk(2), lambda tt: kv[:, tt, bass.ds(g * 2048 + c * 512, 512)], scale=5)

        def attention(heads, d, keys0=128, pe_part=False):
            nk = keys0 + 256
            with act.Fori(0, heads // 4) as i, t.loop(i, heads // 4, at=4):
                for j in range(4):
                    act.wait_ge(S("at_T"), t.at("at", 1 + j))
                    if pe_part:
                        act.activation(QP[j], ps[0:64, j, 0:256], ACT.Copy)
                    act.activation(QK[j][0:d], TB(j)[0:d, :].rearrange("p (m n) -> p m n", m=2), ACT.Copy).then_inc(S("at_TE"), 1)
                for j in range(4):
                    act.wait_ge(S("at_L"), t.at("at", 1 + j))
                    for q, (c0, n) in enumerate(((0, keys0), (keys0, 256))):
                        last = act.activation(LG_[j][:, c0:c0 + n], LG_[j][:, c0:c0 + n], ACT.Exp, bias=nmx[:, j, q:q + 1],
                                              accum_out=psm[:, j, q:q + 1])
                    last.then_inc(S("at_P"), 1)
                for j in range(4):
                    act.wait_ge(S("at_PT"), t.at("at", 1 + j))
                    act.activation(PTS[j].rearrange("p k n -> p (k n)")[:, 0:nk], TB(j)[:, 0:nk], ACT.Copy).then_inc(S("at_PTE"), 1)
                t.add("at", 4)

        attention(HEADS, 128, pe_part=True)
        heads_done(act, "a")
        xpose_hi(xh, KT)
        mixer_out(8, 6)
        layer_end(1, 6)
        xpose_hi(xh, KT, GAIN["mem"])
        squares(memt, 8)
        root(8)
        act.wait_ge(S("rstd8"), 1)
        for c in range(2):
            read_out(chunk(8), lambda tt: kvm[:, tt, c * 512:(c + 1) * 512], scale=8)
        xpose_hi(xh, KT, GAIN["mix"])
        squares(h, 9)
        root(9)
        act.wait_ge(S("rstd9"), 1)
        with act.Fori(0, 6) as g, t.loop(g, 6, unit=16, chunk=2):
            for c in range(2):
                read_out(chunk(8), lambda tt: z[:, tt, bass.ds(g * 1024 + c * 512, 512)], scale=9)
        read_out(chunk(1), lambda tt: z[:, tt, 6144:Z_W], scale=9, width=24)
        act.wait_ge(S("t_full"), t.at("bank", 1))
        b = t.n["bank"] % 4
        act.activation(relrow, TB(b)[0:A_H, 0:384], ACT.Copy).then_inc(S(f"t_free{b}"), 1)
        t.add("bank")
        act.wait_ge(S("ones_set"), 2)
        act.wait_ge(S("t_full"), t.at("bank", 1))
        b = t.n["bank"] % 4
        act.activation(glt[0:16, :], TB(b)[0:16, 0:256], ACT.Copy).then_inc(S(f"t_free{b}"), 1)
        t.add("bank")
        banks_read(act, t)
        act.dma_start(rel_scratch, relrow).then_inc(S("rel_out"), 16)
        act.wait_ge(S("rel_out"), 16)
        for hd in range(A_H):
            act.dma_start(relb[:, hd, :], bass.AP(tensor=rel_scratch.tensor, offset=hd * 384, ap=[[1, 128], [1, 256]]))\
               .then_inc(S("rel_in"), 16)
        t.add("bank", 2)
        act.wait_ge(S("gate_abs"), 1)
        act.activation(la, la, ACT.Exp, scale=-1.0).then_inc(S("gate_exp"), 1)
        act.wait_ge(S("gate_exp"), 1)
        act.activation(la, la, ACT.Ln, bias=1.0).then_inc(S("gate_exp"), 1)
        act.wait_ge(S("t_full"), t.at("bank", 1))
        b = t.n["bank"] % 4
        act.activation(crow, TB(b)[0:B_H, 0:256], ACT.Copy)
        act.activation(ncrow, TB(b)[0:B_H, 0:256], ACT.Copy, scale=-1.0).then_inc(S(f"t_free{b}"), 1)
        t.add("bank")
        for n in range(A_H // 2):
            act.wait_ge(S("t_full"), t.at("bank", 1))
            b = t.n["bank"] % 4
            act.activation(relb[:, 2 * n:2 * n + 2, :].rearrange("p h n -> p (h n)"), TB(b), ACT.Copy).then_inc(S(f"t_free{b}"), 1)
            t.add("bank")
        banks_read(act, t)
        act.sem_inc(S("sums_read"), 1)
        attention(A_H, 64)
        heads_done(act, "b")
        act.wait_ge(S("forget_ones"), 2)
        act.dma_start(ck2[0:1, :, :].rearrange("o h t -> o (h t)"), ncrow).then_inc(S("forget_in"), 16)
        act.dma_start(cq2[1:2, :, :].rearrange("o h t -> o (h t)"), crow).then_inc(S("forget_in"), 16)
        attention(B_H, 64)
        heads_done(act, "cross")
        for hd in range(C_H):
            act.wait_ge(S("t_full"), t.at("bank", 1))
            b = t.n["bank"] % 4
            act.activation(gq[:, hd, :], TB(b)[0:C_DK, 0:256], ACT.Copy, scale=C_DK ** -0.5)
            act.activation(gk[:, hd, :], TB(b)[0:C_DK, 256:512], ACT.Copy).then_inc(S(f"t_free{b}"), 1)
            t.add("bank")
        for lv in range(8):
            act.wait_ge(S("gla_d"), lv + 1)
            if lv:
                act.wait_ge(S("gla_s"), lv)
            s = lv % 2
            act.activation(ge, ps[0:C_DK, 2 * s:2 * s + 2, :].rearrange("p b (h n) -> p (b h) n", h=2), ACT.Exp, scale=1.0 / 16.0)\
               .then_inc(S("gla_e"), 1)
        for tt in range(2):
            last = act.activation(mix[:, tt, A_W + B_W:D], z[:, tt, Z_RC:Z_RC + C_VW], ACT.Silu)
        last.then_inc(S("rc_silu"), 1)
        act.wait_ge(S("gla_ms"), 1)
        act.activation(cst[:, 1, :], cst[:, 0, :], ACT.Sqrt).then_inc(S("gla_root"), 1)
        t.add("bank", 2 + 1 + 2 * 7)
        act.wait_ge(S("gla_o"), 1)
        xpose_hi(xh, KT)
        for c in range(NCH):
            skip(8)
        products(act, "out2")
        xpose_hi(xh, KT, GAIN["cross"])
        evacuated(act, "out2")
        squares(h, 10)
        root(10)
        act.wait_ge(S("rstd10"), 1)
        read_out(chunk(8), lambda tt: cqt[:, tt, :], scale=10)
        attention(4, 128, keys0=256)
        heads_done(act, "end")
        xpose_hi(xh, 4)
        for c in range(NCH):
            skip(2)
        products(act, "co")
        xpose_hi(xh, KT, GAIN["ffn"])
        evacuated(act, "co")
        squares(h, 11)
        root(11)
        act.wait_ge(S("rstd11"), 1)

        def up_pair(width):
            read_out(chunk(8), lambda tt: fgs[:, tt, 0:width], scale=11, width=width)
            skip(8)
            act.wait_ge(S("conv_done"), t.at("conv", 1))
            act.activation(fcv[:, 0:width // 128, :], fcv[:, 0:width // 128, :], ACT.Silu).then_inc(S("conv_silu"), 1)
            t.add("conv")
            t.add("bank", 4)

        with act.Fori(0, 10) as g, t.loop(g, 10, unit=16, chunk=2, conv=1, bank=4):
            up_pair(512)
        up_pair(384)
        banks_read(act, t)
        for n in range(6):
            k = slice(8 * n, min(8 * n + 8, FKT))
            act.activation(fyh[:, k, :], fy[:, k, :], ACT.Copy).then_inc(S("fy_hi"), 1)
        for c in range(NCH):
            skip(len(units_of(FKT)))
        evacuated(act, "down")
        squares(h, 12)
        root(12)

    @block.vector
    def _(dve):
        t = Tally()
        dve.sem_inc(S("w_lo"), RAW)
        for name in ("mm_free0", "mm_free1", "t_free0", "t_free1", "t_free2", "t_free3"):
            dve.sem_inc(S(name), 1)
        dve.sem_inc(S("gated"), 2)
        dve.sem_inc(S("at_done"), 4)
        dve.sem_inc(S("at_PTE"), 4)

        def link(ins):
            ins.then_inc(S("dve_chain"), 1)
            t.add("chain")
            dve.wait_ge(S("dve_chain"), t.at("chain"))

        def lo(k):
            for _ in range(k):
                u = t.n.get("unit", 0)
                if t.reg is not None or u < TOTAL_UNITS:
                    dve.wait_ge(S("w_hi"), t.at("unit", 1))
                    dve.tensor_tensor(w_lo[:, u % RING, :], raw[:, u % RAW, :], w_hi[:, u % RING, :].bitcast(F32), ALU.subtract)\
                       .then_inc(S("w_lo"), 1)
                t.add("unit")

        def chunk(units):
            lo(units)
            s = t.n.get("chunk", 0) % 2
            t.add("chunk")
            dve.wait_ge(S("w_used"), t.at("unit", RING - LEAD))
            return s

        def skip(units):
            lo(units)
            t.add("chunk")

        def xpose_lo(dst, hi_part, nkt, g0=None):
            for g in range(nkt // 2):
                dve.wait_ge(S("x_hi"), t.at("xh", 1))
                b = t.n["bank"] % 4
                if g0 is None:
                    k = slice(2 * g, 2 * g + 2)
                    last = dve.tensor_tensor(dst[:, k, :].rearrange("p k n -> p (k n)"), TB(b),
                                             hi_part[:, k, :].rearrange("p k n -> p (k n)").bitcast(F32), ALU.subtract)
                else:
                    for k in range(2):
                        c = g0 + 2 * g + k
                        last = dve.scalar_tensor_tensor(dst[:, 2 * g + k, :], TB(b)[:, k * 256:k * 256 + 256], gain[:, c:c + 1],
                                                        hi_part[:, 2 * g + k, :].bitcast(F32), ALU.mult, ALU.subtract)
                last.then_inc(S(f"t_free{b}"), 1)
                t.add("bank")
                t.add("xh")

        def mean(slot, width, cols=NCH):
            link(dve.reduce_sum(ms[:, slot, :], sums[:, slot, :, 0:cols], AXX))
            dve.tensor_scalar(ms[:, slot, :], ms[:, slot, :], 1.0 / width, EPS, ALU.mult, ALU.add).then_inc(S(f"mean_square{slot}"), 1)

        def inverse(slot):
            dve.wait_ge(S(f"root{slot}"), 1)
            dve.reciprocal(rstd[:, slot, :], rt[:, slot, :]).then_inc(S(f"rstd{slot}"), 1)
            dve.wait_ge(S(f"rstd{slot}"), 1)

        def norm(slot, width=D):
            dve.wait_ge(S(f"sums{slot}"), 1)
            mean(slot, width)
            inverse(slot)

        dve.wait_ge(S("pos_in"), 32)
        link(dve.tensor_copy(posf, posi))
        for tt in range(2):
            last = dve.tensor_scalar(ang[:, tt, :], freqs, posf[:, tt:tt + 1], None, ALU.mult)
        link(last)
        ROUND = 1.5 * 2.0 ** 23
        PI = float(np.float32(3.1415925))
        link(dve.tensor_scalar(turns_, ang, 1.0 / (2 * math.pi), None, ALU.mult))
        link(dve.tensor_scalar(turns_, turns_, ROUND, ROUND, ALU.add, ALU.subtract))
        link(dve.scalar_tensor_tensor(ang, turns_, -6.28125, ang, ALU.mult, ALU.add))
        link(dve.scalar_tensor_tensor(ang, turns_, -(2 * math.pi - 6.28125), ang, ALU.mult, ALU.add))
        link(dve.tensor_scalar(red, ang, math.pi / 2, math.pi, ALU.add, ALU.is_gt))
        link(dve.tensor_scalar(red, red, -2 * math.pi, math.pi / 2, ALU.mult, ALU.add))
        link(dve.tensor_tensor(red, red, ang, ALU.add))
        dve.tensor_scalar(red, red, PI, -PI, ALU.min, ALU.max).then_inc(S("rope_reduced"), 1)
        dve.tensor_scalar(ang, ang, PI, -PI, ALU.min, ALU.max).then_inc(S("rope_reduced"), 1)

        lo(LEAD)
        t.add("bank")
        dve.wait_ge(S("t_free0"), 2)
        xpose_lo(xl, xh, KT, GAIN["pre0"])
        norm(0)
        with dve.Fori(0, WB) as g, t.loop(g, WB, unit=UNITS_POOL, chunk=6, bank=8, xh=4):
            for c in range(3):
                skip(8)
            xpose_lo(pll, plh, 8)
            skip(8)
            for c in range(2):
                s = chunk(4)
                if c == 0:
                    for k in range(2):
                        dve.wait_ge(S(f"mm_free{k}"), t.reg * 3 + (t.n["chunk"] - 1) // 2 + 1)
                for tt in range(2):
                    last = dve.tensor_tensor(mxs[:, c, tt, :], MM(s, tt), sg[:, tt, c * 512:(c + 1) * 512], ALU.mult)
                last.then_inc(S(f"mm_free{s}"), 1)
            t.add("bank", 4)
        for n in range(4):
            dve.wait_ge(S("y_hi"), n + 1)
            dve.tensor_tensor(yl[:, 8 * n:8 * n + 8, :], y32[:, 8 * n:8 * n + 8, :], yh[:, 8 * n:8 * n + 8, :].bitcast(F32), ALU.subtract)\
               .then_inc(S("y_lo"), 1)

        def columns(turns=2, units=8):
            with dve.Fori(0, turns) as g, t.loop(g, turns, unit=2 * units, chunk=2):
                for c in range(2):
                    skip(units)

        def layer_end(n, slot, mixer):
            evacuated(dve, mixer)
            mean(slot, D)
            inverse(slot)
            dve.wait_ge(S(f"post_gain_in{n}"), 16)
            for c in range(NCH):
                cols = slice(c * 512, c * 512 + 512)
                for tt in range(2):
                    last = dve.scalar_tensor_tensor(outt[:, tt, cols], outt[:, tt, cols], rstd[:, slot, tt:tt + 1], pgain[:, cols],
                                                    ALU.mult, ALU.mult)
                link(last)
                for tt in range(2):
                    last = dve.tensor_tensor(h[:, tt, cols], h[:, tt, cols], outt[:, tt, cols], ALU.add)
                last.then_inc(S(f"h_post{n}"), 1)
            xpose_lo(pl, ph, 2)
            for c in range(NCH):
                skip(1)
            xpose_lo(xl, xh, KT, GAIN[f"ple{n}"])
            norm(slot + 1)
            evacuated(dve, f"proj{n}")
            with dve.Fori(0, 2) as g, t.loop(g, 2, unit=16, chunk=2, chain=2):
                for c in range(2):
                    s = chunk(8)
                    k = t.n["chunk"] - 1
                    dve.wait_ge(S(f"mm_free{s}"), g * 1 + (k // 2 + 2))
                    for tt in range(2):
                        last = dve.tensor_tensor(sig[:, c, tt, :], sig[:, c, tt, :], proj[:, tt, bass.ds(g * 1024 + c * 512, 512)], ALU.mult)
                    link(last)
                    for tt in range(2):
                        hc = h[:, tt, bass.ds(g * 1024 + c * 512, 512)]
                        last = dve.tensor_tensor(hc, hc, sig[:, c, tt, :], ALU.add)
                    last.then_inc(S("gated"), 1)

        columns(units=16)
        layer_end(0, 1, "pool_out")
        xpose_lo(xl, xh, KT, GAIN["pre1"])
        norm(3)
        skip(8)
        skip(8)
        skip(1)
        columns()
        evacuated(dve, "mla_in")
        products(dve, "mla_in")
        for c in range(2):
            mean(4 + c, Q_RANK, 1)
        inverse(4)
        inverse(5)

        def rope(x1, x2, cos, sin, tmp):
            link_all = [dve.tensor_tensor(tmp[0], x1, cos, ALU.mult), dve.tensor_tensor(tmp[1], x2, sin, ALU.mult),
                        dve.tensor_tensor(tmp[2], x2, cos, ALU.mult), dve.tensor_tensor(tmp[3], x1, sin, ALU.mult)]
            link(link_all[-1])
            dve.tensor_tensor(x1, tmp[0], tmp[1], ALU.subtract)
            return dve.tensor_tensor(x2, tmp[2], tmp[3], ALU.add)

        dve.wait_ge(S("rope_tables"), 1)
        last = rope(kpe[:, :, 0:32], kpe[:, :, 32:64], rc_cos, rc_sin, [x[:, :, 0, :] for x in (ra, rb, rc_, rd)])
        last.then_inc(S("k_roped"), 1)
        t.add("bank")
        xpose_lo(qll, qlh, 4, GAIN["q_norm"])
        xpose_lo(kll, klh, 4, GAIN["kv_norm"])
        for c in range(6):
            skip(2)
        with dve.Fori(0, 2) as g, t.loop(g, 2, unit=8, chunk=4):
            for c in range(4):
                skip(2)
        evacuated(dve, "uq")
        q4 = qt.rearrange("p t (h e) -> p t h e", e=192)
        for tt in range(2):
            cos, sin = (x[:, tt, :].unsqueeze(1).broadcast_to([128, HEADS, 32]) for x in (rc_cos, rc_sin))
            last = rope(q4[:, tt, :, 128:160], q4[:, tt, :, 160:192], cos, sin, [x[:, tt] for x in (ra, rb, rc_, rd)])
        link(last)
        evacuated(dve, "ukv")
        products(dve, "ukv")
        dve.sem_inc(S("mla_ready"), 2)

        def attention(heads, dv, scale, mask, put, keys0=128):
            with dve.Fori(0, heads // 4) as i, t.loop(i, heads // 4, at=4, chain=8):
                for j in range(4):
                    dve.wait_ge(S("at_S"), t.at("at", 1 + j))
                    for q, (c0, nk) in enumerate(((0, keys0), (keys0, 256))):
                        src, dst = ps[:, j, c0:c0 + nk], LG_[j][:, c0:c0 + nk]
                        if mask is None:
                            last = dve.tensor_scalar(dst, src, scale, None, ALU.mult)
                        else:
                            last = dve.scalar_tensor_tensor(dst, src, scale, mask(i * 4 + j)[:, 256 - nk:256], ALU.mult, ALU.add)
                    link(last)
                    for q, (c0, nk) in enumerate(((0, keys0), (keys0, 256))):
                        last = dve.reduce_max(nmx[:, j, q:q + 1], LG_[j][:, c0:c0 + nk], AXX, negate=True)
                    last.then_inc(S("at_L"), 1)
                for j in range(4):
                    dve.wait_ge(S("at_O"), t.at("at", 1 + j))
                    link(dve.reciprocal(prc[:, j, :], psm[:, j, :]))
                    for q in range(2):
                        last = put(q, i * 4 + j, ps[:, j, q * dv:q * dv + dv], prc[:, j, q:q + 1])
                    last.then_inc(S("at_done"), 1)
                t.add("at", 4)

        def into(dst, dv, col):
            return lambda q, hd, src, r: dve.tensor_scalar(dst[:, q, bass.ds(hd * dv + col, dv)], src, r, None, ALU.mult)

        def gated_into(q, hd, src, r):
            g = gm[:, q, bass.ds(hd * VD, VD)]
            return dve.scalar_tensor_tensor(g, src, r, g, ALU.mult, ALU.mult)

        dve.wait_ge(S("causal_in"), 16)
        attention(HEADS, VD, (NOPE + ROPE) ** -0.5, lambda hd: causal, gated_into)
        t.add("bank", 8)
        t.n["bank"] -= 8
        xpose_lo(xl, xh, KT)
        columns()
        layer_end(1, 6, "mla_out")
        xpose_lo(xl, xh, KT, GAIN["mem"])
        norm(8)
        skip(8)
        skip(8)
        xpose_lo(xl, xh, KT, GAIN["mix"])
        norm(9)
        columns(6)
        skip(1)
        evacuated(dve, "z")
        products(dve, "z")
        dve.wait_ge(S("hyb_in"), 16 * 7)
        t.add("bank", 2)
        for tt in range(2):
            dve.tensor_tensor(lx[:, tt, C_KW:C_KW + B_H], z[:, tt, Z_FL:Z_FL + B_H], fbias, ALU.add)
        for tt in range(2):
            dve.wait_ge(S("t_full"), t.at("bank", 1))
            b = t.n["bank"] % 4
            dve.tensor_copy(lx[:, tt, 0:C_KW], TB(b)[:, 0:C_KW]).then_inc(S(f"t_free{b}"), 1)
            t.add("bank")
        t.add("bank")
        for b in range(2):
            n = t.n["bank"] - 3 + b
            dve.wait_ge(S(f"t_free{n % 4}"), n // 4 + 2)
        link(dve.tensor_scalar(lm, lx, 0.0, None, ALU.min))
        dve.scalar_tensor_tensor(la, lx, 0.0, lm, ALU.max, ALU.subtract).then_inc(S("gate_abs"), 1)
        dve.wait_ge(S("gate_exp"), 2)
        link(dve.tensor_tensor(lgd, lm, la, ALU.subtract))
        dve.tensor_scalar(lf8, lgd[:, :, C_KW:C_KW + B_H], 8.0, None, ALU.mult).then_inc(S("log_forget"), 1)
        t.add("bank", A_H // 2)
        banks_read(dve, t)
        attention(A_H, 64, 0.125, lambda hd: relb[:, bass.ds(hd, 1), :].rearrange("p o n -> p (o n)"), into(mix, 64, 0))
        attention(B_H, 64, 0.125, lambda hd: causal, into(mix, 64, A_W))
        t.add("bank", C_H)
        dve.wait_ge(S("gla_in"), 48)

        def attn_part(tt, lv, first=False):
            dve.wait_ge(S("t_full"), t.at("bank", 1))
            b = t.n["bank"] % 4
            src = TB(b).rearrange("p (h n) -> p h n", h=C_H)
            if first:
                ins = dve.tensor_tensor(gat[:, tt], src, gmask[:, 0, :].unsqueeze(1).broadcast_to([128, C_H, 128]), ALU.mult)
            elif lv == 0:
                ins = dve.tensor_copy(gat[:, 2], src)
            else:
                ins = dve.copy_predicated(gat[:, tt], gmask[:, lv, :].bitcast(I32).unsqueeze(1).broadcast_to([128, C_H, 128]), src)
            ins.then_inc(S(f"t_free{b}"), 1)
            t.add("bank")

        for tt in range(2):
            attn_part(tt, 0, True)
        banks_read(dve, t)
        for lv in range(8):
            dve.wait_ge(S("gla_e"), lv + 1)
            dve.tensor_tensor(gqs, gq, ge, ALU.mult)
            dve.tensor_tensor(gks, gk, ge, ALU.mult).then_inc(S("gla_s"), 1)
            for tt in range(2 if lv else 1):
                attn_part(tt, lv)
            banks_read(dve, t)
        dve.wait_ge(S("gla_o"), 1)
        for tt in range(2):
            last = dve.tensor_copy(oc[:, tt], ps[:, 0:4, tt * C_DV:(tt + 1) * C_DV])
        link(last)
        link(dve.tensor_tensor(osq, oc, oc, ALU.mult))
        link(dve.reduce_sum(cst[:, 0, :], osq.rearrange("p t h n -> p (t h) n"), AXX))
        dve.tensor_scalar(cst[:, 0, :], cst[:, 0, :], 1.0 / C_DV, EPS, ALU.mult, ALU.add).then_inc(S("gla_ms"), 1)
        dve.wait_ge(S("gla_root"), 1)
        link(dve.reciprocal(cst[:, 2, :], cst[:, 1, :]))
        oc8 = oc.rearrange("p t h n -> p (t h) n")
        link(dve.tensor_tensor(oc8, oc8, cst[:, 2, :].unsqueeze(2).broadcast_to([128, 8, C_DV]), ALU.mult))
        link(dve.tensor_tensor(oc8, oc8, cnb.unsqueeze(1).broadcast_to([128, 8, C_DV]), ALU.mult))
        dve.wait_ge(S("rc_silu"), 1)
        mc = mix[:, :, A_W + B_W:D]
        dve.tensor_tensor(mc, mc, oc.rearrange("p t h n -> p t (h n)"), ALU.mult).then_inc(S("mix_ready"), 1)
        xpose_lo(xl, xh, KT)

        def add_chunk(s, col):
            for tt in range(2):
                hc = h[:, tt, bass.ds(col, 512)]
                last = dve.tensor_tensor(hc, hc, MM(s, tt), ALU.add)
            last.then_inc(S(f"mm_free{s}"), 1)

        with dve.Fori(0, 2) as g, t.loop(g, 2, unit=16, chunk=2):
            for c in range(2):
                add_chunk(chunk(8), g * 1024 + c * 512)
        xpose_lo(xl, xh, KT, GAIN["cross"])
        norm(10)
        skip(8)
        attention(4, 128, 128 ** -0.5, None, into(cot, 128, 0), keys0=256)
        xpose_lo(xl, xh, 4)
        for c in range(NCH):
            add_chunk(chunk(2), c * 512)
        xpose_lo(xl, xh, KT, GAIN["ffn"])
        norm(11)

        def up_pair(width, tile):
            nt = width // 128
            skip(8)
            s = chunk(8)
            for tt in range(2):
                last = dve.tensor_scalar(fvs[:, tt, 0:width], MM(s, tt)[:, 0:width], rstd[:, 11, tt:tt + 1], None, ALU.mult)
            last.then_inc(S(f"mm_free{s}"), 1)
            b0 = t.n["bank"] % 4
            bank = lambda k: TB((b0 + k // 2) % 4)[:, (k % 2) * 256:(k % 2) * 256 + 256]
            col = lambda name, k: gain[:, bass.ds(tile + (GAIN[name] + k), 1)]
            dve.wait_ge(S("t_full"), t.at("bank", 2))
            for k in range(nt):
                last = dve.tensor_scalar(fcv[:, k, :], bank(k), col("conv_w2", k), col("conv_b", k), ALU.mult, ALU.add)
            link(last)
            for k in range(nt):
                last = dve.scalar_tensor_tensor(fcv[:, k, 1:T], bank(k)[:, 0:T - 1], col("conv_w1", k), fcv[:, k, 1:T], ALU.mult, ALU.add)
            link(last)
            for k in range(nt):
                last = dve.scalar_tensor_tensor(fcv[:, k, 2:T], bank(k)[:, 0:T - 2], col("conv_w0", k), fcv[:, k, 2:T], ALU.mult, ALU.add)
                if k == 1:
                    last.then_inc(S(f"t_free{b0}"), 1)
                elif k == nt - 1:
                    last.then_inc(S(f"t_free{(b0 + 1) % 4}"), 1)
            t.add("bank", 2)
            dve.wait_ge(S(f"t_free{(b0 + 1) % 4}"), t.at("conv") + (b0_count(b0 + 1)))
            dve.nop().then_inc(S("conv_done"), 1)
            t.add("conv")
            dve.wait_ge(S("conv_silu"), t.at("conv"))
            dve.wait_ge(S("t_full"), t.at("bank", 2))
            for k2 in range(2):
                n = min(2, nt - 2 * k2)
                b = t.n["bank"] % 4
                dve.tensor_tensor(fy[:, bass.ds(tile + 2 * k2, n), :], fcv[:, 2 * k2:2 * k2 + n, :],
                                  TB(b)[:, 0:n * 256].rearrange("p (k n) -> p k n", n=256), ALU.mult).then_inc(S(f"t_free{b}"), 1)
                t.add("bank")

        b_start = t.n["bank"]

        def b0_count(b):
            b %= 4
            n = (b_start - b + 3) // 4
            return n + 2

        with dve.Fori(0, 10) as g, t.loop(g, 10, unit=16, chunk=2, chain=2, bank=4, conv=1):
            up_pair(512, g * 4)
        up_pair(384, 40)
        for n in range(6):
            k = slice(8 * n, min(8 * n + 8, FKT))
            dve.wait_ge(S("fy_hi"), n + 1)
            dve.tensor_tensor(fyl[:, k, :], fy[:, k, :], fyh[:, k, :].bitcast(F32), ALU.subtract).then_inc(S("fy_lo"), 1)
        for c in range(NCH):
            add_chunk(chunk(len(units_of(FKT))), c * 512)
        norm(12)
        dve.wait_ge(S("final_gain_in"), 16)
        for tt in range(2):
            dve.scalar_tensor_tensor(fout[:, tt, :], h[:, tt, :], rstd[:, 12, tt:tt + 1], fgain, ALU.mult, ALU.mult)\
               .then_inc(S("final"), 1)

    @block.gpsimd
    def _(pool):
        t = Tally()

        def stage(heads, d, q_src, k_src, q_cols=None, rows_src=None):
            with pool.Fori(0, heads // 4) as i, t.loop(i, heads // 4, at=4):
                for j in range(4):
                    if j == 0:
                        pool.wait_ge(S("at_done"), t.at("at", 4))
                    pool.tensor_copy(SQ[j][:, :, 0:q_cols or d], q_src(i * 4 + j))
                    if rows_src is not None:
                        pool.tensor_copy(QP[j][0:2, :], rows_src(i * 4 + j))
                    pool.tensor_copy(SK[j][:, :, 0:d], k_src(i * 4 + j)).then_inc(S("at_stage"), 1)
                t.add("at", 4)

        def load(dst, src, sem):
            pool.dma_start(dst, src).then_inc(S(sem), 16)

        def layer_end(n):
            products(pool, "pool" if n == 0 else "ukv", 1)
            load(pgain, a["post_norm"][n:n + 1, :].broadcast_to([128, D]), f"post_gain_in{n}")
            load(ptok, tokens(a["p"][n, 0]), f"ple_in{n}")

        layer_end(0)
        pool.wait_ge(S("mla_ready"), 2)
        stage(HEADS, 128, lambda hd: qt[:, :, bass.ds(hd * 192, 192)], lambda hd: kv[:, :, bass.ds(hd * 256, 128)], q_cols=192)
        layer_end(1)
        load(memt, tokens(a["mem_2"][0]), "mem_in")
        products(pool, "z")
        pool.memset(reltab, 1.0).then_inc(S("ones_set"), 1)
        pool.memset(glt, 1.0).then_inc(S("ones_set"), 1)
        load(relone, a["c_rel"], "hyb_in")
        load(w2a[0:16, :], a["c_gate_w2_2"][0], "hyb_in")
        load(w2a[16:17, :], a["c_gate_b_2"], "hyb_in")
        load(fbias, a["f_bias_2"].broadcast_to([128, B_H]), "hyb_in")
        load(trio, a["c_trio"], "hyb_in")
        load(flip, a["c_flip"], "hyb_in")
        pool.wait_ge(S("ones_set"), 2)
        load(reltab[0:BUCKETS, :], a["rel_table_2"], "hyb_in")
        pool.wait_ge(S("log_forget"), 1)
        pool.wait_ge(S("rel_out"), 16)
        pool.wait_ge(S("sums_read"), 1)
        stage(A_H, 64, lambda hd: z[:, :, bass.ds(hd * 64 + Z_QA, 64)], lambda hd: z[:, :, bass.ds(hd * 64 + Z_KA, 64)])
        heads_done(pool, "b")
        pool.memset(ck2, 1.0).then_inc(S("forget_ones"), 1)
        pool.memset(cq2, 1.0).then_inc(S("forget_ones"), 1)
        pool.wait_ge(S("forget_in"), 32)
        stage(B_H, 64, lambda hd: z[:, :, bass.ds(hd * 64 + Z_QB, 64)], lambda hd: z[:, :, bass.ds(hd * 64 + Z_KB, 64)],
              rows_src=lambda hd: cq2[:, bass.ds(hd, 1), :].rearrange("p o n -> p (o n)"))
        heads_done(pool, "cross")
        load(gmask.rearrange("p l n -> p (l n)"), a["c_masks"], "gla_in")
        load(dmat.rearrange("p l n -> p (l n)"), a["c_decay"], "gla_in")
        load(cnb, a["c_norm_2"].broadcast_to([128, C_DV]), "gla_in")
        evacuated(pool, "cq")
        stage(4, 128, lambda hd: cqt[:, :, bass.ds(hd * 128, 128)], lambda hd: kvm[:, :, bass.ds(hd * 128, 128)])
        products(pool, "up")
        load(fgain, a["norm_final_2"].unsqueeze(0).broadcast_to([128, D]), "final_gain_in")

    ctx.close()


_INS = ["x", "p", "positions", "pre_norm", "post_norm", "pool_w_in", "pool_w_group", "pool_scale", "pool_w_out", "mla_w_in",
        "mla_q_norm", "mla_w_uq", "mla_kv_norm", "mla_w_ukv", "mla_w_out", "ple_norm", "ple_w_gate", "ple_w_proj", "mem_2",
        "rel_table_2", "mem_norm_2", "norm_final_2", "norm_mix_2", "w_in_2", "f_bias_2", "c_gate_w2_2", "c_gate_b_2",
        "c_norm_2", "w_out_2", "norm_cross_2", "w_cq_2", "w_ckv_2", "w_co_2", "norm_ffn_2", "w_up_2", "conv_w_2",
        "conv_b_2", "w_down_2"]


def kernel(**inputs):
    import concourse.bacc as bacc
    from concourse.bass_utils import run_bass_kernel_spmd

    nc = bacc.Bacc("TRN2", target_bir_lowering=False, num_devices=1)
    given = {name: np.ascontiguousarray(inputs[name]) for name in _INS}
    given.update({f"c_{name}": value for name, value in shape_constants().items()})
    arrays = {f"in_{name}": value for name, value in given.items()}
    aps = {name: nc.dram_tensor(f"in_{name}", value.shape, mybir.dt.from_np(value.dtype), kind="ExternalInput").ap()
           for name, value in given.items()}
    out = nc.dram_tensor("out_0", (1, T, D), F32, kind="ExternalOutput").ap()
    build(nc, aps, out)
    r = run_bass_kernel_spmd(nc, [arrays], core_ids=[0])
    return r.results[0]["out_0"]
```

```python
import math
from contextlib import ExitStack, contextmanager

import numpy as np

import concourse.bass as bass
from concourse import mybir

F32, F32R, I32 = mybir.dt.float32, mybir.dt.float32r, mybir.dt.int32
ACT = mybir.ActivationFunctionType
ALU = mybir.AluOpType
AXX = mybir.AxisListType.X

D = 2048
T = 256
KT = D // 128
NCH = D // 512
EPS = 1e-6
E_POOL = 4096
WINDOWS = (2, 4, 8, 16)
HEADS = 16
Q_RANK = KV_RANK = 512
NOPE, ROPE, VD = 128, 64, 128
A_W, B_W, C_KW, C_VW = 768, 512, 384, 768
A_H, B_H, C_H, C_DK, C_DV = 12, 8, 4, 96, 192
Z_W = 3 * A_W + 3 * B_W + B_H + 2 * C_KW + 2 * C_VW + 16
Z_QA, Z_KA, Z_VA = 0, A_W, 2 * A_W
Z_QB, Z_KB, Z_VB = 3 * A_W, 3 * A_W + B_W, 3 * A_W + 2 * B_W
Z_FL = 3 * A_W + 3 * B_W
Z_QC = Z_FL + B_H
Z_KC = Z_QC + C_KW
Z_VC = Z_KC + C_KW
Z_RC = Z_VC + C_VW
Z_GL = Z_RC + C_VW
D_FF = 5504
FKT = D_FF // 128
BUCKETS, MAX_DIST = 32, 2048
MASKED = -1e30
RAW, RING, LEAD = 8, 4, 3

LINEARS = [("pool", 160, 24), ("pool_out", 64, 4), ("proj0", 4, 4), ("gate0", 32, 4), ("mla_in", 49, 7), ("uq", 12, 6),
           ("ukv", 16, 8), ("mla_out", 32, 4), ("proj1", 4, 4), ("gate1", 32, 4), ("ckv", 16, 2), ("z", 97, 13),
           ("out2", 32, 4), ("cq", 8, 1), ("co", 8, 4), ("up", 176, 22), ("down", 96, 4)]
UNITS_END = {n: sum(u for _, u, _ in LINEARS[:k + 1]) for k, (n, _, _) in enumerate(LINEARS)}
CHUNKS_END = {n: sum(c for _, _, c in LINEARS[:k + 1]) for k, (n, _, _) in enumerate(LINEARS)}
TOTAL_UNITS = UNITS_END["down"]

GAIN_TILES = [
    [("pre0", 16), ("pre1", 16), ("ple0", 16), ("ple1", 16), ("pool_scale", 32), ("q_norm", 4), ("kv_norm", 4), ("mix", 16)],
    [("cross", 16), ("ffn", 16), ("mem", 16), ("conv_b", 43)],
    [("conv_w0", 43), ("conv_w1", 43)],
    [("conv_w2", 43)],
]
GAIN = {name: 128 * t + sum(n for _, n in tile[:k]) for t, tile in enumerate(GAIN_TILES) for k, (name, _) in enumerate(tile)}


def shape_constants():
    s, t = np.arange(128)[:, None], np.arange(256)[None, :]
    ident = np.eye(128, dtype=np.float32)
    band = np.zeros((128, 4, 384), np.float32)
    for j, w in enumerate(WINDOWS):
        full = np.zeros((256, 256), np.float32)
        for q in range(256):
            full[max(0, q - w + 1):q + 1, q] = np.float32(1.0) / np.float32(min(q + 1, w))
            full[q, q] -= 1.0
        band[:, j, :256] = full[:128]
        band[:, j, 256:] = full[128:, 128:]
    causal = np.where(s + 128 - t >= 0, 0.0, MASKED).astype(np.float32)
    m = np.arange(384)
    dist = 255 - m
    d = np.maximum(dist, 1).astype(np.float32)
    half = BUCKETS // 2
    large = half + (np.log(d / half) / math.log(MAX_DIST / half) * (BUCKETS - half)).astype(np.int32)
    bucket = np.where(dist < half, dist, np.minimum(large, BUCKETS - 1))
    rel = np.zeros((33, 384), np.float32)
    for c in range(384):
        if dist[c] >= 0:
            rel[bucket[c], c] = 1.0
            kept = int(dist[c] <= 128) + int(dist[c] % 4 == 0) + int(dist[c] % 16 == 0)
            rel[32, c] = np.log(np.float32(kept)) if kept else MASKED
        else:
            rel[32, c] = MASKED
    a, b = np.arange(128)[:, None], np.arange(128)[None, :]
    decay = [(a > b), (a <= b)]
    masks = [np.eye(128, dtype=bool)]
    for size in (128, 64, 32, 16, 8, 4, 2):
        mid = b // size * size + size // 2
        decay.append(((b >= mid) & (a >= mid) & (a <= b)) | ((b < mid) & (a > b) & (a < mid)))
        masks.append((a // size == b // size) & (b % size >= size // 2) & (a % size < size // 2))
    decay = np.stack(decay, 1).astype(np.float32).reshape(128, 9 * 128)
    masks = np.stack(masks, 1).astype(np.float32).reshape(128, 8 * 128)
    trio = np.concatenate([(a <= b), np.ones((128, 128), bool)], 1).astype(np.float32)
    freq = (10000.0 ** (-np.arange(0, ROPE, 2, dtype=np.float32) / np.float32(ROPE))).astype(np.float32)
    return {"ident": ident, "flip": np.ascontiguousarray(ident[::-1]), "band": band.reshape(128, 4 * 384), "causal": causal, "rel": rel, "decay": decay,
            "masks": masks, "trio": trio, "freq": freq[None, :]}


class Tally:

    def __init__(self):
        self.n, self.reg, self.per = {}, None, {}

    def at(self, name, k=0):
        v = self.n.get(name, 0) + k
        return self.reg * self.per[name] + v if self.reg is not None and self.per.get(name) else v

    def add(self, name, k=1):
        self.n[name] = self.n.get(name, 0) + k

    @contextmanager
    def loop(self, reg, turns, **per):
        begin = dict(self.n)
        self.reg, self.per = reg, per
        yield
        got = {k: v - begin.get(k, 0) for k, v in self.n.items() if v != begin.get(k, 0)}
        assert got == {k: v for k, v in per.items() if v}, f"loop counts {got}, said {per}"
        for k, v in got.items():
            self.n[k] = begin.get(k, 0) + turns * v
        self.reg, self.per = None, {}


def units_of(nkt, width=512):
    if nkt == FKT:
        return [(2 * u, 2 * u + 1) for u in range(19)] + [(k,) for k in range(38, 43)]
    per = 1024 // width if width < 256 else 2
    return [tuple(range(k, min(k + per, nkt))) for k in range(0, nkt, per)]


def build(nc, a, out):
    ctx = ExitStack()
    ctx.enter_context(nc.allow_non_contiguous_dma(reason="narrow weight columns, vectors"))
    sems = {}

    def S(name):
        if name not in sems:
            sems[name] = ctx.enter_context(nc.semaphore(name))
        return sems[name]

    base = (nc.sbuf_base + 63) // 64 * 64
    limit = nc.sbuf_usable_end

    def at(name, off, shape, dt=F32):
        size = int(np.prod(shape[1:])) * 4
        assert base + off + size <= limit, (name, base + off + size - limit)
        return nc.alloc_sbuf_tensor_at(name, shape, dt, offset=base + off)[:]

    pos = [0]

    def fixed(name, shape, dt=F32):
        off = pos[0]
        pos[0] += (int(np.prod(shape[1:])) * 4 + 31) // 32 * 32
        return at(name, off, shape, dt)

    raw = fixed("raw", [128, RAW, 1024])
    w_hi = fixed("w_hi", [128, RING, 1024], F32R)
    w_lo = fixed("w_lo", [128, RING, 1024], F32R)
    h = fixed("h", [128, 2, D])
    ident = fixed("identity", [128, 128])
    gain = fixed("gain_columns", [128, 512])
    causal = fixed("causal_mask", [128, 256])
    junk = fixed("junk", [128, 512])
    sums = fixed("square_sums", [128, 16, 2, 4])
    ms = fixed("mean_square", [128, 16, 2])
    rt = fixed("root", [128, 16, 2])
    rstd = fixed("rstd", [128, 16, 2])
    rc_cos = fixed("rope_cos", [128, 2, 32])
    rc_sin = fixed("rope_sin", [128, 2, 32])
    A0 = pos[0]

    def arena(name, off, shape, dt=F32):
        return at(name, A0 + off, shape, dt)

    xh = arena("x_hi", 0, [128, KT, T], F32R)
    xl = arena("x_lo", 16384, [128, KT, T], F32R)
    rows = arena("gain_rows", 32768, [128, 4, 128])
    y32 = arena("pool_y", 32768, [128, 32, T])
    band = arena("band", 65536, [128, 4, 384])
    ut = arena("u_tokens", 71680, [128, 2, 1024])
    sg = arena("silu_gate", 79872, [128, 2, 1024])
    plh = arena("pooled_hi", 88064, [128, 8, T], F32R)
    pll = arena("pooled_lo", 96256, [128, 8, T], F32R)
    mxs = arena("mixed_gated", 104448, [128, 2, 2, 512])
    yh = arena("pool_y_hi", 0, [128, 32, T], F32R)
    yl = arena("pool_y_lo", 32768, [128, 32, T], F32R)
    outt = arena("mixer_out", 65536, [128, 2, D])
    proj = arena("ple_proj", 81920, [128, 2, D])
    pgain = arena("post_gain", 98304, [128, D])
    sig = arena("ple_gate", 106496, [128, 2, 2, 512])
    ptok = arena("ple_tokens", 116736, [128, 2, 256])
    ph = arena("ple_hi", 118784, [128, 2, T], F32R)
    pl = arena("ple_lo", 120832, [128, 2, T], F32R)
    lat = arena("latents", 32768, [128, 2, 1024])
    kpe = arena("k_pe", 40960, [128, 2, 64])
    kpt = arena("k_pe_T", 41472, [64, T])
    gm = arena("mla_gate", 42496, [128, 2, D])
    qt = arena("mla_q", 58880, [128, 2, HEADS * 192])
    kv = arena("mla_kv", 83456, [128, 2, HEADS * 256])
    qlh = arena("q_lat_hi", 0, [128, 4, T], F32R)
    qll = arena("q_lat_lo", 4096, [128, 4, T], F32R)
    klh = arena("kv_lat_hi", 8192, [128, 4, T], F32R)
    kll = arena("kv_lat_lo", 12288, [128, 4, T], F32R)
    ra = arena("rope_a", 16384, [128, 2, HEADS, 32])
    rb = arena("rope_b", 20480, [128, 2, HEADS, 32])
    rc_ = arena("rope_c", 24576, [128, 2, HEADS, 32])
    rd = arena("rope_d", 28672, [128, 2, HEADS, 32])
    posi = arena("positions", 112640, [128, 2], I32)
    posf = arena("positions_f", 112672, [128, 2])
    freqs = arena("rope_freq", 112704, [128, 32])
    ang = arena("angle", 112896, [128, 2, 32])
    turns_ = arena("angle_turns", 113152, [128, 2, 32])
    red = arena("angle_reduced", 113408, [128, 2, 32])
    SQ = [arena(f"q_staged{j}", 7680 * j, [128, 2, 192]) for j in range(4)]
    SK = [arena(f"k_staged{j}", 7680 * j + 1536, [128, 2, 128]) for j in range(4)]
    QK = [arena(f"qk_T{j}", 7680 * j + 2560, [128, 2, T]) for j in range(4)]
    PTS = [arena(f"p_T{j}", 7680 * j + 2560, [128, 4, 128]) for j in range(4)]
    QP = [arena(f"q_pe_T{j}", 7680 * j + 4608, [64, T]) for j in range(4)]
    LG_ = [arena(f"logits{j}", 7680 * j + 5632, [128, 512]) for j in range(4)]
    assert 7680 * 4 <= 32768
    nmx = arena("neg_max", 30720, [128, 4, 2])
    psm = arena("prob_sum", 30752, [128, 4, 2])
    prc = arena("prob_scale", 30784, [128, 4, 2])
    KVM = 115456 - 512
    memt = arena("mem_tokens", 32768, [128, 2, D])
    kvm = arena("mem_kv", KVM, [128, 2, 1024])
    z = arena("z", 32768, [128, 2, Z_W])
    relb = arena("rel_bias", 82112, [128, A_H, T])
    mix = arena("mixed", 94400, [128, 2, D])
    lgd = arena("log_decay", 110784, [128, 2, 392])
    reltab = arena("rel_table", 0, [33, A_H])
    relone = arena("rel_onehot", 64, [33, 384])
    relrow = arena("rel_rows", 1600, [A_H, 384])
    lx = arena("gate_logits", 4096, [128, 2, 392])
    la = arena("gate_abs", 8192, [128, 2, 392])
    lm = arena("gate_min", 12288, [128, 2, 392])
    glt = arena("gl_T", 16384, [17, T])
    w2a = arena("gate_w2", 18432, [17, C_KW])
    fbias = arena("f_bias", 20480, [128, B_H])
    flip = arena("flip", 24576, [128, 128])
    trio = arena("running_sum", 20736, [128, 256])
    lf8 = arena("log_forget", 21760, [128, 2, B_H])
    crow, ncrow = junk[0:B_H, 0:256], junk[0:B_H, 256:512]
    ck2 = arena("forget_k", 32768, [2, B_H, T])
    cq2 = arena("forget_q", 32768 + 4 * Z_W, [2, B_H, T])
    gq = arena("gla_q_T", 0, [96, C_H, T])
    gk = arena("gla_k_T", 4096, [96, C_H, T])
    ge = arena("gla_decay", 8192, [96, C_H, T])
    gqs = arena("gla_q_decayed", 12288, [96, C_H, T])
    gks = arena("gla_k_decayed", 16384, [96, C_H, T])
    gat = arena("gla_attn", 20480, [128, 3, C_H, 128])
    gmask = arena("gla_masks", 26624, [128, 8, 128])
    dmat = arena("gla_sums", 32768, [128, 9, 128])
    oc = arena("gla_out", 37376, [128, 2, C_H, C_DV])
    cnb = arena("c_norm", 43520, [128, C_DV])
    cst = arena("gla_stats", 44288, [128, 3, 8])
    osq = arena("gla_squares", 32768 + 4 * Z_W, [128, 2, C_H, C_DV])
    cqt = arena("cross_q", 32768, [128, 2, 512])
    cot = arena("cross_out", 36864, [128, 2, 512])
    fy = arena("ffn_y", 32768, [128, FKT, T])
    fgs = arena("ffn_gate", 109568, [128, 2, 512])
    fvs = arena("ffn_val", 113664, [128, 2, 512])
    fcv = arena("ffn_conv", 117760, [128, 4, T])
    fyl = arena("ffn_y_lo", 32768, [128, FKT, T], F32R)
    fyh = arena("ffn_y_hi", 76800, [128, FKT, T], F32R)
    fgain = arena("final_gain", 0, [128, D])
    fout = arena("final_out", 8192, [128, 2, D])

    ps = ctx.enter_context(nc.psum_tensor("ps", [128, 8, 512], F32))[:]

    def MM(s, tt):
        return ps[:, 2 * s + tt, :]

    def TB(b):
        return ps[:, 4 + b, :]

    rel_scratch = nc.dram_tensor("rel_scratch", (A_H, 384), F32, kind="Internal").ap()

    def weights(ap):
        return ap.rearrange("(k p) n -> p k n", p=128)

    w_pool = weights(a["pool_w_in"][0])
    w_group = a["pool_w_group"][0].rearrange("g (k p) n -> p g k n", p=128)
    w_pout = weights(a["pool_w_out"][0])
    w_proj = [weights(a["ple_w_proj"][n]) for n in range(2)]
    w_gate = [weights(a["ple_w_gate"][n]) for n in range(2)]
    w_min = weights(a["mla_w_in"][0])
    w_uq, w_ukv, w_mout = weights(a["mla_w_uq"][0]), weights(a["mla_w_ukv"][0]), weights(a["mla_w_out"][0])
    w_ckv, w_cq, w_co = weights(a["w_ckv_2"][0]), weights(a["w_cq_2"][0]), weights(a["w_co_2"][0])
    w_in2, w_out2 = weights(a["w_in_2"][0]), weights(a["w_out_2"][0])
    w_up, w_down = weights(a["w_up_2"][0]), weights(a["w_down_2"][0])

    def tokens(ap):
        return ap.rearrange("(t p) n -> p t n", p=128)

    UNITS_POOL = 4 * 8 + 2 * 4
    WB = len(WINDOWS)

    def products(eng, linear, more=0):
        eng.wait_ge(S("w_used"), UNITS_END[linear] + RING + more)

    def evacuated(eng, linear):
        for back in (2, 1):
            c = CHUNKS_END[linear] - back
            eng.wait_ge(S(f"mm_free{c % 2}"), c // 2 + 2)

    def chunk_out(eng, linear, c):
        n = CHUNKS_END[linear] - 4 + c
        eng.wait_ge(S(f"mm_free{n % 2}"), n // 2 + 2)

    def banks_read(eng, t):
        for b in range(4):
            eng.wait_ge(S(f"t_free{b}"), (t.n["bank"] - b + 3) // 4 + 1)

    def gated(eng, n, chunks=4):
        eng.wait_ge(S("gated"), 2 + 4 * n + chunks)

    AT = {"mla": 0, "a": 16, "b": 28, "cross": 36, "end": 40}

    def heads_done(eng, before):
        eng.wait_ge(S("at_done"), AT[before] + 4)

    vectors = {"pre0": a["pre_norm"][0], "pre1": a["pre_norm"][1], "ple0": a["ple_norm"][0], "ple1": a["ple_norm"][1],
               "pool_scale": a["pool_scale"][0], "q_norm": a["mla_q_norm"][0], "kv_norm": a["mla_kv_norm"][0],
               "mix": a["norm_mix_2"][0], "cross": a["norm_cross_2"][0], "ffn": a["norm_ffn_2"][0],
               "mem": a["mem_norm_2"], "conv_b": a["conv_b_2"][0], "conv_w0": a["conv_w_2"][0, 0],
               "conv_w1": a["conv_w_2"][0, 1], "conv_w2": a["conv_w_2"][0, 2]}

    def load_gains(eng, tiles, sem):
        for n in tiles:
            at_row = 0
            for name, r in GAIN_TILES[n]:
                eng.dma_start(rows[at_row:at_row + r, n, :], vectors[name].rearrange("(r c) -> r c", c=128)).then_inc(S(sem), 16)
                at_row += r

    def over_heads(eng, t, heads, step, behind=0, **per_turn):
        for j in range(4):
            step(j, lambda b: j - b if j >= b else None)
        t.add("at", 4)
        if heads > 4:
            with eng.Fori(0, heads // 4 - 1) as i, t.loop(i, heads // 4 - 1, at=4, **per_turn):
                for j in range(4):
                    step(j, lambda b: i * 4 + (4 + j - b))
                t.add("at", 4)
        for j in range(behind):
            step(j, lambda b: heads + j - b if b > j else None)

    def slot(j, b):
        return (j - b) % 4

    block = ctx.enter_context(nc.Block())

    @block.sync
    def _(sp):
        t = Tally()

        def unit(src, kts, width):
            slot = t.n.get("unit", 0) % RAW
            sp.wait_ge(S("w_lo"), t.at("unit", 1))
            if t.reg is not None:
                sp.sem_inc(S("units_begun"), 1)
            n = len(kts) * width
            dst = raw[:, slot, 0:n].rearrange("p (k n) -> p k n", n=width)
            sp.dma_start(dst, src).then_inc(S(f"raw_full{slot}"), 16)
            t.add("unit")

        def chunk(w, nkt, col, width=512):
            for kts in units_of(nkt, width):
                unit(w[:, kts[0]:kts[-1] + 1, bass.ds(col, width)], kts, width)

        def load(dst, src, sem):
            sp.dma_start(dst, src).then_inc(S(sem), 16)

        for tt in range(2):
            load(h[:, tt, :], a["x"][0, tt * 128:(tt + 1) * 128, :], "h_in")
        load(band.rearrange("p w n -> p (w n)"), a["c_band"], "band_in")

        with sp.Fori(0, WB) as g, t.loop(g, WB, unit=UNITS_POOL):
            for half in range(2):
                for c in range(2):
                    chunk(w_pool, KT, g * 1024 + (half * E_POOL + c * 512))
            for c in range(2):
                for kts in units_of(8):
                    unit(w_group[:, bass.ds(g, 1), kts[0]:kts[-1] + 1, c * 512:(c + 1) * 512].rearrange("p g k n -> p (g k) n"),
                         kts, 512)
        with sp.Fori(0, 2) as g, t.loop(g, 2, unit=32):
            for c in range(2):
                chunk(w_pout, 32, g * 1024 + c * 512)

        def columns(w, col=0):
            with sp.Fori(0, 2) as g, t.loop(g, 2, unit=16):
                for c in range(2):
                    chunk(w, KT, g * 1024 + (c * 512 + col))

        def layer_end(n):
            for c in range(NCH):
                chunk(w_proj[n], 2, c * 512)
            columns(w_gate[n])

        layer_end(0)
        chunk(w_min, KT, 0)
        chunk(w_min, KT, 512)
        chunk(w_min, KT, 1024, 64)
        columns(w_min, 1088)
        for c in range(6):
            chunk(w_uq, 4, c * 512)
        with sp.Fori(0, 2) as g, t.loop(g, 2, unit=8):
            for c in range(4):
                chunk(w_ukv, 4, g * 2048 + c * 512)
        columns(w_mout)
        layer_end(1)
        for c in range(2):
            chunk(w_ckv, KT, c * 512)
        with sp.Fori(0, 6) as g, t.loop(g, 6, unit=16):
            for c in range(2):
                chunk(w_in2, KT, g * 1024 + c * 512)
        chunk(w_in2, KT, 12 * 512, 24)
        columns(w_out2)
        chunk(w_cq, KT, 0)
        for c in range(NCH):
            chunk(w_co, 4, c * 512)
        with sp.Fori(0, 10) as g, t.loop(g, 10, unit=16):
            chunk(w_up, KT, g * 512 + D_FF)
            chunk(w_up, KT, g * 512)
        chunk(w_up, KT, 5120 + D_FF, 384)
        chunk(w_up, KT, 5120, 384)
        for c in range(NCH):
            chunk(w_down, FKT, c * 512)
        assert t.n["unit"] == TOTAL_UNITS, t.n
        for c in range(2):
            sp.wait_ge(S("final"), c + 1)
            load(out[0, c * 128:(c + 1) * 128, :], fout[:, c, :], "out_done")
        sp.wait_ge(S("out_done"), 32)

    @block.tensor
    def _(pe):
        t = Tally()
        pe.sem_inc(S("w_used"), RING)

        def take_bank():
            b = t.n.get("bank", 0) % 4
            pe.wait_ge(S(f"t_free{b}"), t.at(f"bank{b}", 1))
            t.add("bank")
            t.add(f"bank{b}")
            return b

        def to_bank(src, f0, tiles=2):
            b = take_bank()
            for k in range(tiles):
                for tt in range(2):
                    f = f0 + k * 128
                    last = pe.transpose(TB(b)[:, k * 256 + tt * 128:k * 256 + tt * 128 + 128], src[:, tt, f:f + 128], ident)
            last.then_inc(S("t_full"), 1)

        def xpose(src, nkt, ready=None):
            for g in range(nkt // 2):
                if ready:
                    ready(g)
                to_bank(src, g * 256)

        def last_banks(n):
            total = t.n["bank"]
            def ready(k):
                if k % 2 == 0:
                    g = total - n + k // 2
                    pe.wait_ge(S(f"t_free{g % 4}"), g // 4 + 2)
            return ready

        def chunk(xhi, xlo, nkt, width=512, ready=None):
            s = t.n.get("chunk", 0) % 2
            pe.wait_ge(S(f"mm_free{s}"), t.at(f"set{s}", 1))
            units = units_of(nkt, width)
            for kts in units:
                slot = t.n.get("unit", 0) % RING
                pe.wait_ge(S("w_lo"), t.at("unit", RAW + 1))
                for n, k in enumerate(kts):
                    if ready:
                        ready(k)
                    wh = w_hi[:, slot, n * width:(n + 1) * width]
                    wl = w_lo[:, slot, n * width:(n + 1) * width]
                    for tt in range(2):
                        tok = slice(tt * 128, tt * 128 + 128)
                        dst = MM(s, tt)[:, 0:width]
                        pe.matmul(dst, xhi[:, k, tok], wh, start=k == 0, stop=False)
                        pe.matmul(dst, xhi[:, k, tok], wl, start=False, stop=False)
                        last = pe.matmul(dst, xlo[:, k, tok], wh, start=False, stop=k == nkt - 1)
                last.then_inc(S("w_used"), 1)
                t.add("unit")
            t.add("chunk")
            t.add(f"set{s}")
            return s

        def first_chunk(src, source_ready=None):
            first = t.n["bank"]

            def turn(g):
                if source_ready:
                    source_ready(g)
                to_bank(src, g * 256)

            def ready(k):
                if k % 2 == 0:
                    if k // 2 + 3 < KT // 2:
                        turn(k // 2 + 3)
                    n = first + k // 2
                    pe.wait_ge(S(f"t_free{n % 4}"), n // 4 + 2)

            for g in range(3):
                turn(g)
            chunk(xh, xl, KT, ready=ready)

        def linear(src, source_ready=None):
            first_chunk(src, source_ready)
            for _ in range(3):
                chunk(xh, xl, KT)

        def columns(xhi=xh, xlo=xl, nkt=KT, turns=2, ready=None):
            with pe.Fori(0, turns) as g, t.loop(g, turns, unit=2 * len(units_of(nkt)), chunk=2, set0=1, set1=1):
                for c in range(2):
                    chunk(xhi, xlo, nkt, ready=ready if c == 0 else None)

        pe.wait_ge(S("ident_in"), 16)

        def gain_columns(tiles):
            b = take_bank()
            for n in tiles:
                r = sum(x for _, x in GAIN_TILES[n])
                last = pe.transpose(TB(b)[:, n * 128:n * 128 + r], rows[0:r, n, :], ident[0:r, 0:r])
            last.then_inc(S("t_full"), 1)

        pe.wait_ge(S("rows_in0"), 16 * len(GAIN_TILES[0]))
        gain_columns((0,))

        pe.wait_ge(S("h_in"), 32)
        xpose(h, KT)
        ready = last_banks(8)
        pe.wait_ge(S("rows_in1"), 16 * sum(len(x) for x in GAIN_TILES[1:]))
        gain_columns((1, 2, 3))
        pe.wait_ge(S("band_in"), 16)
        with pe.Fori(0, WB) as g, t.loop(g, WB, unit=UNITS_POOL, chunk=6, set0=3, set1=3, bank=8, bank0=2, bank1=2,
                                         bank2=2, bank3=2):
            for c in range(3):
                chunk(xh, xl, KT, ready=ready if c == 0 else None)
                if c == 1:
                    before = [(f"mm_free{s}", t.at(f"set{s}", 1)) for s in range(2)]
            for name, v in before:
                pe.wait_ge(S(name), v)
            for k2 in range(4):
                b = take_bank()
                for k in range(2):
                    f = (2 * k2 + k) * 128
                    pe.matmul(TB(b)[:, k * 256:k * 256 + 256], ut[:, 0, f:f + 128],
                              band[:, bass.ds(g, 1), 0:256].rearrange("p o n -> p (o n)"), start=True, stop=False)
                    last = pe.matmul(TB(b)[:, k * 256 + 128:k * 256 + 256], ut[:, 1, f:f + 128],
                                     band[:, bass.ds(g, 1), 256:384].rearrange("p o n -> p (o n)"), start=False, stop=True)
                last.then_inc(S("t_full"), 1)
            chunk(xh, xl, KT)
            for b in range(4):
                pe.wait_ge(S(f"t_free{b}"), t.at(f"bank{b}", 1))
            before = []
            for c in range(2):
                s = chunk(plh, pll, 8)
                before.append((f"mm_free{s}", t.at(f"set{s}", 1)))
            for c in range(2):
                pe.wait_ge(S(before[c][0]), before[c][1])
                for k2 in range(2):
                    to_bank(mxs[:, c, :, :], k2 * 256)
        pe.wait_ge(S("ple_in0"), 16)
        xpose(ptok, 2)
        ready_ple = last_banks(1)
        columns(yh, yl, 32, ready=lambda k: pe.wait_ge(S("y_lo"), k // 8 + 1) if k % 8 == 0 else None)

        def layer_end(n, ready_ple):
            for c in range(NCH):
                chunk(ph, pl, 2, ready=ready_ple if c == 0 else None)
            linear(h, lambda g: pe.wait_ge(S(f"h_post{n}"), g // 2 + 1))

        layer_end(0, ready_ple)
        first_chunk(h, lambda g: gated(pe, 0, g // 2 + 1))
        chunk(xh, xl, KT)
        chunk(xh, xl, KT, 64)
        columns()
        pe.wait_ge(S("k_roped"), 1)
        b = take_bank()
        for tt in range(2):
            last = pe.transpose(TB(b)[0:64, tt * 128:tt * 128 + 128], kpe[:, tt, :], ident)
        last.then_inc(S("t_full"), 1)
        xpose(lat[:, :, 0:512], 4)
        ready_q = last_banks(2)
        xpose(lat[:, :, 512:1024], 4)
        ready_kv = last_banks(2)
        for c in range(6):
            chunk(qlh, qll, 4, ready=ready_q if c == 0 else None)
        with pe.Fori(0, 2) as g, t.loop(g, 2, unit=8, chunk=4, set0=2, set1=2):
            for c in range(4):
                chunk(klh, kll, 4, ready=ready_kv if c == 0 else None)

        def attention(heads, d, dv, v_src, keys0=128, pe_part=False, forget=False):
            def step(j, head):
                if head(3) is not None:
                    s = slot(j, 3)
                    pe.wait_ge(S("at_P"), t.at("at", j - 2))
                    for n in range((keys0 + 256) // 128):
                        last = pe.transpose(TB(s)[:, n * 128:n * 128 + 128], LG_[s][:, n * 128:n * 128 + 128], ident)
                    last.then_inc(S("at_PT"), 1)
                if head(0) is not None:
                    s = slot(j, 0)
                    B, A = TB(s), ps[:, s, :]
                    pe.wait_ge(S("at_stage"), t.at("at", 1 + j))
                    pe.wait_ge(S("at_PTE"), t.at("at", 1 + j))
                    pe.wait_ge(S("at_done"), t.at("at", 1 + j))
                    pe.sem_inc(S("heads_begun"), 1)
                    for tt in range(2):
                        pe.transpose(B[0:d, tt * 128:tt * 128 + 128], SQ[s][:, tt, 0:d], ident)
                        if pe_part:
                            pe.transpose(A[0:64, tt * 128:tt * 128 + 128], SQ[s][:, tt, 128:192], ident)
                        last = pe.transpose(B[0:d, 256 + tt * 128:384 + tt * 128], SK[s][:, tt, 0:d], ident)
                    last.then_inc(S("at_T"), 1)
                if head(3) is not None:
                    s = slot(j, 3)
                    pe.wait_ge(S("at_PTE"), t.at("at", 4 + j - 2))
                    n = 0
                    for q, nb in enumerate((keys0 // 128, 2)):
                        for kb in range(nb):
                            last = pe.matmul(ps[:, s, q * dv:q * dv + dv], PTS[s][:, n, :], v_src(kb, head(3)),
                                             start=kb == 0, stop=kb == nb - 1)
                            n += 1
                    last.then_inc(S("at_O"), 1)
                if head(1) is not None:
                    s = slot(j, 1)
                    pe.wait_ge(S("at_TE"), t.at("at", j))
                    for q, (c0, nk) in enumerate(((0, keys0), (keys0, 256))):
                        dst, tok = ps[:, s, c0:c0 + nk], slice(q * 128, q * 128 + 128)
                        if forget:
                            pe.matmul(dst, QP[s][0:2, tok], ck2[:, bass.ds(head(1), 1), 0:nk].rearrange("p o n -> p (o n)"),
                                      start=True, stop=False)
                        if pe_part:
                            pe.matmul(dst, QP[s][0:64, tok], kpt[:, 0:nk], start=True, stop=False)
                        last = pe.matmul(dst, QK[s][0:d, 0, tok], QK[s][0:d, 1, 0:nk], start=not (forget or pe_part), stop=True)
                    last.then_inc(S("at_S"), 1)

            banks_read(pe, t)
            over_heads(pe, t, heads, step, behind=3)
            pe.wait_ge(S("at_done"), t.at("at", 4))

        pe.wait_ge(S("mla_ready"), 1)
        attention(HEADS, 128, VD, lambda kb, hd: kv[:, kb, bass.ds(hd * 256 + 128, 128)], pe_part=True)
        pe.wait_ge(S("ple_in1"), 16)
        xpose(ptok, 2)
        ready_ple = last_banks(1)
        linear(gm)
        layer_end(1, ready_ple)
        pe.wait_ge(S("mem_in"), 16)
        first_chunk(memt)
        chunk(xh, xl, KT)
        first_chunk(h, lambda g: gated(pe, 1, g // 2 + 1))
        chunk(xh, xl, KT)
        columns(turns=5)
        chunk(xh, xl, KT, 24)
        evacuated(pe, "z")
        pe.wait_ge(S("hyb_in"), 16 * 7)
        b = take_bank()
        pe.matmul(TB(b)[0:A_H, 0:384], reltab, relone, start=True, stop=True).then_inc(S("t_full"), 1)
        b = take_bank()
        for tt in range(2):
            last = pe.transpose(TB(b)[0:16, tt * 128:tt * 128 + 128], z[:, tt, Z_GL:Z_GL + 16], ident)
        last.then_inc(S("t_full"), 1)
        banks_read(pe, t)
        for tt in range(2):
            b = take_bank()
            pe.matmul(TB(b)[:, 0:C_KW], glt[:, tt * 128:tt * 128 + 128], w2a, start=True, stop=True).then_inc(S("t_full"), 1)
        pe.wait_ge(S("log_forget"), 1)
        b = take_bank()
        pe.matmul(TB(b)[0:B_H, 0:256], lf8[:, 0, :], trio, start=True, stop=False)
        pe.matmul(TB(b)[0:B_H, 128:256], lf8[:, 1, :], trio[:, 0:128], start=False, stop=True).then_inc(S("t_full"), 1)
        pe.wait_ge(S("rel_in"), 16 * A_H)
        for n in range(A_H // 2):
            b = take_bank()
            pe.matmul(TB(b), flip, relb[:, 2 * n:2 * n + 2, :].rearrange("p h n -> p (h n)"), start=True, stop=True).then_inc(S("t_full"), 1)
        attention(A_H, 64, 64, lambda kb, hd: z[:, kb, bass.ds(hd * 64 + Z_VA, 64)])
        pe.wait_ge(S("forget_in"), 32)
        attention(B_H, 64, 64, lambda kb, hd: z[:, kb, bass.ds(hd * 64 + Z_VB, 64)], forget=True)
        for hd in range(C_H):
            b = take_bank()
            for m, c0 in enumerate((Z_QC, Z_KC)):
                for tt in range(2):
                    last = pe.transpose(TB(b)[0:C_DK, m * 256 + tt * 128:m * 256 + tt * 128 + 128],
                                        z[:, tt, c0 + hd * C_DK:c0 + hd * C_DK + C_DK], ident)
            last.then_inc(S("t_full"), 1)

        def decay_sums(lv):
            s = lv % 2
            if lv >= 2:
                pe.wait_ge(S("gla_e"), lv - 1)
            for hd in range(C_H):
                for tt in range(2):
                    o = ps[0:C_DK, 2 * s + hd // 2, (hd % 2) * 256 + tt * 128:(hd % 2) * 256 + tt * 128 + 128]
                    last = pe.matmul(o, lgd[:, tt, hd * C_DK:hd * C_DK + C_DK], dmat[:, tt if lv == 0 else lv + 1, :], start=True, stop=True)
            last.then_inc(S("gla_d"), 1)

        pe.wait_ge(S("gla_in"), 48)
        decay_sums(0)
        banks_read(pe, t)
        for tt in range(2):
            b = take_bank()
            tok = slice(tt * 128, tt * 128 + 128)
            for hd in range(C_H):
                last = pe.matmul(TB(b)[:, hd * 128:hd * 128 + 128], gk[:, hd, tok], gq[:, hd, tok], start=True, stop=True)
            last.then_inc(S("t_full"), 1)
        for lv in range(8):
            if lv < 7:
                decay_sums(lv + 1)
            pe.wait_ge(S("gla_s"), lv + 1)
            for tt in range(2 if lv else 1):
                b = take_bank()
                ktok = slice(tt * 128, tt * 128 + 128)
                qtok = ktok if lv else slice(128, 256)
                for hd in range(C_H):
                    last = pe.matmul(TB(b)[:, hd * 128:hd * 128 + 128], gks[:, hd, ktok], gqs[:, hd, qtok], start=True, stop=True)
                last.then_inc(S("t_full"), 1)
        banks_read(pe, t)
        pe.wait_ge(S("gla_e"), 8)
        for hd in range(C_H):
            v0, v1 = (z[:, tt, Z_VC + hd * C_DV:Z_VC + (hd + 1) * C_DV] for tt in range(2))
            pe.matmul(ps[:, hd, 0:C_DV], gat[:, 0, hd, :], v0, start=True, stop=True)
            pe.matmul(ps[:, hd, C_DV:2 * C_DV], gat[:, 2, hd, :], v0, start=True, stop=False)
            last = pe.matmul(ps[:, hd, C_DV:2 * C_DV], gat[:, 1, hd, :], v1, start=False, stop=True)
        last.then_inc(S("gla_o"), 1)
        pe.wait_ge(S("mix_ready"), 1)
        linear(mix)
        first_chunk(h, lambda g: chunk_out(pe, "out2", g // 2))
        evacuated(pe, "cq")
        attention(4, 128, 128, lambda kb, hd: kvm[:, kb, bass.ds(hd * 128 + 512, 128)], keys0=256)
        xpose(cot, 4)
        ready = last_banks(2)
        for c in range(NCH):
            chunk(xh, xl, 4, ready=ready if c == 0 else None)
        first_chunk(h, lambda g: chunk_out(pe, "co", g // 2))

        def to_features(src, width, s, v):
            pe.wait_ge(S(f"mm_free{s}"), v)
            for k2 in range(2):
                to_bank(src, k2 * 256, min(2, width // 128 - 2 * k2))

        def gate_out(width):
            s = t.n["chunk"] % 2
            to_features(fgs, width, s, t.at(f"set{s}", 1))

        def up_turn(width, next_width):
            chunk(xh, xl, KT, width)
            gate_out(width)
            chunk(xh, xl, KT, next_width)
            s = t.n["chunk"] % 2
            to_features(fvs, width, s, t.at(f"set{s}", 1))

        with pe.Fori(0, 9) as g, t.loop(g, 9, unit=16, chunk=2, set0=1, set1=1, bank=4, bank0=1, bank1=1, bank2=1, bank3=1):
            up_turn(512, 512)
        up_turn(512, 384)
        chunk(xh, xl, KT, 384)
        gate_out(384)
        s = (t.n["chunk"] - 1) % 2
        to_features(fvs, 384, s, t.at(f"set{s}", 1))
        for c in range(NCH):
            chunk(fyh, fyl, FKT, ready=lambda k: pe.wait_ge(S("fy_lo"), k // 8 + 1) if k % 8 == 0 and c == 0 else None)
        assert t.n["unit"] == TOTAL_UNITS and t.n["chunk"] == CHUNKS_END["down"], t.n

    @block.scalar
    def _(act):
        t = Tally()

        def hi(k):
            for _ in range(k):
                u = t.n.get("unit", 0)
                if t.reg is not None or u < TOTAL_UNITS:
                    slot = u % RAW
                    full = 16 * (u // RAW + 1)
                    act.wait_ge(S(f"raw_full{slot}"), t.reg * (t.per["unit"] * 16 // RAW) + full if t.reg is not None else full)
                    act.wait_ge(S("w_used"), t.at("unit", 1))
                    act.activation(w_hi[:, u % RING, :], raw[:, slot, :], ACT.Copy).then_inc(S("w_hi"), 1)
                t.add("unit")

        def chunk(units):
            hi(units)
            s = t.n.get("chunk", 0) % 2
            t.add("chunk")
            act.wait_ge(S("w_used"), t.at("unit", RING - LEAD))
            return s

        def skip(units):
            hi(units)
            t.add("chunk")

        def xpose_hi(dst, nkt, g0=None):
            for g in range(nkt // 2):
                act.wait_ge(S("t_full"), t.at("bank", 1))
                bank = TB(t.n["bank"] % 4)
                if g0 is None:
                    last = act.activation(dst[:, 2 * g:2 * g + 2, :].rearrange("p k n -> p (k n)"), bank, ACT.Copy)
                else:
                    for k in range(2):
                        last = act.activation(dst[:, 2 * g + k, :], bank[:, k * 256:k * 256 + 256], ACT.Copy,
                                              scale=gain[:, g0 + 2 * g + k:g0 + 2 * g + k + 1])
                last.then_inc(S("x_hi"), 1)
                t.add("bank")

        def square(src, dst, scale=1.0):
            if t.n.get("junk"):
                act.wait_ge(S("junk_written"), t.at("junk"))
            act.activation(junk, src, ACT.Square, scale=scale, accum_out=dst).then_inc(S("junk_written"), 1)
            t.add("junk")

        def squares(src, slot):
            for tt in range(2):
                for c in range(NCH):
                    square(src[:, tt, c * 512:(c + 1) * 512], sums[:, slot, tt, c:c + 1])
            act.wait_ge(S("junk_written"), t.at("junk"))
            act.sem_inc(S(f"sums{slot}"), 1)

        def first_chunk(g0=None, src=None, slot=None):
            for g in range(KT // 2):
                xpose_hi(xh[:, 2 * g:2 * g + 2, :], 2, None if g0 is None else g0 + 2 * g)
                hi(1)
                if src is not None:
                    c, tt = g // 2, g % 2
                    square(src[:, tt, c * 512:(c + 1) * 512], sums[:, slot, tt, c:c + 1])
            if src is not None:
                act.wait_ge(S("junk_written"), t.at("junk"))
                act.sem_inc(S(f"sums{slot}"), 1)
                root(slot)
            s = t.n["chunk"] % 2
            t.add("chunk")
            act.wait_ge(S("w_used"), t.at("unit", RING - LEAD))
            if src is not None:
                act.wait_ge(S(f"rstd{slot}"), 1)
            return s

        def root(slot):
            act.wait_ge(S(f"mean_square{slot}"), 1)
            act.activation(rt[:, slot, :], ms[:, slot, :], ACT.Sqrt).then_inc(S(f"root{slot}"), 1)

        def read_out(s, dst, func=ACT.Copy, scale=None, width=512):
            for tt in range(2):
                last = act.activation(dst(tt), MM(s, tt)[:, 0:width], func, scale=1.0 if scale is None else rstd[:, scale, tt:tt + 1])
            last.then_inc(S(f"mm_free{s}"), 1)

        act.dma_start(ident, a["c_ident"]).then_inc(S("ident_in"), 16)
        load_gains(act, (0,), "rows_in0")
        hi(LEAD)
        act.wait_ge(S("h_in"), 32)
        squares(h, 0)
        root(0)

        def gain_columns(tiles):
            b = t.n.get("bank", 0) % 4
            act.wait_ge(S("t_full"), t.at("bank", 1))
            for n in tiles:
                r = sum(x for _, x in GAIN_TILES[n])
                last = act.activation(gain[:, n * 128:n * 128 + r], TB(b)[:, n * 128:n * 128 + r], ACT.Copy)
            last.then_inc(S(f"t_free{b}"), 1)
            t.add("bank")

        gain_columns((0,))
        act.wait_ge(S("t_free0"), 2)
        xpose_hi(xh, KT, GAIN["pre0"])
        gain_columns((1, 2, 3))
        act.wait_ge(S("rope_reduced"), 2)
        act.activation(rc_sin, ang, ACT.Sin)
        act.activation(rc_cos, red, ACT.Sin).then_inc(S("rope_tables"), 1)
        act.wait_ge(S("rstd0"), 1)
        with act.Fori(0, WB) as g, t.loop(g, WB, unit=UNITS_POOL, chunk=6, bank=8):
            for c in range(2):
                read_out(chunk(8), lambda tt: ut[:, tt, c * 512:c * 512 + 512], scale=0)
            for c in range(2):
                read_out(chunk(8), lambda tt: sg[:, tt, c * 512:c * 512 + 512], ACT.Silu, scale=0)
                if c == 0:
                    xpose_hi(plh, 8)
            for c in range(2):
                skip(4)
            for c in range(2):
                for k2 in range(2):
                    b = t.n["bank"] % 4
                    act.wait_ge(S("t_full"), t.at("bank", 1))
                    for k in range(2):
                        f = c * 4 + 2 * k2 + k
                        last = act.activation(y32[:, bass.ds(g * 8 + f, 1), :].rearrange("p o n -> p (o n)"),
                                              TB(b)[:, k * 256:k * 256 + 256], ACT.Copy,
                                              scale=gain[:, bass.ds(g * 8 + (GAIN["pool_scale"] + f), 1)])
                    last.then_inc(S(f"t_free{b}"), 1)
                    t.add("bank")
        banks_read(act, t)
        products(act, "pool")
        for n in range(4):
            act.activation(yh[:, 8 * n:8 * n + 8, :], y32[:, 8 * n:8 * n + 8, :], ACT.Copy).then_inc(S("y_hi"), 1)

        def mixer_chunk(s, slot, c):
            for tt in range(2):
                square(MM(s, tt), sums[:, slot, tt, c:c + 1])
            read_out(s, lambda tt: outt[:, tt, c * 512:(c + 1) * 512])

        def layer_end(n, slot):
            root(slot)
            for c in range(NCH):
                read_out(chunk(1), lambda tt: proj[:, tt, c * 512:(c + 1) * 512])
            for c in range(NCH):
                s = first_chunk(GAIN[f"ple{n}"], h, slot + 1) if c == 0 else chunk(8)
                act.wait_ge(S("gated"), 4 * n + c + 1)
                read_out(s, lambda tt: sig[:, c % 2, tt, :], ACT.Sigmoid, scale=slot + 1)

        xpose_hi(ph, 2)
        for c in range(NCH):
            mixer_chunk(chunk(16), 1, c)
        layer_end(0, 1)
        for c in range(2):
            s = first_chunk(GAIN["pre1"], h, 3) if c == 0 else chunk(8)
            for tt in range(2):
                square(MM(s, tt), sums[:, 4 + c, tt, 0:1], rstd[:, 3, tt:tt + 1])
            read_out(s, lambda tt: lat[:, tt, c * 512:(c + 1) * 512], scale=3)
        read_out(chunk(1), lambda tt: kpe[:, tt, :], scale=3, width=64)
        with act.Fori(0, 2) as g, t.loop(g, 2, unit=16, chunk=2):
            for c in range(2):
                read_out(chunk(8), lambda tt: gm[:, tt, bass.ds(g * 1024 + c * 512, 512)], ACT.Silu, scale=3)
        root(4)
        root(5)
        act.wait_ge(S("t_full"), t.at("bank", 1))
        b = t.n["bank"] % 4
        act.activation(kpt, TB(b)[0:64, 0:256], ACT.Copy).then_inc(S(f"t_free{b}"), 1)
        t.add("bank")
        xpose_hi(qlh, 4, GAIN["q_norm"])
        xpose_hi(klh, 4, GAIN["kv_norm"])
        act.wait_ge(S("rstd4"), 1)
        act.wait_ge(S("rstd5"), 1)
        for c in range(6):
            read_out(chunk(2), lambda tt: qt[:, tt, c * 512:(c + 1) * 512], scale=4)
        with act.Fori(0, 2) as g, t.loop(g, 2, unit=8, chunk=4):
            for c in range(4):
                read_out(chunk(2), lambda tt: kv[:, tt, bass.ds(g * 2048 + c * 512, 512)], scale=5)

        def attention(heads, d, keys0=128, pe_part=False):
            def step(j, head):
                if head(3) is not None:
                    s = slot(j, 3)
                    act.wait_ge(S("at_PT"), t.at("at", j - 2))
                    act.activation(PTS[s].rearrange("p k n -> p (k n)")[:, 0:keys0 + 256], TB(s)[:, 0:keys0 + 256], ACT.Copy)\
                       .then_inc(S("at_PTE"), 1)
                if head(0) is not None:
                    s = slot(j, 0)
                    act.wait_ge(S("at_T"), t.at("at", 1 + j))
                    if pe_part:
                        act.activation(QP[s], ps[0:64, s, 0:256], ACT.Copy)
                    act.activation(QK[s][0:d], TB(s)[0:d, :].rearrange("p (m n) -> p m n", m=2), ACT.Copy).then_inc(S("at_TE"), 1)
                if head(2) is not None:
                    s = slot(j, 2)
                    act.wait_ge(S("at_L"), t.at("at", j - 1))
                    for q, (c0, n) in enumerate(((0, keys0), (keys0, 256))):
                        last = act.activation(LG_[s][:, c0:c0 + n], LG_[s][:, c0:c0 + n], ACT.Exp, bias=nmx[:, s, q:q + 1],
                                              accum_out=psm[:, s, q:q + 1])
                    last.then_inc(S("at_P"), 1)

            over_heads(act, t, heads, step, behind=3)

        attention(HEADS, 128, pe_part=True)
        heads_done(act, "a")
        xpose_hi(ph, 2)
        for c in range(NCH):
            mixer_chunk(chunk(8) if c else first_chunk(), 6, c)
        layer_end(1, 6)
        for c in range(2):
            read_out(chunk(8) if c else first_chunk(GAIN["mem"], memt, 8), lambda tt: kvm[:, tt, c * 512:(c + 1) * 512], scale=8)
        for c in range(2):
            read_out(chunk(8) if c else first_chunk(GAIN["mix"], h, 9), lambda tt: z[:, tt, c * 512:(c + 1) * 512], scale=9)
        with act.Fori(0, 5) as g, t.loop(g, 5, unit=16, chunk=2):
            for c in range(2):
                read_out(chunk(8), lambda tt: z[:, tt, bass.ds(g * 1024 + (c * 512 + 1024), 512)], scale=9)
        read_out(chunk(1), lambda tt: z[:, tt, 6144:Z_W], scale=9, width=24)
        act.wait_ge(S("t_full"), t.at("bank", 1))
        b = t.n["bank"] % 4
        act.activation(relrow, TB(b)[0:A_H, 0:384], ACT.Copy).then_inc(S(f"t_free{b}"), 1)
        t.add("bank")
        act.wait_ge(S("ones_set"), 2)
        act.wait_ge(S("t_full"), t.at("bank", 1))
        b = t.n["bank"] % 4
        act.activation(glt[0:16, :], TB(b)[0:16, 0:256], ACT.Copy).then_inc(S(f"t_free{b}"), 1)
        t.add("bank")
        banks_read(act, t)
        act.dma_start(rel_scratch, relrow).then_inc(S("rel_out"), 16)
        act.wait_ge(S("rel_out"), 16)
        for hd in range(A_H):
            act.dma_start(relb[:, hd, :], bass.AP(tensor=rel_scratch.tensor, offset=hd * 384, ap=[[1, 128], [1, 256]]))\
               .then_inc(S("rel_in"), 16)
        t.add("bank", 2)
        act.wait_ge(S("gate_abs"), 1)
        act.activation(la, la, ACT.Exp, scale=-1.0).then_inc(S("gate_exp"), 1)
        act.wait_ge(S("gate_exp"), 1)
        act.activation(la, la, ACT.Ln, bias=1.0).then_inc(S("gate_exp"), 1)
        act.wait_ge(S("t_full"), t.at("bank", 1))
        b = t.n["bank"] % 4
        act.activation(crow, TB(b)[0:B_H, 0:256], ACT.Copy)
        act.activation(ncrow, TB(b)[0:B_H, 0:256], ACT.Copy, scale=-1.0).then_inc(S(f"t_free{b}"), 1)
        t.add("bank")
        for n in range(A_H // 2):
            act.wait_ge(S("t_full"), t.at("bank", 1))
            b = t.n["bank"] % 4
            act.activation(relb[:, 2 * n:2 * n + 2, :].rearrange("p h n -> p (h n)"), TB(b), ACT.Copy).then_inc(S(f"t_free{b}"), 1)
            t.add("bank")
        banks_read(act, t)
        act.sem_inc(S("sums_read"), 1)
        attention(A_H, 64)
        heads_done(act, "b")
        act.wait_ge(S("forget_ones"), 2)
        act.dma_start(ck2[0:1, :, :].rearrange("o h t -> o (h t)"), ncrow).then_inc(S("forget_in"), 16)
        act.dma_start(cq2[1:2, :, :].rearrange("o h t -> o (h t)"), crow).then_inc(S("forget_in"), 16)
        attention(B_H, 64)
        heads_done(act, "cross")
        for hd in range(C_H):
            act.wait_ge(S("t_full"), t.at("bank", 1))
            b = t.n["bank"] % 4
            act.activation(gq[:, hd, :], TB(b)[0:C_DK, 0:256], ACT.Copy, scale=C_DK ** -0.5)
            act.activation(gk[:, hd, :], TB(b)[0:C_DK, 256:512], ACT.Copy).then_inc(S(f"t_free{b}"), 1)
            t.add("bank")
        for lv in range(8):
            act.wait_ge(S("gla_d"), lv + 1)
            if lv:
                act.wait_ge(S("gla_s"), lv)
            s = lv % 2
            act.activation(ge, ps[0:C_DK, 2 * s:2 * s + 2, :].rearrange("p b (h n) -> p (b h) n", h=2), ACT.Exp, scale=1.0 / 16.0)\
               .then_inc(S("gla_e"), 1)
        for tt in range(2):
            last = act.activation(mix[:, tt, A_W + B_W:D], z[:, tt, Z_RC:Z_RC + C_VW], ACT.Silu)
        last.then_inc(S("rc_silu"), 1)
        act.wait_ge(S("gla_ms"), 1)
        act.activation(cst[:, 1, :], cst[:, 0, :], ACT.Sqrt).then_inc(S("gla_root"), 1)
        t.add("bank", 2 + 1 + 2 * 7)
        act.wait_ge(S("gla_o"), 1)
        first_chunk()
        for c in range(1, NCH):
            skip(8)
        products(act, "out2")
        read_out(first_chunk(GAIN["cross"], h, 10), lambda tt: cqt[:, tt, :], scale=10)
        attention(4, 128, keys0=256)
        heads_done(act, "end")
        xpose_hi(xh, 4)
        for c in range(NCH):
            skip(2)
        products(act, "co")
        read_out(first_chunk(GAIN["ffn"], h, 11), lambda tt: fgs[:, tt, :], scale=11)

        def silu_conv(width):
            act.wait_ge(S("conv_done"), t.at("conv", 1))
            act.activation(fcv[:, 0:width // 128, :], fcv[:, 0:width // 128, :], ACT.Silu).then_inc(S("conv_silu"), 1)
            t.add("conv")
            t.add("bank", 4)

        def up_turn(width, next_width):
            skip(8)
            hi(4)
            silu_conv(width)
            read_out(chunk(4), lambda tt: fgs[:, tt, 0:next_width], scale=11, width=next_width)

        with act.Fori(0, 9) as g, t.loop(g, 9, unit=16, chunk=2, conv=1, bank=4):
            up_turn(512, 512)
        up_turn(512, 384)
        for n in range(4):
            act.wait_ge(S("y_pairs"), 2 * n + 2)
            act.activation(fyh[:, 8 * n:8 * n + 8, :], fy[:, 8 * n:8 * n + 8, :], ACT.Copy).then_inc(S("fy_hi"), 1)
            hi(2)
        t.add("chunk")
        silu_conv(384)
        act.wait_ge(S("y_pairs"), 11)
        for n in range(4, 6):
            k = slice(8 * n, min(8 * n + 8, FKT))
            act.activation(fyh[:, k, :], fy[:, k, :], ACT.Copy).then_inc(S("fy_hi"), 1)
        for c in range(NCH):
            skip(len(units_of(FKT)))
        evacuated(act, "down")
        squares(h, 12)
        root(12)

    @block.vector
    def _(dve):
        t = Tally()
        dve.sem_inc(S("w_lo"), RAW)
        for name in ("mm_free0", "mm_free1", "t_free0", "t_free1", "t_free2", "t_free3"):
            dve.sem_inc(S(name), 1)
        dve.sem_inc(S("gated"), 2)
        dve.sem_inc(S("at_done"), 4)
        dve.sem_inc(S("at_PTE"), 4)

        def link(ins):
            ins.then_inc(S("dve_chain"), 1)
            t.add("chain")
            dve.wait_ge(S("dve_chain"), t.at("chain"))

        def lo(k):
            for _ in range(k):
                u = t.n.get("unit", 0)
                if t.reg is not None or u < TOTAL_UNITS:
                    dve.wait_ge(S("w_hi"), t.at("unit", 1))
                    dve.tensor_tensor(w_lo[:, u % RING, :], raw[:, u % RAW, :], w_hi[:, u % RING, :].bitcast(F32), ALU.subtract)\
                       .then_inc(S("w_lo"), 1)
                t.add("unit")

        def chunk(units):
            lo(units)
            s = t.n.get("chunk", 0) % 2
            t.add("chunk")
            dve.wait_ge(S("w_used"), t.at("unit", RING - LEAD))
            return s

        def skip(units):
            lo(units)
            t.add("chunk")

        def xpose_lo(dst, hi_part, nkt, g0=None):
            for g in range(nkt // 2):
                dve.wait_ge(S("x_hi"), t.at("xh", 1))
                b = t.n["bank"] % 4
                if g0 is None:
                    k = slice(2 * g, 2 * g + 2)
                    last = dve.tensor_tensor(dst[:, k, :].rearrange("p k n -> p (k n)"), TB(b),
                                             hi_part[:, k, :].rearrange("p k n -> p (k n)").bitcast(F32), ALU.subtract)
                else:
                    for k in range(2):
                        c = g0 + 2 * g + k
                        last = dve.scalar_tensor_tensor(dst[:, 2 * g + k, :], TB(b)[:, k * 256:k * 256 + 256], gain[:, c:c + 1],
                                                        hi_part[:, 2 * g + k, :].bitcast(F32), ALU.mult, ALU.subtract)
                last.then_inc(S(f"t_free{b}"), 1)
                t.add("bank")
                t.add("xh")

        def first_chunk(g0=None, slot=None, between=None):
            for g in range(KT // 2):
                k = slice(2 * g, 2 * g + 2)
                xpose_lo(xl[:, k, :], xh[:, k, :], 2, None if g0 is None else g0 + 2 * g)
                lo(1)
                if between:
                    between(g)
            if slot is not None:
                norm(slot)
            s = t.n["chunk"] % 2
            t.add("chunk")
            return s

        def mean(slot, width, cols=NCH):
            link(dve.reduce_sum(ms[:, slot, :], sums[:, slot, :, 0:cols], AXX))
            dve.tensor_scalar(ms[:, slot, :], ms[:, slot, :], 1.0 / width, EPS, ALU.mult, ALU.add).then_inc(S(f"mean_square{slot}"), 1)

        def inverse(slot):
            dve.wait_ge(S(f"root{slot}"), 1)
            dve.reciprocal(rstd[:, slot, :], rt[:, slot, :]).then_inc(S(f"rstd{slot}"), 1)
            dve.wait_ge(S(f"rstd{slot}"), 1)

        def norm(slot, width=D):
            dve.wait_ge(S(f"sums{slot}"), 1)
            mean(slot, width)
            inverse(slot)

        lo(LEAD)
        norm(0)
        dve.wait_ge(S("pos_in"), 32)
        link(dve.tensor_copy(posf, posi))
        for tt in range(2):
            last = dve.tensor_scalar(ang[:, tt, :], freqs, posf[:, tt:tt + 1], None, ALU.mult)
        link(last)
        ROUND = 1.5 * 2.0 ** 23
        PI = float(np.float32(3.1415925))
        link(dve.tensor_scalar(turns_, ang, 1.0 / (2 * math.pi), None, ALU.mult))
        link(dve.tensor_scalar(turns_, turns_, ROUND, ROUND, ALU.add, ALU.subtract))
        link(dve.scalar_tensor_tensor(ang, turns_, -6.28125, ang, ALU.mult, ALU.add))
        link(dve.scalar_tensor_tensor(ang, turns_, -(2 * math.pi - 6.28125), ang, ALU.mult, ALU.add))
        link(dve.tensor_scalar(red, ang, math.pi / 2, math.pi, ALU.add, ALU.is_gt))
        link(dve.tensor_scalar(red, red, -2 * math.pi, math.pi / 2, ALU.mult, ALU.add))
        link(dve.tensor_tensor(red, red, ang, ALU.add))
        dve.tensor_scalar(red, red, PI, -PI, ALU.min, ALU.max).then_inc(S("rope_reduced"), 1)
        dve.tensor_scalar(ang, ang, PI, -PI, ALU.min, ALU.max).then_inc(S("rope_reduced"), 1)

        t.add("bank")
        dve.wait_ge(S("t_free0"), 2)
        xpose_lo(xl, xh, KT, GAIN["pre0"])
        t.add("bank")
        with dve.Fori(0, WB) as g, t.loop(g, WB, unit=UNITS_POOL, chunk=6, bank=8, xh=4):
            for c in range(3):
                skip(8)
            xpose_lo(pll, plh, 8)
            skip(8)
            for c in range(2):
                s = chunk(4)
                if c == 0:
                    for k in range(2):
                        dve.wait_ge(S(f"mm_free{k}"), t.reg * 3 + (t.n["chunk"] - 1) // 2 + 1)
                for tt in range(2):
                    last = dve.tensor_tensor(mxs[:, c, tt, :], MM(s, tt), sg[:, tt, c * 512:(c + 1) * 512], ALU.mult)
                last.then_inc(S(f"mm_free{s}"), 1)
            t.add("bank", 4)
        for n in range(4):
            dve.wait_ge(S("y_hi"), n + 1)
            dve.tensor_tensor(yl[:, 8 * n:8 * n + 8, :], y32[:, 8 * n:8 * n + 8, :], yh[:, 8 * n:8 * n + 8, :].bitcast(F32), ALU.subtract)\
               .then_inc(S("y_lo"), 1)

        def columns(turns=2, units=8):
            with dve.Fori(0, turns) as g, t.loop(g, turns, unit=2 * units, chunk=2):
                for c in range(2):
                    skip(units)

        def layer_end(n, slot, mixer):
            evacuated(dve, mixer)
            mean(slot, D)
            inverse(slot)
            dve.wait_ge(S(f"post_gain_in{n}"), 16)

            def update(c):
                cols = slice(c * 512, c * 512 + 512)
                for tt in range(2):
                    last = dve.scalar_tensor_tensor(outt[:, tt, cols], outt[:, tt, cols], rstd[:, slot, tt:tt + 1], pgain[:, cols],
                                                    ALU.mult, ALU.mult)
                link(last)
                for tt in range(2):
                    last = dve.tensor_tensor(h[:, tt, cols], h[:, tt, cols], outt[:, tt, cols], ALU.add)
                last.then_inc(S(f"h_post{n}"), 1)

            update(0)
            skip(1)
            update(1)
            for c in range(3):
                skip(1)
            first_chunk(GAIN[f"ple{n}"], slot + 1, lambda g: update(g + 2) if g < 2 else None)
            evacuated(dve, f"proj{n}")
            for c in range(NCH):
                if c:
                    lo(8)
                    t.add("chunk")
                dve.wait_ge(S("w_used"), t.at("unit", RING - LEAD))
                k = t.n["chunk"] - 1
                dve.wait_ge(S(f"mm_free{k % 2}"), k // 2 + 2)
                cols = slice(c * 512, c * 512 + 512)
                for tt in range(2):
                    last = dve.tensor_tensor(sig[:, c % 2, tt, :], sig[:, c % 2, tt, :], proj[:, tt, cols], ALU.mult)
                link(last)
                for tt in range(2):
                    last = dve.tensor_tensor(h[:, tt, cols], h[:, tt, cols], sig[:, c % 2, tt, :], ALU.add)
                last.then_inc(S("gated"), 1)

        xpose_lo(pl, ph, 2)
        columns(units=16)
        layer_end(0, 1, "pool_out")
        first_chunk(GAIN["pre1"], 3)
        skip(8)
        skip(1)
        columns()
        evacuated(dve, "mla_in")
        products(dve, "mla_in")
        for c in range(2):
            mean(4 + c, Q_RANK, 1)
        inverse(4)
        inverse(5)

        def rope(x1, x2, cos, sin, tmp):
            link_all = [dve.tensor_tensor(tmp[0], x1, cos, ALU.mult), dve.tensor_tensor(tmp[1], x2, sin, ALU.mult),
                        dve.tensor_tensor(tmp[2], x2, cos, ALU.mult), dve.tensor_tensor(tmp[3], x1, sin, ALU.mult)]
            link(link_all[-1])
            dve.tensor_tensor(x1, tmp[0], tmp[1], ALU.subtract)
            return dve.tensor_tensor(x2, tmp[2], tmp[3], ALU.add)

        dve.wait_ge(S("rope_tables"), 1)
        last = rope(kpe[:, :, 0:32], kpe[:, :, 32:64], rc_cos, rc_sin, [x[:, :, 0, :] for x in (ra, rb, rc_, rd)])
        last.then_inc(S("k_roped"), 1)
        t.add("bank")
        xpose_lo(qll, qlh, 4, GAIN["q_norm"])
        xpose_lo(kll, klh, 4, GAIN["kv_norm"])
        for c in range(6):
            skip(2)
        with dve.Fori(0, 2) as g, t.loop(g, 2, unit=8, chunk=4):
            for c in range(4):
                skip(2)
        evacuated(dve, "uq")
        q4 = qt.rearrange("p t (h e) -> p t h e", e=192)
        for tt in range(2):
            cos, sin = (x[:, tt, :].unsqueeze(1).broadcast_to([128, HEADS, 32]) for x in (rc_cos, rc_sin))
            last = rope(q4[:, tt, :, 128:160], q4[:, tt, :, 160:192], cos, sin, [x[:, tt] for x in (ra, rb, rc_, rd)])
        link(last)
        evacuated(dve, "ukv")
        products(dve, "ukv")
        dve.sem_inc(S("mla_ready"), 2)

        def attention(heads, dv, scale, mask, put, keys0=128):
            def step(j, head):
                if head(3) is not None:
                    s = slot(j, 3)
                    dve.wait_ge(S("at_O"), t.at("at", j - 2))
                    link(dve.reciprocal(prc[:, s, :], psm[:, s, :]))
                    for q in range(2):
                        last = put(q, head(3), ps[:, s, q * dv:q * dv + dv], prc[:, s, q:q + 1])
                    last.then_inc(S("at_done"), 1)
                if head(1) is not None:
                    s = slot(j, 1)
                    dve.wait_ge(S("at_S"), t.at("at", j))
                    for q, (c0, nk) in enumerate(((0, keys0), (keys0, 256))):
                        src, dst = ps[:, s, c0:c0 + nk], LG_[s][:, c0:c0 + nk]
                        if mask is None:
                            last = dve.tensor_scalar(dst, src, scale, None, ALU.mult)
                        else:
                            last = dve.scalar_tensor_tensor(dst, src, scale, mask(head(1))[:, 256 - nk:256], ALU.mult, ALU.add)
                    link(last)
                    for q, (c0, nk) in enumerate(((0, keys0), (keys0, 256))):
                        last = dve.reduce_max(nmx[:, s, q:q + 1], LG_[s][:, c0:c0 + nk], AXX, negate=True)
                    last.then_inc(S("at_L"), 1)

            over_heads(dve, t, heads, step, behind=3, chain=8)

        def into(dst, dv, col):
            return lambda q, hd, src, r: dve.tensor_scalar(dst[:, q, bass.ds(hd * dv + col, dv)], src, r, None, ALU.mult)

        def gated_into(q, hd, src, r):
            g = gm[:, q, bass.ds(hd * VD, VD)]
            return dve.scalar_tensor_tensor(g, src, r, g, ALU.mult, ALU.mult)

        dve.wait_ge(S("causal_in"), 16)
        attention(HEADS, VD, (NOPE + ROPE) ** -0.5, lambda hd: causal, gated_into)
        xpose_lo(pl, ph, 2)
        first_chunk()
        for c in range(1, NCH):
            skip(8)
        layer_end(1, 6, "mla_out")
        first_chunk(GAIN["mem"], 8)
        skip(8)
        first_chunk(GAIN["mix"], 9)
        skip(8)
        columns(5)
        skip(1)
        evacuated(dve, "z")
        products(dve, "z")
        dve.wait_ge(S("hyb_in"), 16 * 7)
        t.add("bank", 2)
        for tt in range(2):
            dve.tensor_tensor(lx[:, tt, C_KW:C_KW + B_H], z[:, tt, Z_FL:Z_FL + B_H], fbias, ALU.add)
        for tt in range(2):
            dve.wait_ge(S("t_full"), t.at("bank", 1))
            b = t.n["bank"] % 4
            dve.tensor_copy(lx[:, tt, 0:C_KW], TB(b)[:, 0:C_KW]).then_inc(S(f"t_free{b}"), 1)
            t.add("bank")
        t.add("bank")
        for b in range(2):
            n = t.n["bank"] - 3 + b
            dve.wait_ge(S(f"t_free{n % 4}"), n // 4 + 2)
        link(dve.tensor_scalar(lm, lx, 0.0, None, ALU.min))
        dve.scalar_tensor_tensor(la, lx, 0.0, lm, ALU.max, ALU.subtract).then_inc(S("gate_abs"), 1)
        dve.wait_ge(S("gate_exp"), 2)
        link(dve.tensor_tensor(lgd, lm, la, ALU.subtract))
        dve.tensor_scalar(lf8, lgd[:, :, C_KW:C_KW + B_H], 8.0, None, ALU.mult).then_inc(S("log_forget"), 1)
        t.add("bank", A_H // 2)
        banks_read(dve, t)
        attention(A_H, 64, 0.125, lambda hd: relb[:, bass.ds(hd, 1), :].rearrange("p o n -> p (o n)"), into(mix, 64, 0))
        attention(B_H, 64, 0.125, lambda hd: causal, into(mix, 64, A_W))
        t.add("bank", C_H)
        dve.wait_ge(S("gla_in"), 48)

        def attn_part(tt, lv, first=False):
            dve.wait_ge(S("t_full"), t.at("bank", 1))
            b = t.n["bank"] % 4
            src = TB(b).rearrange("p (h n) -> p h n", h=C_H)
            if first:
                ins = dve.tensor_tensor(gat[:, tt], src, gmask[:, 0, :].unsqueeze(1).broadcast_to([128, C_H, 128]), ALU.mult)
            elif lv == 0:
                ins = dve.tensor_copy(gat[:, 2], src)
            else:
                ins = dve.copy_predicated(gat[:, tt], gmask[:, lv, :].bitcast(I32).unsqueeze(1).broadcast_to([128, C_H, 128]), src)
            ins.then_inc(S(f"t_free{b}"), 1)
            t.add("bank")

        for tt in range(2):
            attn_part(tt, 0, True)
        banks_read(dve, t)
        for lv in range(8):
            dve.wait_ge(S("gla_e"), lv + 1)
            dve.tensor_tensor(gqs, gq, ge, ALU.mult)
            dve.tensor_tensor(gks, gk, ge, ALU.mult).then_inc(S("gla_s"), 1)
            for tt in range(2 if lv else 1):
                attn_part(tt, lv)
            banks_read(dve, t)
        dve.wait_ge(S("gla_o"), 1)
        for tt in range(2):
            last = dve.tensor_copy(oc[:, tt], ps[:, 0:4, tt * C_DV:(tt + 1) * C_DV])
        link(last)
        link(dve.tensor_tensor(osq, oc, oc, ALU.mult))
        link(dve.reduce_sum(cst[:, 0, :], osq.rearrange("p t h n -> p (t h) n"), AXX))
        dve.tensor_scalar(cst[:, 0, :], cst[:, 0, :], 1.0 / C_DV, EPS, ALU.mult, ALU.add).then_inc(S("gla_ms"), 1)
        dve.wait_ge(S("gla_root"), 1)
        link(dve.reciprocal(cst[:, 2, :], cst[:, 1, :]))
        oc8 = oc.rearrange("p t h n -> p (t h) n")
        link(dve.tensor_tensor(oc8, oc8, cst[:, 2, :].unsqueeze(2).broadcast_to([128, 8, C_DV]), ALU.mult))
        link(dve.tensor_tensor(oc8, oc8, cnb.unsqueeze(1).broadcast_to([128, 8, C_DV]), ALU.mult))
        dve.wait_ge(S("rc_silu"), 1)
        mc = mix[:, :, A_W + B_W:D]
        dve.tensor_tensor(mc, mc, oc.rearrange("p t h n -> p t (h n)"), ALU.mult).then_inc(S("mix_ready"), 1)

        def add_chunk(s, col):
            for tt in range(2):
                hc = h[:, tt, bass.ds(col, 512)]
                last = dve.tensor_tensor(hc, hc, MM(s, tt), ALU.add)
            last.then_inc(S(f"mm_free{s}"), 1)

        s = first_chunk()
        dve.wait_ge(S("w_used"), t.at("unit", RING - LEAD))
        add_chunk(s, 0)
        for c in range(1, NCH):
            add_chunk(chunk(8), c * 512)
        first_chunk(GAIN["cross"], 10)
        attention(4, 128, 128 ** -0.5, None, into(cot, 128, 0), keys0=256)
        xpose_lo(xl, xh, 4)
        for c in range(NCH):
            add_chunk(chunk(2), c * 512)
        first_chunk(GAIN["ffn"], 11)

        def up_turn(width, tile, then, units=8):
            nt = width // 128
            s = chunk(units)
            for tt in range(2):
                last = dve.tensor_scalar(fvs[:, tt, 0:width], MM(s, tt)[:, 0:width], rstd[:, 11, tt:tt + 1], None, ALU.mult)
            last.then_inc(S(f"mm_free{s}"), 1)
            lo(min(then, 1))
            b0 = t.n["bank"] % 4
            bank = lambda k: TB((b0 + k // 2) % 4)[:, (k % 2) * 256:(k % 2) * 256 + 256]
            col = lambda name, k: gain[:, bass.ds(tile + (GAIN[name] + k), 1)]
            dve.wait_ge(S("t_full"), t.at("bank", 2))
            for k in range(nt):
                last = dve.tensor_scalar(fcv[:, k, :], bank(k), col("conv_w2", k), col("conv_b", k), ALU.mult, ALU.add)
            link(last)
            lo(min(then, 1))
            for k in range(nt):
                last = dve.scalar_tensor_tensor(fcv[:, k, 1:T], bank(k)[:, 0:T - 1], col("conv_w1", k), fcv[:, k, 1:T], ALU.mult, ALU.add)
            link(last)
            lo(min(then, 1))
            for k in range(nt):
                last = dve.scalar_tensor_tensor(fcv[:, k, 2:T], bank(k)[:, 0:T - 2], col("conv_w0", k), fcv[:, k, 2:T], ALU.mult, ALU.add)
                if k == 1:
                    last.then_inc(S(f"t_free{b0}"), 1)
            link(last)
            dve.sem_inc(S(f"t_free{(b0 + 1) % 4}"), 1)
            dve.sem_inc(S("conv_done"), 1)
            t.add("bank", 2)
            t.add("conv")
            if then:
                skip(then - 3)
            dve.wait_ge(S("t_full"), t.at("bank", 2))
            dve.wait_ge(S("conv_silu"), t.at("conv"))
            for k2 in range(2):
                n = min(2, nt - 2 * k2)
                b = t.n["bank"] % 4
                ins = dve.tensor_tensor(fy[:, bass.ds(tile + 2 * k2, n), :], fcv[:, 2 * k2:2 * k2 + n, :],
                                        TB(b)[:, 0:n * 256].rearrange("p (k n) -> p k n", n=256), ALU.mult)
                ins.then_inc(S("y_pairs") if k2 else S(f"t_free{b}"), 1)
                t.add("bank")
            dve.wait_ge(S("y_pairs"), t.at("pair", 1))
            dve.sem_inc(S(f"t_free{b}"), 1)
            t.add("pair")

        with dve.Fori(0, 9) as g, t.loop(g, 9, unit=16, chunk=2, chain=3, bank=4, conv=1, pair=1):
            up_turn(512, g * 4, 8)
        up_turn(512, 36, 8)

        def y_lo(n):
            k = slice(8 * n, min(8 * n + 8, FKT))
            dve.wait_ge(S("fy_hi"), n + 1)
            dve.tensor_tensor(fyl[:, k, :], fy[:, k, :], fyh[:, k, :].bitcast(F32), ALU.subtract).then_inc(S("fy_lo"), 1)

        for n in range(4):
            y_lo(n)
            lo(2)
        up_turn(384, 40, 0, units=0)
        for n in range(4, 6):
            y_lo(n)
        for c in range(NCH):
            add_chunk(chunk(len(units_of(FKT))), c * 512)
        norm(12)
        dve.wait_ge(S("final_gain_in"), 16)
        for tt in range(2):
            dve.scalar_tensor_tensor(fout[:, tt, :], h[:, tt, :], rstd[:, 12, tt:tt + 1], fgain, ALU.mult, ALU.mult)\
               .then_inc(S("final"), 1)

    @block.gpsimd
    def _(pool):
        t = Tally()

        def stage(heads, d, q_src, k_src, q_cols=None, rows_src=None):
            def step(j, head):
                s = slot(j, 0)
                if head(4) is None:
                    if j == 0:
                        pool.wait_ge(S("at_done"), t.at("at", 4))
                elif rows_src is not None:
                    pool.wait_ge(S("at_S"), t.at("at", j - 3))
                else:
                    pool.wait_ge(S("at_T"), t.at("at", j - 3))
                pool.tensor_copy(SQ[s][:, :, 0:q_cols or d], q_src(head(0)))
                if rows_src is not None:
                    pool.tensor_copy(QP[s][0:2, :], rows_src(head(0)))
                pool.tensor_copy(SK[s][:, :, 0:d], k_src(head(0))).then_inc(S("at_stage"), 1)

            over_heads(pool, t, heads, step)

        def load(dst, src, sem):
            pool.dma_start(dst, src).then_inc(S(sem), 16)

        def layer_end(n):
            products(pool, "pool" if n == 0 else "ukv", 8)
            load(pgain, a["post_norm"][n:n + 1, :].broadcast_to([128, D]), f"post_gain_in{n}")

        load(posi, a["positions"].rearrange("o (t p) -> p (o t)", p=128), "pos_in")
        load(freqs, a["c_freq"].broadcast_to([128, 32]), "pos_in")
        load_gains(pool, (1, 2, 3), "rows_in1")
        load(causal, a["c_causal"], "causal_in")
        load(ptok, tokens(a["p"][0, 0]), "ple_in0")
        layer_end(0)
        pool.wait_ge(S("mla_ready"), 2)
        load(ptok, tokens(a["p"][1, 0]), "ple_in1")
        stage(HEADS, 128, lambda hd: qt[:, :, bass.ds(hd * 192, 192)], lambda hd: kv[:, :, bass.ds(hd * 256, 128)], q_cols=192)
        layer_end(1)
        load(memt, tokens(a["mem_2"][0]), "mem_in")
        products(pool, "z")
        pool.memset(reltab, 1.0).then_inc(S("ones_set"), 1)
        pool.memset(glt, 1.0).then_inc(S("ones_set"), 1)
        load(relone, a["c_rel"], "hyb_in")
        load(w2a[0:16, :], a["c_gate_w2_2"][0], "hyb_in")
        load(w2a[16:17, :], a["c_gate_b_2"], "hyb_in")
        load(fbias, a["f_bias_2"].broadcast_to([128, B_H]), "hyb_in")
        load(trio, a["c_trio"], "hyb_in")
        load(flip, a["c_flip"], "hyb_in")
        pool.wait_ge(S("ones_set"), 2)
        load(reltab[0:BUCKETS, :], a["rel_table_2"], "hyb_in")
        pool.wait_ge(S("log_forget"), 1)
        pool.wait_ge(S("rel_out"), 16)
        pool.wait_ge(S("sums_read"), 1)
        stage(A_H, 64, lambda hd: z[:, :, bass.ds(hd * 64 + Z_QA, 64)], lambda hd: z[:, :, bass.ds(hd * 64 + Z_KA, 64)])
        heads_done(pool, "b")
        pool.memset(ck2, 1.0).then_inc(S("forget_ones"), 1)
        pool.memset(cq2, 1.0).then_inc(S("forget_ones"), 1)
        pool.wait_ge(S("forget_in"), 32)
        stage(B_H, 64, lambda hd: z[:, :, bass.ds(hd * 64 + Z_QB, 64)], lambda hd: z[:, :, bass.ds(hd * 64 + Z_KB, 64)],
              rows_src=lambda hd: cq2[:, bass.ds(hd, 1), :].rearrange("p o n -> p (o n)"))
        heads_done(pool, "cross")
        load(gmask.rearrange("p l n -> p (l n)"), a["c_masks"], "gla_in")
        load(dmat.rearrange("p l n -> p (l n)"), a["c_decay"], "gla_in")
        load(cnb, a["c_norm_2"].broadcast_to([128, C_DV]), "gla_in")
        evacuated(pool, "cq")
        stage(4, 128, lambda hd: cqt[:, :, bass.ds(hd * 128, 128)], lambda hd: kvm[:, :, bass.ds(hd * 128, 128)])
        products(pool, "up")
        load(fgain, a["norm_final_2"].unsqueeze(0).broadcast_to([128, D]), "final_gain_in")

    ctx.close()


_INS = ["x", "p", "positions", "pre_norm", "post_norm", "pool_w_in", "pool_w_group", "pool_scale", "pool_w_out", "mla_w_in",
        "mla_q_norm", "mla_w_uq", "mla_kv_norm", "mla_w_ukv", "mla_w_out", "ple_norm", "ple_w_gate", "ple_w_proj", "mem_2",
        "rel_table_2", "mem_norm_2", "norm_final_2", "norm_mix_2", "w_in_2", "f_bias_2", "c_gate_w2_2", "c_gate_b_2",
        "c_norm_2", "w_out_2", "norm_cross_2", "w_cq_2", "w_ckv_2", "w_co_2", "norm_ffn_2", "w_up_2", "conv_w_2",
        "conv_b_2", "w_down_2"]


def kernel(**inputs):
    import concourse.bacc as bacc
    from concourse.bass_utils import run_bass_kernel_spmd

    nc = bacc.Bacc("TRN2", target_bir_lowering=False, num_devices=1)
    given = {name: np.ascontiguousarray(inputs[name]) for name in _INS}
    given.update({f"c_{name}": value for name, value in shape_constants().items()})
    arrays = {f"in_{name}": value for name, value in given.items()}
    aps = {name: nc.dram_tensor(f"in_{name}", value.shape, mybir.dt.from_np(value.dtype), kind="ExternalInput").ap()
           for name, value in given.items()}
    out = nc.dram_tensor("out_0", (1, T, D), F32, kind="ExternalOutput").ap()
    build(nc, aps, out)
    r = run_bass_kernel_spmd(nc, [arrays], core_ids=[0])
    return r.results[0]["out_0"]
```

```python
import math
from collections import namedtuple
from contextlib import ExitStack, contextmanager

import numpy as np

import concourse.bass as bass
from concourse import mybir

F32, F32R, I32 = mybir.dt.float32, mybir.dt.float32r, mybir.dt.int32
ACT = mybir.ActivationFunctionType
ALU = mybir.AluOpType
AXX = mybir.AxisListType.X

D = 2048
T = 256
KT = D // 128
NCH = D // 512
EPS = 1e-6
E_POOL = 4096
WINDOWS = (2, 4, 8, 16)
HEADS = 16
Q_RANK = KV_RANK = 512
NOPE, ROPE, VD = 128, 64, 128
A_W, B_W, C_KW, C_VW = 768, 512, 384, 768
A_H, B_H, C_H, C_DK, C_DV = 12, 8, 4, 96, 192
Z_W = 3 * A_W + 3 * B_W + B_H + 2 * C_KW + 2 * C_VW + 16
Z_QA, Z_KA, Z_VA = 0, A_W, 2 * A_W
Z_QB, Z_KB, Z_VB = 3 * A_W, 3 * A_W + B_W, 3 * A_W + 2 * B_W
Z_FL = 3 * A_W + 3 * B_W
Z_QC = Z_FL + B_H
Z_KC = Z_QC + C_KW
Z_VC = Z_KC + C_KW
Z_RC = Z_VC + C_VW
Z_GL = Z_RC + C_VW
D_FF = 5504
FKT = D_FF // 128
BUCKETS, MAX_DIST = 32, 2048
MASKED = -1e30
MIN_W = (Q_RANK + KV_RANK + ROPE + D) // 7
ZW = 480
Z_FIRST = [(8 * ZW, ZW), (12 * ZW, Z_W - 12 * ZW)] + [(c * ZW, ZW) for c in range(4)]
Z_LAST = [(c * ZW, ZW) for c in (9, 10, 11)]
assert Z_FL == 8 * ZW and 12 * ZW <= Z_W - 16
RAW, RING, LEAD = 8, 4, 3

LINEARS = [("pool", 160, 24), ("pool_out", 64, 4), ("proj0", 4, 4), ("gate0", 32, 4), ("mla_in", 56, 7), ("uq", 12, 6),
           ("ukv", 16, 8), ("mla_out", 32, 4), ("proj1", 4, 4), ("gate1", 32, 4), ("ckv", 16, 2), ("z", 104, 13),
           ("out2", 32, 4), ("cq", 8, 1), ("co", 8, 4), ("up", 176, 22), ("down", 96, 4)]
UNITS_END = {n: sum(u for _, u, _ in LINEARS[:k + 1]) for k, (n, _, _) in enumerate(LINEARS)}
CHUNKS_END = {n: sum(c for _, _, c in LINEARS[:k + 1]) for k, (n, _, _) in enumerate(LINEARS)}
TOTAL_UNITS = UNITS_END["down"]

GAIN_TILES = [
    [("pre0", 16), ("pre1", 16), ("ple0", 16), ("ple1", 16), ("pool_scale", 32), ("q_norm", 4), ("kv_norm", 4), ("mix", 16)],
    [("cross", 16), ("ffn", 16), ("mem", 16), ("conv_b", 43)],
    [("conv_w0", 43), ("conv_w1", 43)],
    [("conv_w2", 43)],
]
GAIN = {name: 128 * t + sum(n for _, n in tile[:k]) for t, tile in enumerate(GAIN_TILES) for k, (name, _) in enumerate(tile)}


def shape_constants():
    s, t = np.arange(128)[:, None], np.arange(256)[None, :]
    ident = np.eye(128, dtype=np.float32)
    band = np.zeros((128, 4, 384), np.float32)
    for j, w in enumerate(WINDOWS):
        full = np.zeros((256, 256), np.float32)
        for q in range(256):
            full[max(0, q - w + 1):q + 1, q] = np.float32(1.0) / np.float32(min(q + 1, w))
            full[q, q] -= 1.0
        band[:, j, :256] = full[:128]
        band[:, j, 256:] = full[128:, 128:]
    causal = np.where(s + 128 - t >= 0, 0.0, MASKED).astype(np.float32)
    m = np.arange(384)
    dist = 255 - m
    d = np.maximum(dist, 1).astype(np.float32)
    half = BUCKETS // 2
    large = half + (np.log(d / half) / math.log(MAX_DIST / half) * (BUCKETS - half)).astype(np.int32)
    bucket = np.where(dist < half, dist, np.minimum(large, BUCKETS - 1))
    rel = np.zeros((33, 384), np.float32)
    for c in range(384):
        if dist[c] >= 0:
            rel[bucket[c], c] = 1.0
            kept = int(dist[c] <= 128) + int(dist[c] % 4 == 0) + int(dist[c] % 16 == 0)
            rel[32, c] = np.log(np.float32(kept)) if kept else MASKED
        else:
            rel[32, c] = MASKED
    a, b = np.arange(128)[:, None], np.arange(128)[None, :]
    decay = [(a > b), (a <= b)]
    masks = [np.eye(128, dtype=bool)]
    for size in (128, 64, 32, 16, 8, 4, 2):
        mid = b // size * size + size // 2
        decay.append(((b >= mid) & (a >= mid) & (a <= b)) | ((b < mid) & (a > b) & (a < mid)))
        masks.append((a // size == b // size) & (b % size >= size // 2) & (a % size < size // 2))
    decay = np.stack(decay, 1).astype(np.float32).reshape(128, 9 * 128)
    masks = np.stack(masks, 1).astype(np.float32).reshape(128, 8 * 128)
    trio = np.concatenate([(a <= b), np.ones((128, 128), bool)], 1).astype(np.float32)
    freq = (10000.0 ** (-np.arange(0, ROPE, 2, dtype=np.float32) / np.float32(ROPE))).astype(np.float32)
    return {"ident": ident, "flip": np.ascontiguousarray(ident[::-1]), "band": band.reshape(128, 4 * 384), "causal": causal, "rel": rel, "decay": decay,
            "masks": masks, "trio": trio, "freq": freq[None, :],
            "ones": np.ones((1, B_H * T), np.float32)}


Attention = namedtuple("Attention", "name heads d dv keys0")


class Tally:

    def __init__(self):
        self.n, self.reg, self.per = {}, None, {}

    def at(self, name, k=0):
        v = self.n.get(name, 0) + k
        return self.reg * self.per[name] + v if self.reg is not None and self.per.get(name) else v

    def add(self, name, k=1):
        self.n[name] = self.n.get(name, 0) + k

    @contextmanager
    def loop(self, reg, turns, **per):
        begin = dict(self.n)
        self.reg, self.per = reg, per
        yield
        got = {k: v - begin.get(k, 0) for k, v in self.n.items() if v != begin.get(k, 0)}
        assert got == {k: v for k, v in per.items() if v}, f"loop counts {got}, said {per}"
        for k, v in got.items():
            self.n[k] = begin.get(k, 0) + turns * v
        self.reg, self.per = None, {}


def units_of(nkt, width=512):
    if nkt == FKT:
        return [(2 * u, 2 * u + 1) for u in range(19)] + [(k,) for k in range(38, 43)]
    per = 1024 // width if width < 256 else 2
    return [tuple(range(k, min(k + per, nkt))) for k in range(0, nkt, per)]


def build(nc, a, out):
    ctx = ExitStack()
    ctx.enter_context(nc.allow_non_contiguous_dma(reason="narrow weight columns, vectors"))
    sems = {}

    def S(name):
        if name not in sems:
            sems[name] = ctx.enter_context(nc.semaphore(name))
        return sems[name]

    base = (nc.sbuf_base + 63) // 64 * 64
    limit = nc.sbuf_usable_end

    def at(name, off, shape, dt=F32):
        size = int(np.prod(shape[1:])) * 4
        assert base + off + size <= limit, (name, base + off + size - limit)
        return nc.alloc_sbuf_tensor_at(name, shape, dt, offset=base + off)[:]

    pos = [0]

    def fixed(name, shape, dt=F32):
        off = pos[0]
        pos[0] += (int(np.prod(shape[1:])) * 4 + 31) // 32 * 32
        return at(name, off, shape, dt)

    raw = fixed("raw", [128, RAW, 1024])
    w_hi = fixed("w_hi", [128, RING, 1024], F32R)
    w_lo = fixed("w_lo", [128, RING, 1024], F32R)
    h = fixed("h", [128, 2, D])
    ident = fixed("identity", [128, 128])
    gain = fixed("gain_columns", [128, 512])
    causal = fixed("causal_mask", [128, 256])
    junk = fixed("junk", [128, 512])
    sums = fixed("square_sums", [128, 16, 2, 4])
    ms = fixed("mean_square", [128, 16, 2])
    rt = fixed("root", [128, 16, 2])
    rstd = fixed("rstd", [128, 16, 2])
    rc_cos = fixed("rope_cos", [128, 2, 32])
    rc_sin = fixed("rope_sin", [128, 2, 32])
    A0 = pos[0]

    def arena(name, off, shape, dt=F32):
        return at(name, A0 + off, shape, dt)

    xh = arena("x_hi", 0, [128, KT, T], F32R)
    xl = arena("x_lo", 16384, [128, KT, T], F32R)
    rows = arena("gain_rows", 32768, [128, 4, 128])
    hsq = arena("x_squares", 71680, [128, 2, D])
    y32 = arena("pool_y", 32768, [128, 32, T])
    band = arena("band", 65536, [128, 4, 384])
    ut = arena("u_tokens", 71680, [128, 2, 1024])
    sg = arena("silu_gate", 79872, [128, 2, 1024])
    plh = arena("pooled_hi", 88064, [128, 8, T], F32R)
    pll = arena("pooled_lo", 96256, [128, 8, T], F32R)
    mxs = arena("mixed_gated", 104448, [128, 2, 2, 512])
    yh = arena("pool_y_hi", 0, [128, 32, T], F32R)
    yl = arena("pool_y_lo", 32768, [128, 32, T], F32R)
    outt = arena("mixer_out", 65536, [128, 2, D])
    proj = arena("ple_proj", 81920, [128, 2, D])
    pgain = arena("post_gain", 98304, [128, D])
    sig = arena("ple_gate", 106496, [128, 2, 2, 512])
    ptok = arena("ple_tokens", 116736, [128, 2, 256])
    ph = arena("ple_hi", 118784, [128, 2, T], F32R)
    pl = arena("ple_lo", 120832, [128, 2, T], F32R)
    lat = arena("latents", 32768, [128, 2, 1024])
    kpe = arena("k_pe", 40960, [128, 2, 64])
    kpt = arena("k_pe_T", 41472, [64, T])
    gm = arena("mla_gate", 42496, [128, 2, D])
    qt = arena("mla_q", 58880, [128, 2, HEADS * 192])
    kv = arena("mla_kv", 83456, [128, 2, HEADS * 256])
    qlh = arena("q_lat_hi", 83456, [128, 4, T], F32R)
    qll = arena("q_lat_lo", 87552, [128, 4, T], F32R)
    klh = arena("kv_lat_hi", 8192, [128, 4, T], F32R)
    kll = arena("kv_lat_lo", 12288, [128, 4, T], F32R)
    krope = [arena(f"k_rope{n}", 91648 + 256 * n, [128, 2, 32]) for n in range(4)]
    ra = arena("rope_a", 16384, [128, 2, HEADS, 32])
    rb = arena("rope_b", 20480, [128, 2, HEADS, 32])
    rc_ = arena("rope_c", 24576, [128, 2, HEADS, 32])
    rd = arena("rope_d", 28672, [128, 2, HEADS, 32])
    posi = arena("positions", 112640, [128, 2], I32)
    posf = arena("positions_f", 112672, [128, 2])
    freqs = arena("rope_freq", 112704, [128, 32])
    ang = arena("angle", 112896, [128, 2, 32])
    turns_ = arena("angle_turns", 113152, [128, 2, 32])
    red = arena("angle_reduced", 113408, [128, 2, 32])
    MLA_STAGE = [32768, 35328, 37888, 118784]
    SQ = {"mla": [arena(f"q_staged{j}", MLA_STAGE[j], [128, 2, 192]) for j in range(4)]}
    SK = {"mla": [arena(f"k_staged{j}", MLA_STAGE[j] + 1536, [128, 2, 128]) for j in range(4)]}
    QK = [arena(f"qk_T{j}", 7680 * j + 2560, [128, 2, T]) for j in range(4)]
    PTS = [arena(f"p_T{j}", 7680 * j + 2560, [128, 4, 128]) for j in range(4)]
    QP = [arena(f"q_pe_T{j}", 7680 * j + 4608, [64, T]) for j in range(4)]
    LG_ = [arena(f"logits{j}", 7680 * j + 5632, [128, 512]) for j in range(4)]
    assert 7680 * 4 <= 32768
    nmx = arena("neg_max", 30720, [128, 4, 2])
    psm = arena("prob_sum", 30752, [128, 4, 2])
    prc = arena("prob_scale", 30784, [128, 4, 2])
    KVM = 115456 - 512
    memt = arena("mem_tokens", 32768, [128, 2, D])
    kvm = arena("mem_kv", KVM, [128, 2, 1024])
    relb = arena("rel_bias", 32768, [128, A_H, T])
    Z0 = 32768 + A_H * T * 4
    z = arena("z", Z0, [128, 2, Z_W])
    MIX0 = Z0 + 2 * Z_W * 4
    mix = arena("mixed", MIX0, [128, 2, D])
    hyb_stage = [MIX0 + 4 * (A_W + B_W) + 1024 * j for j in range(3)] + [MIX0 + 4 * D + 4 * (A_W + B_W)]
    SQ["a"] = SQ["b"] = [arena(f"hybrid_q_staged{j}", hyb_stage[j], [128, 2, 64]) for j in range(4)]
    SK["a"] = SK["b"] = [arena(f"hybrid_k_staged{j}", hyb_stage[j] + 512, [128, 2, 64]) for j in range(4)]
    lgd = arena("log_decay", 110784, [128, 2, 392])
    la = arena("gate_abs", MIX0, [128, 2, 392])
    lm = arena("gate_min", MIX0 + 3136, [128, 2, 392])
    glt = arena("gl_T", MIX0 + 6272, [17, T])
    w2a = arena("gate_w2", MIX0 + 7296, [17, C_KW])
    trio = arena("running_sum", MIX0 + 8832, [128, 256])
    relone = arena("rel_onehot", MIX0 + 9856, [33, 384])
    relrow = arena("rel_rows", MIX0 + 11392, [A_H, 384])
    flip = arena("flip", MIX0 + 12928, [128, 128])
    reltab = arena("rel_table", MIX0 + 13440, [33, A_H])
    fbias = arena("f_bias", MIX0 + 13504, [128, B_H])
    lf8 = arena("log_forget", MIX0 + 13536, [128, 2, B_H])
    crow, ncrow = junk[0:B_H, 0:256], junk[0:B_H, 256:512]
    cq2 = arena("forget_q", 32768, [2, B_H, T])
    ck2 = arena("forget_k", 40960, [2, B_H, T])
    dmat = arena("gla_sums", Z0 + 4096, [128, 9, 128])
    gmask = arena("gla_masks", Z0 + 4 * Z_W, [128, 8, 128])
    cnb = arena("c_norm", Z0 + 4 * Z_W + 4096, [128, C_DV])
    assert 4096 + 9 * 512 <= 3 * A_W * 4 and 4096 + C_DV * 4 <= 3 * A_W * 4
    gq = arena("gla_q_T", 0, [96, C_H, T])
    gk = arena("gla_k_T", 4096, [96, C_H, T])
    ge = [arena(f"gla_decay{n}", o, [96, C_H, T]) for n, o in enumerate((8192, 26624))]
    gqs = [arena(f"gla_q_decayed{n}", o, [96, C_H, T]) for n, o in enumerate((12288, 32768))]
    gks = [arena(f"gla_k_decayed{n}", o, [96, C_H, T]) for n, o in enumerate((16384, 36864))]
    gat = arena("gla_attn", 20480, [128, 3, C_H, 128])
    oc = arena("gla_out", 40960, [128, 2, C_H, C_DV])
    osq = arena("gla_squares", 32768, [128, 2, C_H, C_DV])
    cst = arena("gla_stats", 47104, [128, 3, 8])
    cqt = arena("cross_q", 32768, [128, 2, 512])
    cot = arena("cross_out", 36864, [128, 2, 512])
    fy = arena("ffn_y", 32768, [128, FKT, T])
    fgs = arena("ffn_gate", 109568, [128, 2, 512])
    fvs = arena("ffn_val", 113664, [128, 2, 512])
    fcv = arena("ffn_conv", 117760, [128, 4, T])
    fyl = arena("ffn_y_lo", 32768, [128, FKT, T], F32R)
    fyh = arena("ffn_y_hi", 76800, [128, FKT, T], F32R)
    fgain = arena("final_gain", 0, [128, D])
    fout = arena("final_out", 8192, [128, 2, D])

    ps = ctx.enter_context(nc.psum_tensor("ps", [128, 8, 512], F32))[:]

    def MM(s, tt):
        return ps[:, 2 * s + tt, :]

    def TB(b):
        return ps[:, 4 + b, :]

    rel_scratch = nc.dram_tensor("rel_scratch", (A_H, 384), F32, kind="Internal").ap()

    def weights(ap):
        return ap.rearrange("(k p) n -> p k n", p=128)

    w_pool = weights(a["pool_w_in"][0])
    w_group = a["pool_w_group"][0].rearrange("g (k p) n -> p g k n", p=128)
    w_pout = weights(a["pool_w_out"][0])
    w_proj = [weights(a["ple_w_proj"][n]) for n in range(2)]
    w_gate = [weights(a["ple_w_gate"][n]) for n in range(2)]
    w_min = weights(a["mla_w_in"][0])
    w_uq, w_ukv, w_mout = weights(a["mla_w_uq"][0]), weights(a["mla_w_ukv"][0]), weights(a["mla_w_out"][0])
    w_ckv, w_cq, w_co = weights(a["w_ckv_2"][0]), weights(a["w_cq_2"][0]), weights(a["w_co_2"][0])
    w_in2, w_out2 = weights(a["w_in_2"][0]), weights(a["w_out_2"][0])
    w_up, w_down = weights(a["w_up_2"][0]), weights(a["w_down_2"][0])

    def tokens(ap):
        return ap.rearrange("(t p) n -> p t n", p=128)

    UNITS_POOL = 4 * 8 + 2 * 4
    Y_PIECES = [0, 2, 4, 8, 16, 24, 32]
    WB = len(WINDOWS)

    def products(eng, linear, more=0):
        eng.wait_ge(S("w_used"), UNITS_END[linear] + RING + more)

    def evacuated(eng, linear):
        for back in (2, 1):
            c = CHUNKS_END[linear] - back
            eng.wait_ge(S(f"mm_free{c % 2}"), c // 2 + 2)

    def gate_columns_out(eng):
        for n in (CHUNKS_END["ckv"], CHUNKS_END["ckv"] + 1):
            eng.wait_ge(S(f"mm_free{n % 2}"), n // 2 + 2)

    def chunk_out(eng, linear, c, of=4):
        n = CHUNKS_END[linear] - of + c
        eng.wait_ge(S(f"mm_free{n % 2}"), n // 2 + 2)

    def banks_read(eng, t):
        for b in range(4):
            eng.wait_ge(S(f"t_free{b}"), (t.n["bank"] - b + 3) // 4 + 1)

    def gated(eng, n, chunks=4):
        eng.wait_ge(S("gated"), 2 + 4 * n + chunks)

    AT = {"mla": 0, "a": 16, "b": 28, "cross": 36, "end": 40}

    def heads_done(eng, before):
        eng.wait_ge(S("at_done"), AT[before] + 4)

    vectors = {"pre0": a["pre_norm"][0], "pre1": a["pre_norm"][1], "ple0": a["ple_norm"][0], "ple1": a["ple_norm"][1],
               "pool_scale": a["pool_scale"][0], "q_norm": a["mla_q_norm"][0], "kv_norm": a["mla_kv_norm"][0],
               "mix": a["norm_mix_2"][0], "cross": a["norm_cross_2"][0], "ffn": a["norm_ffn_2"][0],
               "mem": a["mem_norm_2"], "conv_b": a["conv_b_2"][0], "conv_w0": a["conv_w_2"][0, 0],
               "conv_w1": a["conv_w_2"][0, 1], "conv_w2": a["conv_w_2"][0, 2]}

    def load_gains(eng, tiles, sem):
        for n in tiles:
            at_row = 0
            for name, r in GAIN_TILES[n]:
                eng.dma_start(rows[at_row:at_row + r, n, :], vectors[name].rearrange("(r c) -> r c", c=128)).then_inc(S(sem), 16)
                at_row += r

    MLA = Attention("mla", HEADS, NOPE, VD, 128)
    DILATED = Attention("a", A_H, 64, 64, 128)
    FORGETTING = Attention("b", B_H, 64, 64, 128)
    CROSS = Attention("cross", 4, 128, 128, 256)

    def over_heads(eng, t, parts, step, behind=0, **per_turn):
        before = None
        for part in parts:
            for j in range(4):
                step(j, lambda b: (part, j - b) if j >= b else before and (before, before.heads + j - b))
            t.add("at", 4)
            if part.heads > 4:
                with eng.Fori(0, part.heads // 4 - 1) as i, t.loop(i, part.heads // 4 - 1, at=4, **per_turn):
                    for j in range(4):
                        step(j, lambda b: (part, i * 4 + (4 + j - b)))
                    t.add("at", 4)
            before = part
        for j in range(behind):
            step(j, lambda b: (before, before.heads + j - b) if b > j else None)

    def slot(j, b):
        return (j - b) % 4

    block = ctx.enter_context(nc.Block())

    @block.sync
    def _(sp):
        t = Tally()

        def unit(src, kts, width):
            slot = t.n.get("unit", 0) % RAW
            sp.wait_ge(S("w_lo"), t.at("unit", 1))
            if t.reg is not None:
                sp.sem_inc(S("units_begun"), 1)
            n = len(kts) * width
            dst = raw[:, slot, 0:n].rearrange("p (k n) -> p k n", n=width)
            sp.dma_start(dst, src).then_inc(S(f"raw_full{slot}"), 16)
            t.add("unit")

        def chunk(w, nkt, col, width=512):
            for kts in units_of(nkt, width):
                unit(w[:, kts[0]:kts[-1] + 1, bass.ds(col, width)], kts, width)

        def load(dst, src, sem):
            sp.dma_start(dst, src).then_inc(S(sem), 16)

        load(ident, a["c_ident"], "ident_in")
        load_gains(sp, (0,), "rows_in0")
        for tt in range(2):
            load(h[:, tt, :], a["x"][0, tt * 128:(tt + 1) * 128, :], "h_in")
        load(band.rearrange("p w n -> p (w n)"), a["c_band"], "band_in")

        with sp.Fori(0, WB) as g, t.loop(g, WB, unit=UNITS_POOL):
            for half in range(2):
                for c in range(2):
                    chunk(w_pool, KT, g * 1024 + (half * E_POOL + c * 512))
            for c in range(2):
                for kts in units_of(8):
                    unit(w_group[:, bass.ds(g, 1), kts[0]:kts[-1] + 1, c * 512:(c + 1) * 512].rearrange("p g k n -> p (g k) n"),
                         kts, 512)
        with sp.Fori(0, 2) as g, t.loop(g, 2, unit=32):
            for c in range(2):
                chunk(w_pout, 32, g * 1024 + c * 512)

        def columns(w, col=0):
            with sp.Fori(0, 2) as g, t.loop(g, 2, unit=16):
                for c in range(2):
                    chunk(w, KT, g * 1024 + (c * 512 + col))

        def layer_end(n):
            for c in range(NCH):
                chunk(w_proj[n], 2, c * 512)
            columns(w_gate[n])

        layer_end(0)
        for c in range(7):
            chunk(w_min, KT, c * MIN_W, MIN_W)
        for c in range(6):
            chunk(w_uq, 4, c * 512)
        with sp.Fori(0, 2) as g, t.loop(g, 2, unit=8):
            for c in range(4):
                chunk(w_ukv, 4, g * 2048 + c * 512)
        columns(w_mout)
        layer_end(1)
        for c in range(2):
            chunk(w_ckv, KT, c * 512)
        for col, width in Z_FIRST:
            chunk(w_in2, KT, col, width)
        with sp.Fori(0, 2) as g, t.loop(g, 2, unit=16):
            for c in range(2):
                chunk(w_in2, KT, g * 2 * ZW + (c + 4) * ZW, ZW)
        for col, width in Z_LAST:
            chunk(w_in2, KT, col, width)
        chunk(w_out2, KT, 0)
        def forget_rows(dst, heads, ones_row, sums, sem):
            n = heads.stop - heads.start
            load(dst[ones_row:ones_row + 1].rearrange("o h t -> o (h t)"), a["c_ones"][:, 0:n * T], sem)
            load(dst[1 - ones_row:2 - ones_row].rearrange("o h t -> o (h t)"), sums[heads, :], sem)

        sp.wait_ge(S("at_L"), AT["a"] + 8)
        forget_rows(cq2, slice(0, 8), 0, crow, "forget_q")
        sp.wait_ge(S("at_stage"), AT["b"])
        forget_rows(ck2[:, 4:8, :], slice(0, 4), 1, ncrow, "forget_k0")
        sp.wait_ge(S("at_L"), AT["b"])
        forget_rows(ck2[:, 0:4, :], slice(4, 8), 1, ncrow, "forget_k1")
        for c in range(1, NCH):
            chunk(w_out2, KT, c * 512)
        chunk(w_cq, KT, 0)
        for c in range(NCH):
            chunk(w_co, 4, c * 512)
        with sp.Fori(0, 10) as g, t.loop(g, 10, unit=16):
            chunk(w_up, KT, g * 512 + D_FF)
            chunk(w_up, KT, g * 512)
        chunk(w_up, KT, 5120 + D_FF, 384)
        chunk(w_up, KT, 5120, 384)
        for c in range(NCH):
            chunk(w_down, FKT, c * 512)
        assert t.n["unit"] == TOTAL_UNITS, t.n
        for n in range(4):
            tt, cols = n // 2, slice(n % 2 * 1024, n % 2 * 1024 + 1024)
            sp.wait_ge(S("final"), n + 1)
            load(out[0, tt * 128:(tt + 1) * 128, cols], fout[:, tt, cols], "out_done")
        sp.wait_ge(S("out_done"), 64)

    @block.tensor
    def _(pe):
        t = Tally()
        pe.sem_inc(S("w_used"), RING)

        def take_bank():
            b = t.n.get("bank", 0) % 4
            pe.wait_ge(S(f"t_free{b}"), t.at(f"bank{b}", 1))
            t.add("bank")
            t.add(f"bank{b}")
            return b

        def to_bank(src, f0, tiles=2):
            b = take_bank()
            for k in range(tiles):
                for tt in range(2):
                    f = f0 + k * 128
                    last = pe.transpose(TB(b)[:, k * 256 + tt * 128:k * 256 + tt * 128 + 128], src[:, tt, f:f + 128], ident)
            last.then_inc(S("t_full"), 1)

        def xpose(src, nkt, ready=None):
            for g in range(nkt // 2):
                if ready:
                    ready(g)
                to_bank(src, g * 256)

        def last_banks(n):
            total = t.n["bank"]
            def ready(k):
                if k % 2 == 0:
                    g = total - n + k // 2
                    pe.wait_ge(S(f"t_free{g % 4}"), g // 4 + 2)
            return ready

        def chunk(xhi, xlo, nkt, width=512, ready=None):
            s = t.n.get("chunk", 0) % 2
            pe.wait_ge(S(f"mm_free{s}"), t.at(f"set{s}", 1))
            units = units_of(nkt, width)
            for kts in units:
                slot = t.n.get("unit", 0) % RING
                pe.wait_ge(S("w_lo"), t.at("unit", RAW + 1))
                for n, k in enumerate(kts):
                    if ready:
                        ready(k)
                    wh = w_hi[:, slot, n * width:(n + 1) * width]
                    wl = w_lo[:, slot, n * width:(n + 1) * width]
                    for tt in range(2):
                        tok = slice(tt * 128, tt * 128 + 128)
                        dst = MM(s, tt)[:, 0:width]
                        pe.matmul(dst, xhi[:, k, tok], wh, start=k == 0, stop=False)
                        pe.matmul(dst, xhi[:, k, tok], wl, start=False, stop=False)
                        last = pe.matmul(dst, xlo[:, k, tok], wh, start=False, stop=k == nkt - 1)
                last.then_inc(S("w_used"), 1)
                t.add("unit")
            t.add("chunk")
            t.add(f"set{s}")
            return s

        def first_chunk(src, source_ready=None, width=512, banks_ready=None):
            first = t.n["bank"]

            def turn(g):
                if source_ready:
                    source_ready(g)
                to_bank(src, g * 256)

            def ready(k):
                if k % 2 == 0:
                    if k // 2 + 3 < KT // 2:
                        turn(k // 2 + 3)
                    n = first + k // 2
                    pe.wait_ge(S(f"t_free{n % 4}"), n // 4 + 2)

            for g in range(3):
                turn(g)
            if banks_ready:
                banks_ready()
            chunk(xh, xl, KT, width, ready)

        def linear(src, source_ready=None, banks_ready=None):
            first_chunk(src, source_ready, banks_ready=banks_ready)
            for _ in range(3):
                chunk(xh, xl, KT)

        def columns(xhi=xh, xlo=xl, nkt=KT, turns=2, ready=None, width=512):
            with pe.Fori(0, turns) as g, t.loop(g, turns, unit=2 * len(units_of(nkt)), chunk=2, set0=1, set1=1):
                for c in range(2):
                    chunk(xhi, xlo, nkt, width, ready if c == 0 else None)

        pe.wait_ge(S("ident_in"), 16)

        def gain_columns(tiles):
            b = take_bank()
            for n in tiles:
                r = sum(x for _, x in GAIN_TILES[n])
                last = pe.transpose(TB(b)[:, n * 128:n * 128 + r], rows[0:r, n, :], ident[0:r, 0:r])
            last.then_inc(S("t_full"), 1)

        pe.wait_ge(S("rows_in0"), 16 * len(GAIN_TILES[0]))
        gain_columns((0,))

        pe.wait_ge(S("h_in"), 32)
        xpose(h, KT)
        ready = last_banks(8)
        pe.wait_ge(S("rows_in1"), 16 * sum(len(x) for x in GAIN_TILES[1:]))
        gain_columns((1, 2, 3))
        pe.wait_ge(S("band_in"), 16)
        with pe.Fori(0, WB) as g, t.loop(g, WB, unit=UNITS_POOL, chunk=6, set0=3, set1=3, bank=8, bank0=2, bank1=2,
                                         bank2=2, bank3=2):
            for c in range(3):
                chunk(xh, xl, KT, ready=ready if c == 0 else None)
                if c == 1:
                    before = [(f"mm_free{s}", t.at(f"set{s}", 1)) for s in range(2)]
            for name, v in before:
                pe.wait_ge(S(name), v)
            for k2 in range(4):
                b = take_bank()
                for k in range(2):
                    f = (2 * k2 + k) * 128
                    pe.matmul(TB(b)[:, k * 256:k * 256 + 256], ut[:, 0, f:f + 128],
                              band[:, bass.ds(g, 1), 0:256].rearrange("p o n -> p (o n)"), start=True, stop=False)
                    last = pe.matmul(TB(b)[:, k * 256 + 128:k * 256 + 256], ut[:, 1, f:f + 128],
                                     band[:, bass.ds(g, 1), 256:384].rearrange("p o n -> p (o n)"), start=False, stop=True)
                last.then_inc(S("t_full"), 1)
            chunk(xh, xl, KT)
            for b in range(4):
                pe.wait_ge(S(f"t_free{b}"), t.at(f"bank{b}", 1))
            before = []
            for c in range(2):
                s = chunk(plh, pll, 8)
                before.append((f"mm_free{s}", t.at(f"set{s}", 1)))
            for c in range(2):
                pe.wait_ge(S(before[c][0]), before[c][1])
                for k2 in range(2):
                    to_bank(mxs[:, c, :, :], k2 * 256)
        pe.wait_ge(S("ple_in0"), 16)
        xpose(ptok, 2)
        ready_ple = last_banks(1)
        columns(yh, yl, 32, ready=lambda k: pe.wait_ge(S("y_lo"), Y_PIECES.index(k) + 1) if k in Y_PIECES else None)

        def layer_end(n, ready_ple):
            for c in range(NCH):
                chunk(ph, pl, 2, ready=ready_ple if c == 0 else None)
            linear(h, lambda g: pe.wait_ge(S(f"h_post{n}"), g // 2 + 1))

        layer_end(0, ready_ple)
        first_chunk(h, lambda g: gated(pe, 0, g // 2 + 1), MIN_W)
        for _ in range(4):
            chunk(xh, xl, KT, MIN_W)
        pe.wait_ge(S("k_roped"), 1)
        b = take_bank()
        for tt in range(2):
            last = pe.transpose(TB(b)[0:64, tt * 128:tt * 128 + 128], kpe[:, tt, :], ident)
        last.then_inc(S("t_full"), 1)
        xpose(lat[:, :, 0:512], 4)
        ready_q = last_banks(2)
        for _ in range(2):
            chunk(xh, xl, KT, MIN_W)
        for c in range(6):
            chunk(qlh, qll, 4, ready=ready_q if c == 0 else None)
            if c == 0:
                xpose(lat[:, :, 512:1024], 4)
                ready_kv = last_banks(2)
        with pe.Fori(0, 2) as g, t.loop(g, 2, unit=8, chunk=4, set0=2, set1=2):
            for c in range(4):
                chunk(klh, kll, 4, ready=ready_kv if c == 0 else None)

        V = {"mla": lambda kb, hd: kv[:, kb, bass.ds(hd * 256 + 128, 128)],
             "a": lambda kb, hd: z[:, kb, bass.ds(hd * 64 + Z_VA, 64)],
             "b": lambda kb, hd: z[:, kb, bass.ds(hd * 64 + Z_VB, 64)],
             "cross": lambda kb, hd: kvm[:, kb, bass.ds(hd * 128 + 512, 128)]}

        def keep_warm(n):
            for _ in range(n):
                pe.matmul(ps[:, 3, 0:256], ident, causal, start=True, stop=True)

        def attention(parts, chunks):
            def scores(j, head):
                s, (at, hd) = slot(j, 1), head(1)
                if t.reg is None and t.n.get("at", 0) == AT[parts[0].name] and j == 1:
                    evacuated(pe, chunks)
                pe.wait_ge(S("at_done"), t.at("at", j))
                if at is FORGETTING:
                    pe.wait_ge(S("rows_staged"), t.at("at", j) - AT["b"])
                    pe.wait_ge(S("forget_k0" if t.reg is None else "forget_k1"), 32)
                pe.wait_ge(S("at_TE"), t.at("at", j))
                for q, (c0, nk) in enumerate(((0, at.keys0), (at.keys0, 256))):
                    dst, tok = ps[:, s, c0:c0 + nk], slice(q * 128, q * 128 + 128)
                    if at is FORGETTING:
                        row = hd + 4 if isinstance(hd, int) and hd < 4 else hd - 4
                        pe.matmul(dst, QP[s][0:2, tok], ck2[:, bass.ds(row, 1), 0:nk].rearrange("p o n -> p (o n)"),
                                  start=True, stop=False)
                    if at is MLA:
                        pe.matmul(dst, QP[s][0:ROPE, tok], kpt[:, 0:nk], start=True, stop=False)
                    last = pe.matmul(dst, QK[s][0:at.d, 0, tok], QK[s][0:at.d, 1, 0:nk],
                                     start=at is not FORGETTING and at is not MLA, stop=True)
                last.then_inc(S("at_S"), 1)
                if t.reg is None and t.n.get("at", 0) == AT[parts[0].name] and j < 3:
                    keep_warm(6)

            def output(j, head):
                s, (at, hd) = slot(j, 3), head(3)
                pe.wait_ge(S("at_PTE"), t.at("at", 4 + j - 2))
                n = 0
                for q, nb in enumerate((at.keys0 // 128, 2)):
                    for kb in range(nb):
                        last = pe.matmul(ps[:, s, q * at.dv:q * at.dv + at.dv], PTS[s][:, n, :], V[at.name](kb, hd),
                                         start=kb == 0, stop=kb == nb - 1)
                        n += 1
                last.then_inc(S("at_O"), 1)

            def step(j, head):
                if head(3):
                    s, (at, hd) = slot(j, 3), head(3)
                    pe.wait_ge(S("at_P"), t.at("at", j - 2))
                    for n in range((at.keys0 + 256) // 128):
                        last = pe.transpose(TB(s)[:, n * 128:n * 128 + 128], LG_[s][:, n * 128:n * 128 + 128], ident)
                    last.then_inc(S("at_PT"), 1)
                if head(0):
                    s, (at, hd) = slot(j, 0), head(0)
                    B, A = TB(s), ps[:, s, :]
                    if at is CROSS:
                        q_st, k_st = cqt[:, :, hd * 128:hd * 128 + 128], kvm[:, :, hd * 128:hd * 128 + 128]
                    else:
                        q_st, k_st = SQ[at.name][s], SK[at.name][s]
                        pe.wait_ge(S("at_stage"), t.at("at", 1 + j))
                    pe.wait_ge(S("at_PTE"), t.at("at", 1 + j))
                    if at is MLA:
                        pe.wait_ge(S("at_done"), t.at("at", 1 + j))
                    pe.sem_inc(S("heads_begun"), 1)
                    for tt in range(2):
                        pe.transpose(B[0:at.d, tt * 128:tt * 128 + 128], q_st[:, tt, 0:at.d], ident)
                        if at is MLA:
                            pe.transpose(A[0:ROPE, tt * 128:tt * 128 + 128], q_st[:, tt, NOPE:NOPE + ROPE], ident)
                        last = pe.transpose(B[0:at.d, 256 + tt * 128:384 + tt * 128], k_st[:, tt, 0:at.d], ident)
                    last.then_inc(S("at_T"), 1)
                if head(3) and parts == [MLA]:
                    output(j, head)
                if head(1):
                    scores(j, head)
                if head(3) and parts != [MLA]:
                    output(j, head)

            banks_read(pe, t)
            over_heads(pe, t, parts, step, behind=3)
            pe.wait_ge(S("at_done"), t.at("at", 4))

        evacuated(pe, "ukv")
        attention([MLA], "ukv")
        pe.wait_ge(S("ple_in1"), 16)
        xpose(ptok, 2)
        ready_ple = last_banks(1)
        linear(gm)
        layer_end(1, ready_ple)
        pe.wait_ge(S("mem_in"), 16)
        first_chunk(memt)
        chunk(xh, xl, KT)
        pe.wait_ge(S("rel_tables"), 16 * 3)
        pe.wait_ge(S("hyb_in"), 16 * 4)
        b = take_bank()
        pe.matmul(TB(b)[0:A_H, 0:384], reltab, relone, start=True, stop=True).then_inc(S("t_full"), 1)
        first_chunk(h, lambda g: gated(pe, 1, g // 2 + 1), Z_FIRST[0][1])
        chunk(xh, xl, KT, Z_FIRST[1][1])
        for n in range(A_H // 2):
            if n == 0:
                pe.wait_ge(S("rel_in"), 16 * A_H)
            b = take_bank()
            pe.matmul(TB(b), flip, relb[:, 2 * n:2 * n + 2, :].rearrange("p h n -> p (h n)"), start=True, stop=True).then_inc(S("t_full"), 1)
        chunk(xh, xl, KT, ZW)
        gate_columns_out(pe)
        b = take_bank()
        for tt in range(2):
            last = pe.transpose(TB(b)[0:16, tt * 128:tt * 128 + 128], z[:, tt, Z_GL:Z_GL + 16], ident)
        last.then_inc(S("t_full"), 1)
        chunk(xh, xl, KT, ZW)
        banks_read(pe, t)
        for tt in range(2):
            b = take_bank()
            pe.matmul(TB(b)[:, 0:C_KW], glt[:, tt * 128:tt * 128 + 128], w2a, start=True, stop=True).then_inc(S("t_full"), 1)
        chunk(xh, xl, KT, ZW)
        pe.wait_ge(S("log_forget"), 1)
        b = take_bank()
        pe.matmul(TB(b)[0:B_H, 0:256], lf8[:, 0, :], trio, start=True, stop=False)
        pe.matmul(TB(b)[0:B_H, 128:256], lf8[:, 1, :], trio[:, 0:128], start=False, stop=True).then_inc(S("t_full"), 1)
        chunk(xh, xl, KT, ZW)
        columns(turns=2, width=ZW)
        for _, width in Z_LAST:
            chunk(xh, xl, KT, width)
        attention([DILATED, FORGETTING], "z")
        for hd in range(C_H):
            b = take_bank()
            for m, c0 in enumerate((Z_QC, Z_KC)):
                for tt in range(2):
                    last = pe.transpose(TB(b)[0:C_DK, m * 256 + tt * 128:m * 256 + tt * 128 + 128],
                                        z[:, tt, c0 + hd * C_DK:c0 + hd * C_DK + C_DK], ident)
            last.then_inc(S("t_full"), 1)

        def decay_sums(lv):
            s = lv % 2
            if lv >= 2:
                pe.wait_ge(S("gla_e"), lv - 1)
            for hd in range(C_H):
                for tt in range(2):
                    o = ps[0:C_DK, 2 * s + hd // 2, (hd % 2) * 256 + tt * 128:(hd % 2) * 256 + tt * 128 + 128]
                    last = pe.matmul(o, lgd[:, tt, hd * C_DK:hd * C_DK + C_DK], dmat[:, tt if lv == 0 else lv + 1, :], start=True, stop=True)
            last.then_inc(S("gla_d"), 1)

        pe.wait_ge(S("gla_in"), 48)
        decay_sums(0)
        banks_read(pe, t)
        for tt in range(2):
            b = take_bank()
            tok = slice(tt * 128, tt * 128 + 128)
            for hd in range(C_H):
                last = pe.matmul(TB(b)[:, hd * 128:hd * 128 + 128], gk[:, hd, tok], gq[:, hd, tok], start=True, stop=True)
            last.then_inc(S("t_full"), 1)
        for lv in range(8):
            if lv < 7:
                decay_sums(lv + 1)
            pe.wait_ge(S("gla_s"), lv + 1)
            for tt in range(2 if lv else 1):
                b = take_bank()
                ktok = slice(tt * 128, tt * 128 + 128)
                qtok = ktok if lv else slice(128, 256)
                for hd in range(C_H):
                    last = pe.matmul(TB(b)[:, hd * 128:hd * 128 + 128], gks[lv % 2][:, hd, ktok], gqs[lv % 2][:, hd, qtok], start=True, stop=True)
                last.then_inc(S("t_full"), 1)
        banks_read(pe, t)
        pe.wait_ge(S("gla_e"), 8)
        for hd in range(C_H):
            v0, v1 = (z[:, tt, Z_VC + hd * C_DV:Z_VC + (hd + 1) * C_DV] for tt in range(2))
            pe.matmul(ps[:, hd, 0:C_DV], gat[:, 0, hd, :], v0, start=True, stop=True)
            pe.matmul(ps[:, hd, C_DV:2 * C_DV], gat[:, 2, hd, :], v0, start=True, stop=False)
            last = pe.matmul(ps[:, hd, C_DV:2 * C_DV], gat[:, 1, hd, :], v1, start=False, stop=True)
        last.then_inc(S("gla_o"), 1)
        linear(mix, lambda g: pe.wait_ge(S("mix_ready"), 1) if g == (A_W + B_W) // 256 else None,
               lambda: pe.wait_ge(S("gla_out_read"), 1))
        first_chunk(h, lambda g: chunk_out(pe, "out2", g // 2))
        evacuated(pe, "cq")
        attention([CROSS], "cq")
        xpose(cot, 4)
        ready = last_banks(2)
        for c in range(NCH):
            chunk(xh, xl, 4, ready=ready if c == 0 else None)
        first_chunk(h, lambda g: chunk_out(pe, "co", g // 2))

        def to_features(src, width, s, v):
            pe.wait_ge(S(f"mm_free{s}"), v)
            for k2 in range(2):
                to_bank(src, k2 * 256, min(2, width // 128 - 2 * k2))

        def gate_out(width):
            s = t.n["chunk"] % 2
            to_features(fgs, width, s, t.at(f"set{s}", 1))

        def up_turn(width, next_width):
            chunk(xh, xl, KT, width)
            gate_out(width)
            chunk(xh, xl, KT, next_width)
            s = t.n["chunk"] % 2
            to_features(fvs, width, s, t.at(f"set{s}", 1))

        with pe.Fori(0, 9) as g, t.loop(g, 9, unit=16, chunk=2, set0=1, set1=1, bank=4, bank0=1, bank1=1, bank2=1, bank3=1):
            up_turn(512, 512)
        up_turn(512, 384)
        chunk(xh, xl, KT, 384)
        gate_out(384)
        s = (t.n["chunk"] - 1) % 2
        value_out = s, t.at(f"set{s}", 1)

        def y_ready(k):
            if k == 8:
                to_features(fvs, 384, *value_out)
            if k % 8 == 0:
                pe.wait_ge(S("fy_lo"), k // 8 + 1)

        for c in range(NCH):
            chunk(fyh, fyl, FKT, ready=None if c else y_ready)
        assert t.n["unit"] == TOTAL_UNITS and t.n["chunk"] == CHUNKS_END["down"], t.n

    @block.scalar
    def _(act):
        t = Tally()

        def hi(k):
            for _ in range(k):
                u = t.n.get("unit", 0)
                if t.reg is not None or u < TOTAL_UNITS:
                    slot = u % RAW
                    full = 16 * (u // RAW + 1)
                    act.wait_ge(S(f"raw_full{slot}"), t.reg * (t.per["unit"] * 16 // RAW) + full if t.reg is not None else full)
                    act.wait_ge(S("w_used"), t.at("unit", 1))
                    act.activation(w_hi[:, u % RING, :], raw[:, slot, :], ACT.Copy).then_inc(S("w_hi"), 1)
                t.add("unit")

        def chunk(units):
            hi(units)
            s = t.n.get("chunk", 0) % 2
            t.add("chunk")
            act.wait_ge(S("w_used"), t.at("unit", RING - LEAD))
            return s

        def skip(units):
            hi(units)
            t.add("chunk")

        def xpose_hi(dst, nkt, g0=None):
            for g in range(nkt // 2):
                act.wait_ge(S("t_full"), t.at("bank", 1))
                bank = TB(t.n["bank"] % 4)
                if g0 is None:
                    last = act.activation(dst[:, 2 * g:2 * g + 2, :].rearrange("p k n -> p (k n)"), bank, ACT.Copy)
                else:
                    for k in range(2):
                        last = act.activation(dst[:, 2 * g + k, :], bank[:, k * 256:k * 256 + 256], ACT.Copy,
                                              scale=gain[:, g0 + 2 * g + k:g0 + 2 * g + k + 1])
                last.then_inc(S("x_hi"), 1)
                t.add("bank")

        def square(src, dst, scale=1.0, width=512):
            if t.n.get("junk"):
                act.wait_ge(S("junk_written"), t.at("junk"))
            act.activation(junk[:, 0:width], src, ACT.Square, scale=scale, accum_out=dst).then_inc(S("junk_written"), 1)
            t.add("junk")

        def first_chunk(g0=None, src=None, slot=None, between=None):
            for g in range(KT // 2):
                xpose_hi(xh[:, 2 * g:2 * g + 2, :], 2, None if g0 is None else g0 + 2 * g)
                hi(1)
                if between:
                    between(g)
                if src is not None:
                    c, tt = g // 2, g % 2
                    square(src[:, tt, c * 512:(c + 1) * 512], sums[:, slot, tt, c:c + 1])
            if src is not None:
                act.wait_ge(S("junk_written"), t.at("junk"))
                act.sem_inc(S(f"sums{slot}"), 1)
                root(slot)
            s = t.n["chunk"] % 2
            t.add("chunk")
            act.wait_ge(S("w_used"), t.at("unit", RING - LEAD))
            if src is not None:
                act.wait_ge(S(f"rstd{slot}"), 1)
            return s

        def root(slot):
            act.wait_ge(S(f"mean_square{slot}"), 1)
            act.activation(rt[:, slot, :], ms[:, slot, :], ACT.Sqrt).then_inc(S(f"root{slot}"), 1)

        def read_out(s, dst, func=ACT.Copy, scale=None, width=512):
            for tt in range(2):
                last = act.activation(dst(tt), MM(s, tt)[:, 0:width], func, scale=1.0 if scale is None else rstd[:, scale, tt:tt + 1])
            last.then_inc(S(f"mm_free{s}"), 1)


        def from_bank(dst, src, *more):
            b = t.n["bank"] % 4
            act.wait_ge(S("t_full"), t.at("bank", 1))
            last = act.activation(dst, TB(b)[src], ACT.Copy)
            if more:
                last = act.activation(more[0], TB(b)[src], ACT.Copy, scale=more[1])
            last.then_inc(S(f"t_free{b}"), 1)
            t.add("bank")

        def gain_columns(tiles):
            b = t.n.get("bank", 0) % 4
            act.wait_ge(S("t_full"), t.at("bank", 1))
            for n in tiles:
                r = sum(x for _, x in GAIN_TILES[n])
                last = act.activation(gain[:, n * 128:n * 128 + r], TB(b)[:, n * 128:n * 128 + r], ACT.Copy)
            last.then_inc(S(f"t_free{b}"), 1)
            t.add("bank")

        gain_columns((0,))
        act.wait_ge(S("t_free0"), 2)
        for g in range(KT // 2):
            xpose_hi(xh[:, 2 * g:2 * g + 2, :], 2, GAIN["pre0"] + 2 * g)
            if g in (2, 4, 6):
                hi(LEAD // 3)
        gain_columns((1, 2, 3))
        root(0)
        act.wait_ge(S("rstd0"), 1)
        with act.Fori(0, WB) as g, t.loop(g, WB, unit=UNITS_POOL, chunk=6, bank=8):
            for c in range(2):
                read_out(chunk(8), lambda tt: ut[:, tt, c * 512:c * 512 + 512], scale=0)
            for c in range(2):
                read_out(chunk(8), lambda tt: sg[:, tt, c * 512:c * 512 + 512], ACT.Silu, scale=0)
                if c == 0:
                    xpose_hi(plh, 8)
            for c in range(2):
                skip(4)
            for c in range(2):
                for k2 in range(2):
                    b = t.n["bank"] % 4
                    act.wait_ge(S("t_full"), t.at("bank", 1))
                    for k in range(2):
                        f = c * 4 + 2 * k2 + k
                        last = act.activation(y32[:, bass.ds(g * 8 + f, 1), :].rearrange("p o n -> p (o n)"),
                                              TB(b)[:, k * 256:k * 256 + 256], ACT.Copy,
                                              scale=gain[:, bass.ds(g * 8 + (GAIN["pool_scale"] + f), 1)])
                    last.then_inc(S(f"t_free{b}"), 1)
                    t.add("bank")
        banks_read(act, t)
        products(act, "pool")
        for n in range(6):
            k = slice(Y_PIECES[n], Y_PIECES[n + 1])
            act.activation(yh[:, k, :], y32[:, k, :], ACT.Copy).then_inc(S("y_hi"), 1)
            if n >= 3:
                hi(1)

        def mixer_chunk(s, slot, c):
            for tt in range(2):
                square(MM(s, tt), sums[:, slot, tt, c:c + 1])
            read_out(s, lambda tt: outt[:, tt, c * 512:(c + 1) * 512])

        def layer_end(n, slot):
            root(slot)
            for c in range(NCH):
                read_out(chunk(1), lambda tt: proj[:, tt, c * 512:(c + 1) * 512])
            for c in range(NCH):
                s = first_chunk(GAIN[f"ple{n}"], h, slot + 1) if c == 0 else chunk(8)
                act.wait_ge(S("gated"), 4 * n + c + 1)
                read_out(s, lambda tt: sig[:, c % 2, tt, :], ACT.Sigmoid, scale=slot + 1)

        xpose_hi(ph, 2)
        for c in range(NCH):
            mixer_chunk(chunk(16 if c else 13), 1, c)
            if c == 0:
                act.wait_ge(S("rope_reduced"), 2)
                act.activation(rc_sin, ang, ACT.Sin)
                act.activation(rc_cos, red, ACT.Sin).then_inc(S("rope_tables"), 1)
        layer_end(0, 1)
        s = first_chunk(GAIN["pre1"], h, 3)

        def latent(s, tt, c0, c1, col, slot, part):
            square(MM(s, tt)[:, c0:c1], sums[:, slot, tt, part:part + 1], rstd[:, 3, tt:tt + 1], c1 - c0)
            return act.activation(lat[:, tt, col:col + c1 - c0], MM(s, tt)[:, c0:c1], ACT.Copy, scale=rstd[:, 3, tt:tt + 1])

        for tt in range(2):
            last = latent(s, tt, 0, MIN_W, 0, 4, 0)
        last.then_inc(S(f"mm_free{s}"), 1)
        s = chunk(8)
        more = Q_RANK - MIN_W
        for tt in range(2):
            latent(s, tt, 0, more, MIN_W, 4, 1)
            last = latent(s, tt, more, MIN_W, Q_RANK, 5, 0)
        last.then_inc(S(f"mm_free{s}"), 1)
        s = chunk(8)
        more = Q_RANK + KV_RANK - 2 * MIN_W
        for tt in range(2):
            latent(s, tt, 0, more, 2 * MIN_W, 5, 1)
            act.activation(kpe[:, tt, :], MM(s, tt)[:, more:more + ROPE], ACT.Copy, scale=rstd[:, 3, tt:tt + 1])
            last = act.activation(gm[:, tt, 0:MIN_W - more - ROPE], MM(s, tt)[:, more + ROPE:MIN_W], ACT.Silu, scale=rstd[:, 3, tt:tt + 1])
        last.then_inc(S(f"mm_free{s}"), 1)
        for c in range(4):
            if c == 1:
                root(4)
                root(5)
            if c == 2:
                hi(2)
                from_bank(kpt, (slice(0, 64), slice(0, 256)))
                xpose_hi(qlh, 4, GAIN["q_norm"])
            col = c * MIN_W + MIN_W - more - ROPE
            read_out(chunk(6 if c == 2 else 8), lambda tt: gm[:, tt, col:col + MIN_W], ACT.Silu, scale=3, width=MIN_W)
        act.wait_ge(S("rstd4"), 1)
        act.wait_ge(S("rstd5"), 1)
        for c in range(6):
            read_out(chunk(2), lambda tt: qt[:, tt, c * 512:(c + 1) * 512], scale=4)
            if c == 0:
                xpose_hi(klh, 4, GAIN["kv_norm"])
        with act.Fori(0, 2) as g, t.loop(g, 2, unit=8, chunk=4):
            for c in range(4):
                read_out(chunk(2), lambda tt: kv[:, tt, bass.ds(g * 2048 + c * 512, 512)], scale=5)

        def attention(parts):
            def step(j, head):
                if head(3):
                    s, (at, hd) = slot(j, 3), head(3)
                    act.wait_ge(S("at_PT"), t.at("at", j - 2))
                    act.activation(PTS[s].rearrange("p k n -> p (k n)")[:, 0:at.keys0 + 256], TB(s)[:, 0:at.keys0 + 256], ACT.Copy)\
                       .then_inc(S("at_PTE"), 1)
                if head(0):
                    s, (at, hd) = slot(j, 0), head(0)
                    act.wait_ge(S("at_T"), t.at("at", 1 + j))
                    if at is MLA:
                        act.activation(QP[s], ps[0:ROPE, s, 0:256], ACT.Copy)
                    act.activation(QK[s][0:at.d], TB(s)[0:at.d, :].rearrange("p (m n) -> p m n", m=2), ACT.Copy).then_inc(S("at_TE"), 1)
                if head(2):
                    s, (at, hd) = slot(j, 2), head(2)
                    act.wait_ge(S("at_L"), t.at("at", j - 1))
                    for q, (c0, n) in enumerate(((0, at.keys0), (at.keys0, 256))):
                        last = act.activation(LG_[s][:, c0:c0 + n], LG_[s][:, c0:c0 + n], ACT.Exp, bias=nmx[:, s, q:q + 1],
                                              accum_out=psm[:, s, q:q + 1])
                    last.then_inc(S("at_P"), 1)

            over_heads(act, t, parts, step, behind=3)

        attention([MLA])
        heads_done(act, "a")
        xpose_hi(ph, 2)
        for c in range(NCH):
            mixer_chunk(chunk(8) if c else first_chunk(), 6, c)
        layer_end(1, 6)
        for c in range(2):
            read_out(chunk(8) if c else first_chunk(GAIN["mem"], memt, 8), lambda tt: kvm[:, tt, c * 512:(c + 1) * 512], scale=8)
        from_bank(relrow, (slice(0, A_H), slice(0, 384)))
        banks_read(act, t)
        act.dma_start(rel_scratch, relrow).then_inc(S("rel_out"), 16)

        def z_out(s, col, width):
            read_out(s, lambda tt: z[:, tt, bass.ds(col, width)], scale=9, width=width)

        z_out(first_chunk(GAIN["mix"], h, 9), *Z_FIRST[0])
        z_out(chunk(8), *Z_FIRST[1])
        for n in range(A_H // 2):
            from_bank(relb[:, 2 * n:2 * n + 2, :].rearrange("p h n -> p (h n)"), (slice(0, 128), slice(0, 512)))
            if n % 2:
                hi(1)
        z_out(chunk(5), *Z_FIRST[2])
        act.wait_ge(S("ones_set"), 2)
        from_bank(glt[0:16, :], (slice(0, 16), slice(0, 256)))
        z_out(chunk(8), *Z_FIRST[3])
        t.add("bank", 2)
        hi(3)
        act.wait_ge(S("gate_abs"), 1)
        act.activation(la, la, ACT.Exp, scale=-1.0).then_inc(S("gate_exp"), 1)
        act.wait_ge(S("gate_exp"), 1)
        act.activation(la, la, ACT.Ln, bias=1.0).then_inc(S("gate_exp"), 1)
        z_out(chunk(5), *Z_FIRST[4])
        from_bank(crow, (slice(0, B_H), slice(0, 256)), ncrow, -1.0)
        z_out(chunk(8), *Z_FIRST[5])
        with act.Fori(0, 2) as g, t.loop(g, 2, unit=16, chunk=2):
            for c in range(2):
                z_out(chunk(8), g * 2 * ZW + (c + 4) * ZW, ZW)
        for col, width in Z_LAST:
            z_out(chunk(8), col, width)
        attention([DILATED, FORGETTING])
        heads_done(act, "cross")
        for hd in range(C_H):
            act.wait_ge(S("t_full"), t.at("bank", 1))
            b = t.n["bank"] % 4
            act.activation(gq[:, hd, :], TB(b)[0:C_DK, 0:256], ACT.Copy, scale=C_DK ** -0.5)
            act.activation(gk[:, hd, :], TB(b)[0:C_DK, 256:512], ACT.Copy).then_inc(S(f"t_free{b}"), 1)
            t.add("bank")
        for lv in range(8):
            act.wait_ge(S("gla_d"), lv + 1)
            if lv >= 2:
                act.wait_ge(S("gla_s"), lv - 1)
            s = lv % 2
            act.activation(ge[s], ps[0:C_DK, 2 * s:2 * s + 2, :].rearrange("p b (h n) -> p (b h) n", h=2), ACT.Exp, scale=1.0 / 16.0)\
               .then_inc(S("gla_e"), 1)
        for tt in range(2):
            last = act.activation(mix[:, tt, A_W + B_W:D], z[:, tt, Z_RC:Z_RC + C_VW], ACT.Silu)
        last.then_inc(S("rc_silu"), 1)
        t.add("bank", 2 + 1 + 2 * 7)

        def gla_norm(g):
            if g == 0:
                act.wait_ge(S("gla_out_read"), 1)
                for tt in range(2):
                    act.activation(osq[:, tt], oc[:, tt], ACT.Square).then_inc(S("gla_squares"), 1)
            if g == 1:
                act.wait_ge(S("gla_ms"), 1)
                act.activation(cst[:, 1, :], cst[:, 0, :], ACT.Sqrt).then_inc(S("gla_root"), 1)

        act.wait_ge(S("gla_o"), 1)
        first_chunk(between=gla_norm)
        for c in range(1, NCH):
            skip(8)
        products(act, "out2")
        read_out(first_chunk(GAIN["cross"], h, 10), lambda tt: cqt[:, tt, :], scale=10)
        attention([CROSS])
        heads_done(act, "end")
        xpose_hi(xh, 4)
        for c in range(NCH):
            skip(2)
        products(act, "co")
        read_out(first_chunk(GAIN["ffn"], h, 11), lambda tt: fgs[:, tt, :], scale=11)

        def silu_conv(width):
            act.wait_ge(S("conv_done"), t.at("conv", 1))
            act.activation(fcv[:, 0:width // 128, :], fcv[:, 0:width // 128, :], ACT.Silu).then_inc(S("conv_silu"), 1)
            t.add("conv")
            t.add("bank", 4)

        def up_turn(width, next_width, units=8):
            skip(units)
            hi(4)
            silu_conv(width)
            read_out(chunk(4), lambda tt: fgs[:, tt, 0:next_width], scale=11, width=next_width)

        with act.Fori(0, 9) as g, t.loop(g, 9, unit=16, chunk=2, conv=1, bank=4):
            up_turn(512, 512)

        def square_out(c):
            chunk_out(act, "down", c)
            for tt in range(2):
                square(h[:, tt, c * 512:(c + 1) * 512], sums[:, 12, tt, c:c + 1])

        def y_hi(n):
            k = slice(8 * n, min(8 * n + 8, FKT))
            act.wait_ge(S("y_pairs"), 2 * n + 2 if n < 4 else 11)
            act.activation(fyh[:, k, :], fy[:, k, :], ACT.Copy).then_inc(S("fy_hi"), 1)

        for n in range(2):
            y_hi(n)
            hi(2)
        up_turn(512, 384, 4)
        for n in range(2, 4):
            y_hi(n)
            hi(2)
        hi(4)
        t.add("chunk")
        hi(3)
        silu_conv(384)
        for n in range(4, 6):
            y_hi(n)
        for c in range(NCH):
            skip(len(units_of(FKT)) - (0 if c else 3))
            if c:
                square_out(c - 1)
        square_out(NCH - 1)
        act.wait_ge(S("junk_written"), t.at("junk"))
        act.sem_inc(S("sums12"), 1)
        root(12)

    @block.vector
    def _(dve):
        t = Tally()
        dve.sem_inc(S("w_lo"), RAW)
        for name in ("mm_free0", "mm_free1", "t_free0", "t_free1", "t_free2", "t_free3"):
            dve.sem_inc(S(name), 1)
        dve.sem_inc(S("gated"), 2)
        dve.sem_inc(S("at_done"), 4)
        dve.sem_inc(S("at_PTE"), 4)

        def link(ins):
            ins.then_inc(S("dve_chain"), 1)
            t.add("chain")
            dve.wait_ge(S("dve_chain"), t.at("chain"))

        def lo(k):
            for _ in range(k):
                u = t.n.get("unit", 0)
                if t.reg is not None or u < TOTAL_UNITS:
                    dve.wait_ge(S("w_hi"), t.at("unit", 1))
                    dve.tensor_tensor(w_lo[:, u % RING, :], raw[:, u % RAW, :], w_hi[:, u % RING, :].bitcast(F32), ALU.subtract)\
                       .then_inc(S("w_lo"), 1)
                t.add("unit")

        def chunk(units):
            lo(units)
            s = t.n.get("chunk", 0) % 2
            t.add("chunk")
            dve.wait_ge(S("w_used"), t.at("unit", RING - LEAD))
            return s

        def skip(units):
            lo(units)
            t.add("chunk")

        def xpose_lo(dst, hi_part, nkt, g0=None):
            for g in range(nkt // 2):
                dve.wait_ge(S("x_hi"), t.at("xh", 1))
                b = t.n["bank"] % 4
                if g0 is None:
                    k = slice(2 * g, 2 * g + 2)
                    last = dve.tensor_tensor(dst[:, k, :].rearrange("p k n -> p (k n)"), TB(b),
                                             hi_part[:, k, :].rearrange("p k n -> p (k n)").bitcast(F32), ALU.subtract)
                else:
                    for k in range(2):
                        c = g0 + 2 * g + k
                        last = dve.scalar_tensor_tensor(dst[:, 2 * g + k, :], TB(b)[:, k * 256:k * 256 + 256], gain[:, c:c + 1],
                                                        hi_part[:, 2 * g + k, :].bitcast(F32), ALU.mult, ALU.subtract)
                last.then_inc(S(f"t_free{b}"), 1)
                t.add("bank")
                t.add("xh")

        def first_chunk(g0=None, slot=None, between=None):
            for g in range(KT // 2):
                k = slice(2 * g, 2 * g + 2)
                xpose_lo(xl[:, k, :], xh[:, k, :], 2, None if g0 is None else g0 + 2 * g)
                lo(1)
                if between:
                    between(g)
            if slot is not None:
                norm(slot)
            s = t.n["chunk"] % 2
            t.add("chunk")
            return s

        def mean(slot, width, cols=NCH):
            link(dve.reduce_sum(ms[:, slot, :], sums[:, slot, :, 0:cols], AXX))
            dve.tensor_scalar(ms[:, slot, :], ms[:, slot, :], 1.0 / width, EPS, ALU.mult, ALU.add).then_inc(S(f"mean_square{slot}"), 1)

        def inverse(slot):
            dve.wait_ge(S(f"root{slot}"), 1)
            dve.reciprocal(rstd[:, slot, :], rt[:, slot, :]).then_inc(S(f"rstd{slot}"), 1)
            dve.wait_ge(S(f"rstd{slot}"), 1)

        def norm(slot, width=D):
            dve.wait_ge(S(f"sums{slot}"), 1)
            mean(slot, width)
            inverse(slot)

        dve.wait_ge(S("pos_in"), 32)
        link(dve.tensor_copy(posf, posi))
        for tt in range(2):
            last = dve.tensor_scalar(ang[:, tt, :], freqs, posf[:, tt:tt + 1], None, ALU.mult)
        link(last)
        ROUND = 1.5 * 2.0 ** 23
        PI = float(np.float32(3.1415925))
        link(dve.tensor_scalar(turns_, ang, 1.0 / (2 * math.pi), None, ALU.mult))
        link(dve.tensor_scalar(turns_, turns_, ROUND, ROUND, ALU.add, ALU.subtract))
        link(dve.scalar_tensor_tensor(ang, turns_, -6.28125, ang, ALU.mult, ALU.add))
        link(dve.scalar_tensor_tensor(ang, turns_, -(2 * math.pi - 6.28125), ang, ALU.mult, ALU.add))
        link(dve.tensor_scalar(red, ang, math.pi / 2, math.pi, ALU.add, ALU.is_gt))
        link(dve.tensor_scalar(red, red, -2 * math.pi, math.pi / 2, ALU.mult, ALU.add))
        link(dve.tensor_tensor(red, red, ang, ALU.add))
        dve.tensor_scalar(red, red, PI, -PI, ALU.min, ALU.max).then_inc(S("rope_reduced"), 1)
        dve.tensor_scalar(ang, ang, PI, -PI, ALU.min, ALU.max).then_inc(S("rope_reduced"), 1)

        t.add("bank")
        dve.wait_ge(S("t_free0"), 2)

        def x_sums(c):
            dve.wait_ge(S("x_squared"), c + 1)
            return dve.reduce_sum(sums[:, 0, :, c:c + 1], hsq[:, :, c * 512:(c + 1) * 512], AXX)

        for g in range(KT // 2):
            xpose_lo(xl[:, 2 * g:2 * g + 2, :], xh[:, 2 * g:2 * g + 2, :], 2, GAIN["pre0"] + 2 * g)
            if g in (2, 4, 6):
                lo(LEAD // 3)
            if g in (3, 5):
                x_sums(g // 2 - 1)
        t.add("bank")
        x_sums(2)
        link(x_sums(3))
        mean(0, D)
        inverse(0)
        with dve.Fori(0, WB) as g, t.loop(g, WB, unit=UNITS_POOL, chunk=6, bank=8, xh=4):
            for c in range(3):
                skip(8)
            xpose_lo(pll, plh, 8)
            skip(8)
            for c in range(2):
                s = chunk(4)
                if c == 0:
                    for k in range(2):
                        dve.wait_ge(S(f"mm_free{k}"), t.reg * 3 + (t.n["chunk"] - 1) // 2 + 1)
                for tt in range(2):
                    last = dve.tensor_tensor(mxs[:, c, tt, :], MM(s, tt), sg[:, tt, c * 512:(c + 1) * 512], ALU.mult)
                last.then_inc(S(f"mm_free{s}"), 1)
            t.add("bank", 4)
        for n in range(6):
            k = slice(Y_PIECES[n], Y_PIECES[n + 1])
            dve.wait_ge(S("y_hi"), n + 1)
            dve.tensor_tensor(yl[:, k, :], y32[:, k, :], yh[:, k, :].bitcast(F32), ALU.subtract).then_inc(S("y_lo"), 1)
            if n >= 3:
                lo(1)

        def columns(turns=2, units=8):
            with dve.Fori(0, turns) as g, t.loop(g, turns, unit=2 * units, chunk=2):
                for c in range(2):
                    skip(units)

        def layer_end(n, slot, mixer):
            evacuated(dve, mixer)
            mean(slot, D)
            inverse(slot)

            def update(c):
                cols = slice(c * 512, c * 512 + 512)
                dve.wait_ge(S("post_gained"), 4 * n + c + 1)
                for tt in range(2):
                    last = dve.scalar_tensor_tensor(h[:, tt, cols], outt[:, tt, cols], rstd[:, slot, tt:tt + 1], h[:, tt, cols],
                                                    ALU.mult, ALU.add)
                last.then_inc(S(f"h_post{n}"), 1)

            update(0)
            skip(1)
            update(1)
            for c in range(3):
                skip(1)
            first_chunk(GAIN[f"ple{n}"], slot + 1, lambda g: update(g + 2) if g < 2 else None)
            evacuated(dve, f"proj{n}")
            for c in range(NCH):
                if c:
                    lo(8)
                    t.add("chunk")
                dve.wait_ge(S("w_used"), t.at("unit", RING - LEAD))
                k = t.n["chunk"] - 1
                dve.wait_ge(S(f"mm_free{k % 2}"), k // 2 + 2)
                if c < NCH - 1:
                    gate_times_proj(c)
                    add_gated(c)

        def gate_times_proj(c):
            for tt in range(2):
                last = dve.tensor_tensor(sig[:, c % 2, tt, :], sig[:, c % 2, tt, :], proj[:, tt, c * 512:(c + 1) * 512], ALU.mult)
            link(last)

        def add_gated(c):
            for tt in range(2):
                hc = h[:, tt, c * 512:(c + 1) * 512]
                last = dve.tensor_tensor(hc, hc, sig[:, c % 2, tt, :], ALU.add)
            last.then_inc(S("gated"), 1)

        def last_gated(g):
            if g == 0:
                gate_times_proj(NCH - 1)
            if g == 1:
                add_gated(NCH - 1)

        def rope(x1, x2, cos, sin, tmp):
            link_all = [dve.tensor_tensor(tmp[0], x1, cos, ALU.mult), dve.tensor_tensor(tmp[1], x2, sin, ALU.mult),
                        dve.tensor_tensor(tmp[2], x2, cos, ALU.mult), dve.tensor_tensor(tmp[3], x1, sin, ALU.mult)]
            link(link_all[-1])
            dve.tensor_tensor(x1, tmp[0], tmp[1], ALU.subtract)
            return dve.tensor_tensor(x2, tmp[2], tmp[3], ALU.add)

        def early_latents():
            chunk_out(dve, "mla_in", 1, of=7)
            chunk_out(dve, "mla_in", 2, of=7)
            for c in range(2):
                mean(4 + c, Q_RANK, 2)
            inverse(4)
            inverse(5)
            dve.wait_ge(S("rope_tables"), 1)
            rope(kpe[:, :, 0:32], kpe[:, :, 32:64], rc_cos, rc_sin, krope).then_inc(S("k_roped"), 1)
            t.add("bank")

        xpose_lo(pl, ph, 2)
        for c in range(NCH):
            skip(16 if c else 13)
        layer_end(0, 1, "pool_out")
        first_chunk(GAIN["pre1"], 3, last_gated)
        for c in range(1, 7):
            skip(8)
            if c == 3:
                early_latents()
            if c == 4:
                xpose_lo(qll, qlh, 4, GAIN["q_norm"])
        evacuated(dve, "mla_in")
        for c in range(6):
            skip(2)
            if c == 0:
                xpose_lo(kll, klh, 4, GAIN["kv_norm"])
        skip(2)
        skip(2)
        evacuated(dve, "uq")
        q4 = qt.rearrange("p t (h e) -> p t h e", e=192)
        for tt in range(2):
            cos, sin = (x[:, tt, :].unsqueeze(1).broadcast_to([128, HEADS, 32]) for x in (rc_cos, rc_sin))
            last = rope(q4[:, tt, :, 128:160], q4[:, tt, :, 160:192], cos, sin, [x[:, tt] for x in (ra, rb, rc_, rd)])
            last.then_inc(S("q_roped"), 1)
            skip(2)
            skip(2)
        skip(2)
        skip(2)

        def attention(parts):
            def logits(j, head):
                s, (at, hd) = slot(j, 1), head(1)
                dve.wait_ge(S("at_S"), t.at("at", j))
                scale = (NOPE + ROPE if at is MLA else at.d) ** -0.5
                for q, (c0, nk) in enumerate(((0, at.keys0), (at.keys0, 256))):
                    src, dst = ps[:, s, c0:c0 + nk], LG_[s][:, c0:c0 + nk]
                    if at is CROSS:
                        last = dve.tensor_scalar(dst, src, scale, None, ALU.mult)
                    else:
                        mask = relb[:, bass.ds(hd, 1), :].rearrange("p o n -> p (o n)") if at is DILATED else causal
                        last = dve.scalar_tensor_tensor(dst, src, scale, mask[:, 256 - nk:256], ALU.mult, ALU.add)
                link(last)
                for q, (c0, nk) in enumerate(((0, at.keys0), (at.keys0, 256))):
                    last = dve.reduce_max(nmx[:, s, q:q + 1], LG_[s][:, c0:c0 + nk], AXX, negate=True)
                last.then_inc(S("at_L"), 1)

            def output(j, head):
                s, (at, hd) = slot(j, 3), head(3)
                dve.wait_ge(S("at_O"), t.at("at", j - 2))
                link(dve.reciprocal(prc[:, s, :], psm[:, s, :]))
                for q in range(2):
                    src, scale = ps[:, s, q * at.dv:q * at.dv + at.dv], prc[:, s, q:q + 1]
                    if at is MLA:
                        gate = gm[:, q, bass.ds(hd * VD, VD)]
                        last = dve.scalar_tensor_tensor(gate, src, scale, gate, ALU.mult, ALU.mult)
                    else:
                        dst, col = {"a": (mix, 0), "b": (mix, A_W), "cross": (cot, 0)}[at.name]
                        last = dve.tensor_scalar(dst[:, q, bass.ds(hd * at.dv + col, at.dv)], src, scale, None, ALU.mult)
                last.then_inc(S("at_done"), 1)

            def step(j, head):
                if head(3) and parts == [MLA]:
                    output(j, head)
                if head(1):
                    logits(j, head)
                if head(3) and parts != [MLA]:
                    output(j, head)

            over_heads(dve, t, parts, step, behind=3, chain=8)

        dve.wait_ge(S("causal_in"), 16)
        attention([MLA])
        xpose_lo(pl, ph, 2)
        first_chunk()
        for c in range(1, NCH):
            skip(8)
        layer_end(1, 6, "mla_out")
        first_chunk(GAIN["mem"], 8, last_gated)
        skip(8)
        t.add("bank")
        first_chunk(GAIN["mix"], 9)
        skip(8)
        t.add("bank", A_H // 2)
        skip(8)
        t.add("bank")
        skip(8)
        gate_columns_out(dve)
        link(dve.tensor_tensor(la[:, :, C_KW:C_KW + B_H], z[:, :, Z_FL:Z_FL + B_H], fbias.unsqueeze(1).broadcast_to([128, 2, B_H]), ALU.add))
        for tt in range(2):
            dve.wait_ge(S("t_full"), t.at("bank", 1))
            b = t.n["bank"] % 4
            dve.tensor_copy(la[:, tt, 0:C_KW], TB(b)[:, 0:C_KW]).then_inc(S(f"t_free{b}"), 1)
            t.add("bank")
        banks_read(dve, t)
        link(dve.tensor_scalar(lm, la, 0.0, None, ALU.min))
        dve.scalar_tensor_tensor(la, la, 0.0, lm, ALU.max, ALU.subtract).then_inc(S("gate_abs"), 1)
        lo(3)
        dve.wait_ge(S("gate_exp"), 2)
        link(dve.tensor_tensor(lgd, lm, la, ALU.subtract))
        dve.tensor_scalar(lf8, lgd[:, :, C_KW:C_KW + B_H], 8.0, None, ALU.mult).then_inc(S("log_forget"), 1)
        skip(5)
        t.add("bank")
        skip(8)
        columns(2)
        for _ in Z_LAST:
            skip(8)
        evacuated(dve, "z")
        products(dve, "z")
        banks_read(dve, t)
        attention([DILATED, FORGETTING])
        t.add("bank", C_H)
        dve.wait_ge(S("gla_in"), 48)

        def attn_part(tt, lv, first=False):
            dve.wait_ge(S("t_full"), t.at("bank", 1))
            b = t.n["bank"] % 4
            src = TB(b).rearrange("p (h n) -> p h n", h=C_H)
            if first:
                ins = dve.tensor_tensor(gat[:, tt], src, gmask[:, 0, :].unsqueeze(1).broadcast_to([128, C_H, 128]), ALU.mult)
            elif lv == 0:
                ins = dve.tensor_copy(gat[:, 2], src)
            else:
                ins = dve.copy_predicated(gat[:, tt], gmask[:, lv, :].bitcast(I32).unsqueeze(1).broadcast_to([128, C_H, 128]), src)
            ins.then_inc(S(f"t_free{b}"), 1)
            t.add("bank")

        for tt in range(2):
            attn_part(tt, 0, True)
        banks_read(dve, t)

        def decayed(lv):
            dve.wait_ge(S("gla_e"), lv + 1)
            dve.tensor_tensor(gqs[lv % 2], gq, ge[lv % 2], ALU.mult)
            dve.tensor_tensor(gks[lv % 2], gk, ge[lv % 2], ALU.mult).then_inc(S("gla_s"), 1)

        decayed(0)
        for lv in range(8):
            if lv < 7:
                decayed(lv + 1)
            banks_read(dve, t)
            for tt in range(2 if lv else 1):
                attn_part(tt, lv)
        dve.wait_ge(S("gla_o"), 1)
        for tt in range(2):
            last = dve.tensor_copy(oc[:, tt], ps[:, 0:4, tt * C_DV:(tt + 1) * C_DV])
        link(last)
        dve.sem_inc(S("gla_out_read"), 1)

        def gla_norm(g):
            if g == 0:
                for tt in range(2):
                    dve.wait_ge(S("gla_squares"), tt + 1)
                    last = dve.reduce_sum(cst[:, 0, tt * C_H:tt * C_H + C_H], osq[:, tt], AXX)
                link(last)
                dve.tensor_scalar(cst[:, 0, :], cst[:, 0, :], 1.0 / C_DV, EPS, ALU.mult, ALU.add).then_inc(S("gla_ms"), 1)
            if g == 1:
                dve.wait_ge(S("gla_root"), 1)
                link(dve.reciprocal(cst[:, 2, :], cst[:, 1, :]))
                dve.wait_ge(S("rc_gate"), 1)
                for tt in range(2):
                    for hd in range(C_H):
                        n = tt * C_H + hd
                        mc = mix[:, tt, A_W + B_W + hd * C_DV:A_W + B_W + (hd + 1) * C_DV]
                        last = dve.scalar_tensor_tensor(mc, oc[:, tt, hd, :], cst[:, 2, n:n + 1], mc, ALU.mult, ALU.mult)
                last.then_inc(S("mix_ready"), 1)

        def add_chunk(s, col):
            for tt in range(2):
                hc = h[:, tt, bass.ds(col, 512)]
                last = dve.tensor_tensor(hc, hc, MM(s, tt), ALU.add)
            last.then_inc(S(f"mm_free{s}"), 1)

        s = first_chunk(between=gla_norm)
        dve.wait_ge(S("w_used"), t.at("unit", RING - LEAD))
        add_chunk(s, 0)
        for c in range(1, NCH):
            add_chunk(chunk(8), c * 512)
        first_chunk(GAIN["cross"], 10)
        attention([CROSS])
        xpose_lo(xl, xh, 4)
        for c in range(NCH):
            add_chunk(chunk(2), c * 512)
        first_chunk(GAIN["ffn"], 11)

        def up_turn(width, tile, then, units=8):
            nt = width // 128
            s = chunk(units)
            for tt in range(2):
                last = dve.tensor_scalar(fvs[:, tt, 0:width], MM(s, tt)[:, 0:width], rstd[:, 11, tt:tt + 1], None, ALU.mult)
            last.then_inc(S(f"mm_free{s}"), 1)
            lo(min(then, 1))
            b0 = t.n["bank"] % 4
            bank = lambda k: TB((b0 + k // 2) % 4)[:, (k % 2) * 256:(k % 2) * 256 + 256]
            col = lambda name, k: gain[:, bass.ds(tile + (GAIN[name] + k), 1)]
            dve.wait_ge(S("t_full"), t.at("bank", 2))
            for k in range(nt):
                last = dve.tensor_scalar(fcv[:, k, :], bank(k), col("conv_w2", k), col("conv_b", k), ALU.mult, ALU.add)
            link(last)
            lo(min(then, 1))
            for k in range(nt):
                last = dve.scalar_tensor_tensor(fcv[:, k, 1:T], bank(k)[:, 0:T - 1], col("conv_w1", k), fcv[:, k, 1:T], ALU.mult, ALU.add)
            link(last)
            lo(min(then, 1))
            for k in range(nt):
                last = dve.scalar_tensor_tensor(fcv[:, k, 2:T], bank(k)[:, 0:T - 2], col("conv_w0", k), fcv[:, k, 2:T], ALU.mult, ALU.add)
                if k == 1:
                    last.then_inc(S(f"t_free{b0}"), 1)
            link(last)
            dve.sem_inc(S(f"t_free{(b0 + 1) % 4}"), 1)
            dve.sem_inc(S("conv_done"), 1)
            t.add("bank", 2)
            t.add("conv")
            if then > 3:
                skip(then - 3)
            dve.wait_ge(S("t_full"), t.at("bank", 2))
            dve.wait_ge(S("conv_silu"), t.at("conv"))
            for k2 in range(2):
                n = min(2, nt - 2 * k2)
                b = t.n["bank"] % 4
                ins = dve.tensor_tensor(fy[:, bass.ds(tile + 2 * k2, n), :], fcv[:, 2 * k2:2 * k2 + n, :],
                                        TB(b)[:, 0:n * 256].rearrange("p (k n) -> p k n", n=256), ALU.mult)
                ins.then_inc(S("y_pairs") if k2 else S(f"t_free{b}"), 1)
                t.add("bank")
            dve.wait_ge(S("y_pairs"), t.at("pair", 1))
            dve.sem_inc(S(f"t_free{b}"), 1)
            t.add("pair")

        with dve.Fori(0, 9) as g, t.loop(g, 9, unit=16, chunk=2, chain=3, bank=4, conv=1, pair=1):
            up_turn(512, g * 4, 8)
        def y_lo(n):
            k = slice(8 * n, min(8 * n + 8, FKT))
            dve.wait_ge(S("fy_hi"), n + 1)
            dve.tensor_tensor(fyl[:, k, :], fy[:, k, :], fyh[:, k, :].bitcast(F32), ALU.subtract).then_inc(S("fy_lo"), 1)

        for n in range(2):
            y_lo(n)
            lo(2)
        up_turn(512, 36, 8, units=4)
        for n in range(2, 4):
            y_lo(n)
            lo(2)
        lo(4)
        up_turn(384, 40, 3, units=0)
        for n in range(4, 6):
            y_lo(n)
        for c in range(NCH):
            add_chunk(chunk(len(units_of(FKT)) - (0 if c else 3)), c * 512)
        norm(12)
        dve.wait_ge(S("final_gained"), NCH)
        for tt in range(2):
            for c in range(2):
                cols = slice(c * 1024, c * 1024 + 1024)
                dve.tensor_scalar(fout[:, tt, cols], fout[:, tt, cols], rstd[:, 12, tt:tt + 1], None, ALU.mult).then_inc(S("final"), 1)

    @block.gpsimd
    def _(pool):
        t = Tally()

        Q = {"mla": lambda hd: qt[:, :, bass.ds(hd * 192, 192)], "a": lambda hd: z[:, :, bass.ds(hd * 64 + Z_QA, 64)],
             "b": lambda hd: z[:, :, bass.ds(hd * 64 + Z_QB, 64)]}
        K = {"mla": lambda hd: kv[:, :, bass.ds(hd * 256, 128)], "a": lambda hd: z[:, :, bass.ds(hd * 64 + Z_KA, 64)],
             "b": lambda hd: z[:, :, bass.ds(hd * 64 + Z_KB, 64)]}

        def stage(part, first=None):
            def rows_of(s, hd):
                pool.tensor_copy(QP[s][0:2, :], cq2[:, bass.ds(hd, 1), :].rearrange("p o n -> p (o n)")).then_inc(S("rows_staged"), 1)

            def step(j, head):
                s, (at, hd) = slot(j, 0), head(0)
                if first and not head(4):
                    first(j)
                if head(4) or t.n.get("at"):
                    pool.wait_ge(S("at_T"), t.at("at", j - 3))
                pool.tensor_copy(SQ[at.name][s], Q[at.name](hd))
                pool.tensor_copy(SK[at.name][s], K[at.name](hd)).then_inc(S("at_stage"), 1)
                if at is FORGETTING and head(4):
                    pool.wait_ge(S("at_S"), t.at("at", j - 3))
                    rows_of(s, hd)
                elif at is FORGETTING and j == 3:
                    pool.wait_ge(S("forget_q"), 32)
                    for n in range(4):
                        rows_of(n, n)

            over_heads(pool, t, [part], step)

        def load(dst, src, sem):
            pool.dma_start(dst, src).then_inc(S(sem), 16)

        def layer_end(n):
            products(pool, "pool" if n == 0 else "ukv", 8)
            load(pgain, a["post_norm"][n:n + 1, :].broadcast_to([128, D]), f"post_gain_in{n}")
            pool.wait_ge(S(f"post_gain_in{n}"), 16)
            for c in range(NCH):
                chunk_out(pool, ("pool_out", "mla_out")[n], c)
                cols = slice(c * 512, c * 512 + 512)
                for tt in range(2):
                    last = pool.tensor_tensor(outt[:, tt, cols], outt[:, tt, cols], pgain[:, cols], ALU.mult)
                last.then_inc(S("post_gained"), 1)

        load(posi, a["positions"].rearrange("o (t p) -> p (o t)", p=128), "pos_in")
        load(freqs, a["c_freq"].broadcast_to([128, 32]), "pos_in")
        load_gains(pool, (1, 2, 3), "rows_in1")
        load(causal, a["c_causal"], "causal_in")
        load(ptok, tokens(a["p"][0, 0]), "ple_in0")
        pool.wait_ge(S("h_in"), 32)
        for c in range(NCH):
            cols = slice(c * 512, c * 512 + 512)
            for tt in range(2):
                last = pool.tensor_tensor(hsq[:, tt, cols], h[:, tt, cols], h[:, tt, cols], ALU.mult)
            last.then_inc(S("x_squared"), 1)
        layer_end(0)
        products(pool, "proj0")
        load(ptok, tokens(a["p"][1, 0]), "ple_in1")

        def first_mla(j):
            if j == 0:
                pool.wait_ge(S("q_roped"), 2)
            chunk_out(pool, "ukv", j // 2, of=8)

        stage(MLA, first_mla)
        layer_end(1)
        load(memt, tokens(a["mem_2"][0]), "mem_in")
        gated(pool, 1)
        pool.memset(reltab, 1.0).then_inc(S("ones_set"), 1)
        pool.memset(glt, 1.0).then_inc(S("ones_set"), 1)
        load(relone, a["c_rel"], "rel_tables")
        load(flip, a["c_flip"], "rel_tables")
        pool.wait_ge(S("ones_set"), 2)
        load(reltab[0:BUCKETS, :], a["rel_table_2"], "rel_tables")
        load(w2a[0:16, :], a["c_gate_w2_2"][0], "hyb_in")
        load(w2a[16:17, :], a["c_gate_b_2"], "hyb_in")
        load(fbias, a["f_bias_2"].broadcast_to([128, B_H]), "hyb_in")
        load(trio, a["c_trio"], "hyb_in")
        pool.wait_ge(S("rel_out"), 16)
        for hd in range(A_H):
            load(relb[:, hd, :], bass.AP(tensor=rel_scratch.tensor, offset=hd * 384, ap=[[1, 128], [1, 256]]), "rel_in")
        stage(DILATED, lambda j: chunk_out(pool, "z", 5, of=13))
        stage(FORGETTING)
        heads_done(pool, "b")
        load(gmask.rearrange("p l n -> p (l n)"), a["c_masks"], "gla_in")
        load(dmat.rearrange("p l n -> p (l n)"), a["c_decay"], "gla_in")
        load(cnb, a["c_norm_2"].broadcast_to([128, C_DV]), "gla_in")
        pool.wait_ge(S("gla_in"), 48)
        pool.wait_ge(S("rc_silu"), 1)
        mc8 = mix[:, :, A_W + B_W:D].rearrange("p t (h n) -> p t h n", n=C_DV)
        for tt in range(2):
            last = pool.tensor_tensor(mc8[:, tt], mc8[:, tt], cnb.unsqueeze(1).broadcast_to([128, C_H, C_DV]), ALU.mult)
        last.then_inc(S("rc_gate"), 1)
        products(pool, "up")
        load(fgain, a["norm_final_2"].unsqueeze(0).broadcast_to([128, D]), "final_gain_in")
        pool.wait_ge(S("final_gain_in"), 16)
        for c in range(NCH):
            chunk_out(pool, "down", c)
            cols = slice(c * 512, c * 512 + 512)
            for tt in range(2):
                last = pool.tensor_tensor(fout[:, tt, cols], h[:, tt, cols], fgain[:, cols], ALU.mult)
            last.then_inc(S("final_gained"), 1)

    ctx.close()


_INS = ["x", "p", "positions", "pre_norm", "post_norm", "pool_w_in", "pool_w_group", "pool_scale", "pool_w_out", "mla_w_in",
        "mla_q_norm", "mla_w_uq", "mla_kv_norm", "mla_w_ukv", "mla_w_out", "ple_norm", "ple_w_gate", "ple_w_proj", "mem_2",
        "rel_table_2", "mem_norm_2", "norm_final_2", "norm_mix_2", "w_in_2", "f_bias_2", "c_gate_w2_2", "c_gate_b_2",
        "c_norm_2", "w_out_2", "norm_cross_2", "w_cq_2", "w_ckv_2", "w_co_2", "norm_ffn_2", "w_up_2", "conv_w_2",
        "conv_b_2", "w_down_2"]


def kernel(**inputs):
    import concourse.bacc as bacc
    from concourse.bass_utils import run_bass_kernel_spmd

    nc = bacc.Bacc("TRN2", target_bir_lowering=False, num_devices=1)
    given = {name: np.ascontiguousarray(inputs[name]) for name in _INS}
    given.update({f"c_{name}": value for name, value in shape_constants().items()})
    arrays = {f"in_{name}": value for name, value in given.items()}
    aps = {name: nc.dram_tensor(f"in_{name}", value.shape, mybir.dt.from_np(value.dtype), kind="ExternalInput").ap()
           for name, value in given.items()}
    out = nc.dram_tensor("out_0", (1, T, D), F32, kind="ExternalOutput").ap()
    build(nc, aps, out)
    r = run_bass_kernel_spmd(nc, [arrays], core_ids=[0])
    return r.results[0]["out_0"]
```
